# Optimizing a Trainium2 kernel written in Bass

```python
import jax, jax.numpy as jnp
from jax import lax
import numpy as np

D_MODEL = 1024
BATCH = 1
SEQ = 512
DEPTH = 1
DEC_BATCH = 8
DEC_SEQ = 8
PAST_LEN = 2048
PAGE_SIZE = 128

A_HEADS = 4
A_KDIM = 128
A_VDIM = 128
A_WIDTH = A_HEADS * A_KDIM
A_CHUNK = 64
B_HEADS = 8
B_HEAD_DIM = 64
B_WIDTH = B_HEADS * B_HEAD_DIM
MOBA_BLOCK = 256
MOBA_TOPK = 3
MOBA_QBLOCK = 64
ROT_DIM = B_HEAD_DIM // 4
ROPE_THETA = 500000.0
N_GROUPS = 4
EXPERTS_PER_GROUP = 8
N_EXPERTS = N_GROUPS * EXPERTS_PER_GROUP
EXPERT_TOPK = 2
D_EXPERT = D_MODEL // 2
MOE_ROWS = 128
IN_WIDTH = 4 * A_WIDTH + 3 * B_WIDTH + 2 * D_MODEL
NORM_EPS = 1e-6

kernel_name = 'hybrid_hgrn2_moba_hmoe_step'

F32 = jnp.float32

def _rmsnorm(x, g):
    xf = x.astype(F32)
    y = xf * lax.rsqrt(jnp.mean(xf * xf, axis=-1, keepdims=True) + NORM_EPS)
    return (y * g.astype(F32)).astype(x.dtype)

def _modulation(c, w, b):
    m = jax.nn.silu(c.astype(F32)) @ w.astype(F32) + b.astype(F32)
    return [a[:, None, :].astype(c.dtype) for a in jnp.split(m, 6, axis=-1)]

def _rope_partial(x, pos):
    half = ROT_DIM // 2
    inv = jnp.power(ROPE_THETA, -(jnp.arange(half, dtype=F32) * 2.0 / ROT_DIM))
    ang = pos.astype(F32)[:, None] * inv[None, :]
    cos = jnp.cos(ang)[:, None, :]
    sin = jnp.sin(ang)[:, None, :]
    xr = x[..., :ROT_DIM].astype(F32)
    x1, x2 = xr[..., :half], xr[..., half:]
    rot = jnp.concatenate([x1 * cos - x2 * sin, x1 * sin + x2 * cos], axis=-1)
    return jnp.concatenate([rot.astype(x.dtype), x[..., ROT_DIM:]], axis=-1)

def _hgrn2_scan(q, logf, k, v, s0):
    n, h, t, _ = q.shape
    dv = v.shape[-1]
    c = min(A_CHUNK, t)
    n_chunks = -(-t // c)
    pad = n_chunks * c - t

    def prep(a):
        a = jnp.pad(a.astype(F32), ((0, 0), (0, 0), (0, pad), (0, 0)))
        return jnp.moveaxis(a.reshape(n, h, n_chunks, c, a.shape[-1]), 2, 0)

    qc, fc, kc, vc = prep(q), prep(logf), prep(k), prep(v)
    causal = jnp.tril(jnp.ones((c, c), dtype=bool))

    def step(s, inp):
        qb, fb, kb, vb = inp
        b = jnp.cumsum(fb, axis=2)
        o_inter = jnp.einsum('nhtk,nhkv->nhtv', qb * jnp.exp(b), s)
        diff = b[:, :, :, None, :] - b[:, :, None, :, :]
        decay = jnp.exp(jnp.where(causal[:, :, None], diff, -jnp.inf))
        attn = jnp.einsum('nhtk,nhtsk,nhsk->nhts', qb, decay, kb)
        o = o_inter + jnp.einsum('nhts,nhsv->nhtv', attn, vb)
        b_last = b[:, :, -1:, :]
        s_new = (jnp.exp(b_last[:, :, 0, :])[..., None] * s
                 + jnp.einsum('nhsk,nhsv->nhkv', kb * jnp.exp(b_last - b), vb))
        return s_new, o

    s_fin, o = lax.scan(step, s0.astype(F32), (qc, fc, kc, vc))
    o = jnp.moveaxis(o, 0, 2).reshape(n, h, n_chunks * c, dv)[:, :, :t]
    return o, s_fin

def _hgrn2_branch(q_raw, f_raw, i_raw, g_raw, lb, gain, s0):
    n, t, _ = q_raw.shape
    heads = lambda a: a.reshape(n, t, A_HEADS, -1).transpose(0, 2, 1, 3)
    lbb = lb[None, :, None, :]
    q = jax.nn.silu(heads(q_raw).astype(F32))
    f = lbb + (1.0 - lbb) * jax.nn.sigmoid(heads(f_raw).astype(F32))
    o, s = _hgrn2_scan(q, jnp.log(f), 1.0 - f, heads(i_raw), s0)
    o = o.transpose(0, 2, 1, 3)
    o = _rmsnorm(o, gain) * jax.nn.silu(g_raw.astype(F32).reshape(n, t, A_HEADS, A_VDIM))
    return o.reshape(n, t, A_WIDTH).astype(q_raw.dtype), s

def _moba_qkv(bq, bk, bv, pos):
    n, t, _ = bq.shape
    shp = (n, t, B_HEADS, B_HEAD_DIM)
    q = _rope_partial(bq.reshape(shp), pos).transpose(0, 2, 1, 3)
    k = _rope_partial(bk.reshape(shp), pos).transpose(0, 2, 1, 3)
    v = bv.reshape(shp).transpose(0, 2, 1, 3)
    return q, k, v

def _moba_prompt(q, k, v):
    b, h, s, dh = q.shape
    n_blk = -(-s // MOBA_BLOCK)
    pad = n_blk * MOBA_BLOCK - s
    kb = jnp.pad(k, ((0, 0), (0, 0), (0, pad), (0, 0))).reshape(b, h, n_blk, MOBA_BLOCK, dh)
    vb = jnp.pad(v, ((0, 0), (0, 0), (0, pad), (0, 0))).reshape(b, h, n_blk, MOBA_BLOCK, dh)
    k_mean = kb.astype(F32).mean(axis=3)
    k_sel = min(MOBA_TOPK, n_blk - 1)
    n_qb = s // MOBA_QBLOCK
    qs = jnp.moveaxis(q.reshape(b, h, n_qb, MOBA_QBLOCK, dh), 2, 0)
    scale = dh ** -0.5
    bi = jnp.arange(b)[:, None, None, None]
    hi = jnp.arange(h)[None, :, None, None]
    sel_len = k_sel * MOBA_BLOCK

    def one_block(args):
        qblk, qi = args
        q0 = qi * MOBA_QBLOCK
        j = q0 // MOBA_BLOCK
        qpos = q0 + jnp.arange(MOBA_QBLOCK)
        qf = qblk.astype(F32) * scale
        own_k = lax.dynamic_index_in_dim(kb, j, axis=2, keepdims=False).astype(F32)
        own_v = lax.dynamic_index_in_dim(vb, j, axis=2, keepdims=False).astype(F32)
        kpos = j * MOBA_BLOCK + jnp.arange(MOBA_BLOCK)
        s_own = jnp.einsum('bhqd,bhkd->bhqk', qf, own_k)
        s_own = jnp.where(kpos[None, :] <= qpos[:, None], s_own, -jnp.inf)
        if k_sel == 0:
            return jnp.einsum('bhqk,bhkd->bhqd', jax.nn.softmax(s_own, axis=-1), own_v)
        blk_score = jnp.einsum('bhqd,bhnd->bhqn', qf, k_mean)
        blk_score = jnp.where(jnp.arange(n_blk) < j, blk_score, -jnp.inf)
        _, idx = lax.top_k(blk_score, k_sel)
        valid = idx < j
        ks = kb[bi, hi, idx].astype(F32)
        vs = vb[bi, hi, idx].astype(F32)
        s_sel = jnp.einsum('bhqd,bhqnkd->bhqnk', qf, ks)
        s_sel = jnp.where(valid[..., None], s_sel, -jnp.inf).reshape(b, h, MOBA_QBLOCK, sel_len)
        p = jax.nn.softmax(jnp.concatenate([s_sel, s_own], axis=-1), axis=-1)
        p_sel = p[..., :sel_len].reshape(b, h, MOBA_QBLOCK, k_sel, MOBA_BLOCK)
        return (jnp.einsum('bhqnk,bhqnkd->bhqd', p_sel, vs)
                + jnp.einsum('bhqk,bhkd->bhqd', p[..., sel_len:], own_v))

    o = lax.map(one_block, (qs, jnp.arange(n_qb)))
    return jnp.moveaxis(o, 0, 2).reshape(b, h, s, dh)

def _moba_sample(q, k_new, v_new, cache_k, cache_v, page_table):
    n, h, t, dh = q.shape
    ppb = MOBA_BLOCK // PAGE_SIZE
    n_full = PAST_LEN // MOBA_BLOCK
    n_tail = (PAST_LEN - n_full * MOBA_BLOCK) // PAGE_SIZE
    qf = q.astype(F32) * dh ** -0.5
    scores, values = [], []
    k_sel = min(MOBA_TOPK, n_full)
    if k_sel > 0:
        page_mean = cache_k.astype(F32).mean(axis=2)
        blk_mean = page_mean[page_table[:, :n_full * ppb]].reshape(n, n_full, ppb, h, dh).mean(axis=2)
        blk_score = jnp.einsum('nhtd,nbhd->nhtb', qf, blk_mean)
        _, idx = lax.top_k(blk_score, k_sel)
        logical = idx[..., None] * ppb + jnp.arange(ppb)
        phys = page_table[jnp.arange(n)[:, None, None, None, None], logical]
        hi = jnp.arange(h)[None, :, None, None, None]
        ks = cache_k[phys, hi].astype(F32).reshape(n, h, t, k_sel * MOBA_BLOCK, dh)
        vs = cache_v[phys, hi].astype(F32).reshape(n, h, t, k_sel * MOBA_BLOCK, dh)
        scores.append(jnp.einsum('nhtd,nhtkd->nhtk', qf, ks))
        values.append((vs, True))
    if n_tail > 0:
        tail = page_table[:, n_full * ppb:n_full * ppb + n_tail]
        kt = cache_k[tail].astype(F32).transpose(0, 2, 1, 3, 4).reshape(n, h, n_tail * PAGE_SIZE, dh)
        vt = cache_v[tail].astype(F32).transpose(0, 2, 1, 3, 4).reshape(n, h, n_tail * PAGE_SIZE, dh)
        scores.append(jnp.einsum('nhtd,nhkd->nhtk', qf, kt))
        values.append((vt, False))
    s_new = jnp.einsum('nhtd,nhsd->nhts', qf, k_new.astype(F32))
    scores.append(jnp.where(jnp.tril(jnp.ones((t, t), dtype=bool)), s_new, -jnp.inf))
    values.append((v_new.astype(F32), False))
    p = jax.nn.softmax(jnp.concatenate(scores, axis=-1), axis=-1)
    offs = np.cumsum([0] + [a.shape[-1] for a in scores]).tolist()
    parts = []
    for (vals, per_query), lo, hi_ in zip(values, offs[:-1], offs[1:]):
        pp = p[..., lo:hi_]
        parts.append(jnp.einsum('nhtk,nhtkd->nhtd', pp, vals) if per_query
                     else jnp.einsum('nhtk,nhkd->nhtd', pp, vals))
    return sum(parts)

def _hier_moe(x, w_group, b_group, w_er, b_er, w_gate, w_up, w_down):
    m, d = x.shape
    xf = x.astype(F32)
    rows = jnp.arange(m)
    g_logits = xf @ w_group.astype(F32) + b_group.astype(F32)
    g_sel = jnp.argmax(g_logits, axis=-1)
    p_group = jax.nn.softmax(g_logits, axis=-1)[rows, g_sel]
    e_logits = jnp.einsum('md,gde->mge', xf, w_er.astype(F32)) + b_er.astype(F32)
    e_logits = e_logits[rows, g_sel]
    top_p, top_i = lax.top_k(jax.nn.softmax(e_logits, axis=-1), EXPERT_TOPK)
    gate_w = p_group[:, None] * top_p / jnp.sum(top_p, axis=-1, keepdims=True)
    expert = (g_sel[:, None] * EXPERTS_PER_GROUP + top_i).astype(jnp.int32)

    n_assign = m * EXPERT_TOPK
    flat_e = expert.reshape(-1)
    flat_tok = jnp.repeat(jnp.arange(m, dtype=jnp.int32), EXPERT_TOPK)
    flat_w = gate_w.reshape(-1)
    order = jnp.argsort(flat_e)
    e_sorted = flat_e[order]
    counts = jnp.bincount(flat_e, length=N_EXPERTS)
    padded = (counts + MOE_ROWS - 1) // MOE_ROWS * MOE_ROWS
    start = jnp.cumsum(counts) - counts
    pad_end = jnp.cumsum(padded)
    pad_start = pad_end - padded
    dest = pad_start[e_sorted] + jnp.arange(n_assign) - start[e_sorted]
    n_blocks = -(-(n_assign + N_EXPERTS * (MOE_ROWS - 1)) // MOE_ROWS)
    n_rows = n_blocks * MOE_ROWS
    row_tok = jnp.zeros((n_rows,), jnp.int32).at[dest].set(flat_tok[order])
    row_w = jnp.zeros((n_rows,), F32).at[dest].set(flat_w[order])
    block_expert = jnp.minimum(
        jnp.searchsorted(pad_end, jnp.arange(n_blocks) * MOE_ROWS, side='right'), N_EXPERTS - 1)

    def run_block(args):
        tok, e = args
        xb = x[tok]
        hid = jax.nn.silu(xb @ w_gate[e]) * (xb @ w_up[e])
        return hid @ w_down[e]

    y = lax.map(run_block, (row_tok.reshape(n_blocks, MOE_ROWS), block_expert))
    out = jnp.zeros((m, d), F32).at[row_tok].add(y.reshape(n_rows, d).astype(F32) * row_w[:, None])
    return out.astype(x.dtype)

def setup_inputs(seed: int = 0) -> dict:
    key = jax.random.key(seed)
    ks = jax.random.split(key, 32)
    n_pages = PAST_LEN // PAGE_SIZE
    n_pool = (DEC_BATCH * n_pages * 5) // 4
    nrm = lambda k, shape, s: jax.random.normal(k, shape, jnp.float32) * s
    return {
        'x_prompt': nrm(ks[0], (BATCH, SEQ, D_MODEL), 1.0),
        'x_sample': nrm(ks[1], (DEC_BATCH, DEC_SEQ, D_MODEL), 1.0),
        'c_prompt': nrm(ks[2], (BATCH, D_MODEL), 1.0),
        'c_sample': nrm(ks[3], (DEC_BATCH, D_MODEL), 1.0),
        'cache_k': nrm(ks[4], (DEPTH, n_pool, B_HEADS, PAGE_SIZE, B_HEAD_DIM), 1.0),
        'cache_v': nrm(ks[5], (DEPTH, n_pool, B_HEADS, PAGE_SIZE, B_HEAD_DIM), 1.0),
        'state_hgrn': nrm(ks[6], (DEPTH, DEC_BATCH, A_HEADS, A_KDIM, A_VDIM), 0.3),
        'page_table': jax.random.permutation(ks[7], n_pool)[:DEC_BATCH * n_pages]
                      .reshape(DEC_BATCH, n_pages).astype(jnp.int32),
        'w_ada': nrm(ks[8], (DEPTH, D_MODEL, 6 * D_MODEL), D_MODEL ** -0.5),
        'b_ada': nrm(ks[9], (DEPTH, 6 * D_MODEL), 0.01),
        'norm_mix': 1.0 + nrm(ks[10], (DEPTH, D_MODEL), 0.02),
        'norm_ffn': 1.0 + nrm(ks[11], (DEPTH, D_MODEL), 0.02),
        'w_in': nrm(ks[12], (DEPTH, D_MODEL, IN_WIDTH), D_MODEL ** -0.5),
        'hgrn_lb_logits': nrm(ks[13], (DEPTH + 1, A_WIDTH), 0.5),
        'hgrn_norm': 1.0 + nrm(ks[14], (DEPTH, A_VDIM), 0.02),
        'w_proj_a': nrm(ks[15], (DEPTH, A_WIDTH, D_MODEL), A_WIDTH ** -0.5),
        'w_proj_b': nrm(ks[16], (DEPTH, B_WIDTH, D_MODEL), B_WIDTH ** -0.5),
        'w_out': nrm(ks[17], (DEPTH, D_MODEL, D_MODEL), D_MODEL ** -0.5),
        'w_group': nrm(ks[18], (DEPTH, D_MODEL, N_GROUPS), D_MODEL ** -0.5),
        'b_group': nrm(ks[19], (DEPTH, N_GROUPS), 0.01),
        'w_expert_router': nrm(ks[20], (DEPTH, N_GROUPS, D_MODEL, EXPERTS_PER_GROUP), D_MODEL ** -0.5),
        'b_expert_router': nrm(ks[21], (DEPTH, N_GROUPS, EXPERTS_PER_GROUP), 0.01),
        'w_gate': nrm(ks[22], (DEPTH, N_EXPERTS, D_MODEL, D_EXPERT), D_MODEL ** -0.5),
        'w_up': nrm(ks[23], (DEPTH, N_EXPERTS, D_MODEL, D_EXPERT), D_MODEL ** -0.5),
        'w_down': nrm(ks[24], (DEPTH, N_EXPERTS, D_EXPERT, D_MODEL), D_EXPERT ** -0.5),
        'norm_final': 1.0 + nrm(ks[25], (D_MODEL,), 0.02),
    }

def reference(x_prompt, x_sample, c_prompt, c_sample, cache_k, cache_v, state_hgrn, page_table,
              w_ada, b_ada, norm_mix, norm_ffn, w_in, hgrn_lb_logits, hgrn_norm,
              w_proj_a, w_proj_b, w_out, w_group, b_group, w_expert_router, b_expert_router,
              w_gate, w_up, w_down, norm_final):
    xp, xs = x_prompt, x_sample
    bp, tp, d = xp.shape
    bs, ts, _ = xs.shape
    pos_p = jnp.arange(tp)
    pos_s = PAST_LEN + jnp.arange(ts)
    lb_all = jnp.cumsum(jax.nn.softmax(hgrn_lb_logits.astype(F32), axis=0), axis=0)
    splits = np.cumsum([A_WIDTH] * 4 + [B_WIDTH] * 3 + [D_MODEL]).tolist()
    kp_l, vp_l, sp_l, ks_l, vs_l, ss_l = [], [], [], [], [], []

    for l in range(DEPTH):
        mp = _modulation(c_prompt, w_ada[l], b_ada[l])
        ms = _modulation(c_sample, w_ada[l], b_ada[l])
        lb = lb_all[l].reshape(A_HEADS, A_KDIM)

        hp = _rmsnorm(xp, norm_mix[l]) * (1 + mp[1]) + mp[0]
        hs = _rmsnorm(xs, norm_mix[l]) * (1 + ms[1]) + ms[0]
        aq_p, af_p, ai_p, ag_p, bq_p, bk_p, bv_p, ga_p, gb_p = jnp.split(hp @ w_in[l], splits, axis=-1)
        aq_s, af_s, ai_s, ag_s, bq_s, bk_s, bv_s, ga_s, gb_s = jnp.split(hs @ w_in[l], splits, axis=-1)

        s0_p = jnp.zeros((bp, A_HEADS, A_KDIM, A_VDIM), F32)
        oa_p, st_p = _hgrn2_branch(aq_p, af_p, ai_p, ag_p, lb, hgrn_norm[l], s0_p)
        oa_s, st_s = _hgrn2_branch(aq_s, af_s, ai_s, ag_s, lb, hgrn_norm[l], state_hgrn[l])

        q_p, k_p, v_p = _moba_qkv(bq_p, bk_p, bv_p, pos_p)
        q_s, k_s, v_s = _moba_qkv(bq_s, bk_s, bv_s, pos_s)
        ob_p = _moba_prompt(q_p, k_p, v_p).transpose(0, 2, 1, 3).reshape(bp, tp, B_WIDTH).astype(xp.dtype)
        ob_s = _moba_sample(q_s, k_s, v_s, cache_k[l], cache_v[l], page_table)
        ob_s = ob_s.transpose(0, 2, 1, 3).reshape(bs, ts, B_WIDTH).astype(xs.dtype)

        y_p = (jax.nn.sigmoid(ga_p) * (oa_p @ w_proj_a[l]) + jax.nn.sigmoid(gb_p) * (ob_p @ w_proj_b[l])) @ w_out[l]
        y_s = (jax.nn.sigmoid(ga_s) * (oa_s @ w_proj_a[l]) + jax.nn.sigmoid(gb_s) * (ob_s @ w_proj_b[l])) @ w_out[l]
        xp = xp + mp[2] * y_p
        xs = xs + ms[2] * y_s

        h2p = _rmsnorm(xp, norm_ffn[l]) * (1 + mp[4]) + mp[3]
        h2s = _rmsnorm(xs, norm_ffn[l]) * (1 + ms[4]) + ms[3]
        f = _hier_moe(jnp.concatenate([h2p.reshape(-1, d), h2s.reshape(-1, d)], axis=0),
                      w_group[l], b_group[l], w_expert_router[l], b_expert_router[l],
                      w_gate[l], w_up[l], w_down[l])
        xp = xp + mp[5] * f[:bp * tp].reshape(bp, tp, d)
        xs = xs + ms[5] * f[bp * tp:].reshape(bs, ts, d)

        kp_l.append(k_p); vp_l.append(v_p); sp_l.append(st_p.astype(state_hgrn.dtype))
        ks_l.append(k_s); vs_l.append(v_s); ss_l.append(st_s.astype(state_hgrn.dtype))

    y_prompt = _rmsnorm(xp, norm_final)
    y_sample = _rmsnorm(xs, norm_final)
    return (y_prompt, y_sample, jnp.stack(kp_l), jnp.stack(vp_l), jnp.stack(sp_l),
            jnp.stack(ks_l), jnp.stack(vs_l), jnp.stack(ss_l))


_drawn_inputs = setup_inputs


def setup_inputs(seed=0):
    import zlib

    import numpy as np

    out = dict(_drawn_inputs(seed))
    spreads = {}
    factors = {'b_expert_router': 7.419, 'norm_final': 21.558, 'hgrn_norm': 2.896, 'b_group': 3.455}
    for name, (base, spread) in spreads.items():
        noise = np.random.default_rng([zlib.crc32(name.encode()), seed]).standard_normal(out[name].shape)
        drawn = base * np.exp(spread * noise) if base else spread * noise
        out[name] = __import__('jax').numpy.asarray(drawn.astype(out[name].dtype))
    for name, factor in factors.items():
        out[name] = (out[name] * factor).astype(out[name].dtype)
    return out
```

```python
from contextlib import ExitStack

import concourse.bass as bass
from concourse import mybir

F32 = mybir.dt.float32
I32 = mybir.dt.int32
ALU = mybir.AluOpType
ACT = mybir.ActivationFunctionType
AX = mybir.AxisListType.X

P = 128
D = 1024
KD = D // P
SEQ = 512
NSEQ = 8
TS = 8
NSMP = NSEQ * TS
T = SEQ + NSMP
PT_ = SEQ // P
NT = PT_ + 1
NCOND = 1 + NSEQ
AH = 4
BH = 8
DH = 64
BLK = 256
NBLK = 8
PAGE = 128
TOPK = 3
EPS = 1e-6
NG, EPG = 4, 8
NE = NG * EPG
DE = 512
CAP = 128
EXTRA = 8
NJ = NE + EXTRA
BIG = 1.0e30
ABSENT = 8192.0
CHUNK = 4096
SAMPLE_PHASES = (("k", 0), ("k", 1), ("v", 0), ("k", 2), ("v", 1), ("k", 3), ("v", 2), ("v", 3))
LEVELS = (64, 32, 16, 8, 4, 2, 1)
NL = len(LEVELS)

CONST = {}
_at = 0
for _name, _n in (("ident", 128), ("ones", 128), ("seqmask", 8),
                  ("causal", 128), ("newmask", 112), ("fold", 64), ("cos", NT * 8), ("sin", NT * 8), ("tie", 64),
                  ("before", 128), ("iota", 128), ("iotaE", NE), ("ranks8", 8), ("valid", NT), ("payload", NT),
                  ("reset", T), ("levels", 8 * 128)):
    CONST[_name] = (_at, _n)
    _at += _n
NCONST = _at
KEPT = CONST["causal"][0]
ATTN = (KEPT, CONST["before"][0])
ROUTE = (ATTN[1], CONST["reset"][0])


def part(t, at, *dims):
    n = 1
    for d in dims:
        n *= d
    v = t[:, at:at + n]
    if len(dims) == 1:
        return v
    names = "abcde"[:len(dims)]
    return v.rearrange("p (" + " ".join(names) + ") -> p " + " ".join(names), **dict(zip(names, dims)))


def bass_hybrid_step(nc, x_prompt, x_sample, c_prompt, c_sample, cache_k, cache_v, state_hgrn, page_table,
                     w_ada, b_ada, norm_mix, norm_ffn, w_in, lb_logits, hgrn_norm, w_proj_a, w_proj_b, w_out,
                     w_group, b_group, w_er, b_er, w_gate, w_up, w_down, norm_final, consts,
                     y_prompt, y_sample, k_prompt, v_prompt, s_prompt, k_sample, v_sample, s_sample):
    h2_rows = nc.dram_tensor("h2_rows", (T, D), F32, kind="Internal").ap()
    y_rows = nc.dram_tensor("y_rows", (2 * T, D), F32, kind="Internal").ap()

    with ExitStack() as ctx:
        def sb(name, cols, dt=F32):
            return ctx.enter_context(nc.sbuf_tensor(name, [P, cols], dt))

        def sem(name):
            return ctx.enter_context(nc.semaphore(name))

        ps = [ctx.enter_context(nc.psum_tensor(f"bank{i}", [P, 512], F32)) for i in range(8)]

        arena = sb("arena", 6 * CHUNK + 4608 + 5120 + 17408)
        ringA = 0
        SC = 4 * CHUNK
        HT = 6 * CHUNK
        XR = HT + 4608
        QF = XR + 5120
        AG = QF + 4608
        BQ = AG + 5120
        ring = [part(arena, ringA + s * CHUNK, CHUNK) for s in range(6)]
        hT = part(arena, HT, KD, T)
        xr = part(arena, XR, NT, D)
        aq = part(arena, QF, AH, T)
        af = part(arena, QF + 2304, AH, T)
        ai = part(arena, AG, NT, 512)
        ag = part(arena, AG + 2560, NT, 512)
        bqkv = [part(arena, BQ + 2560 * i, NT, 512) for i in range(3)]
        bq, bk, bv = bqkv
        bsum = part(arena, SC, AH, T)
        diff = [part(arena, SC + 2304 + 576 * i, T) for i in range(2)]
        qdec = [part(arena, SC + 3456 + 576 * i, T) for i in range(2)]
        kdec = [part(arena, SC + 4608 + 576 * i, T) for i in range(2)]
        atmp = part(arena, SC + 5760, T)
        level = part(arena, SC + 7168, 8, 128)
        attnT = part(arena, XR, AH, T)
        logf = part(arena, XR + 2304, AH, T)
        kdT = part(arena, XR + 2304, AH, NT, 128)
        oa = part(arena, SC, NT, 512)
        stP = part(arena, SC + 2560, AH, 128)
        st0 = [part(arena, SC + 3072 + 1024 * i, NSEQ, 128) for i in range(2)]
        st1 = [part(arena, SC + 5120 + 1024 * i, NSEQ, 128) for i in range(2)]
        vbd = part(arena, SC + 7168, NSEQ, 128)
        osqr = part(arena, XR, NT * AH, 128)
        oaT = part(arena, QF, AH, T)
        obT = part(arena, QF + 2304, AH, T)
        qT = part(arena, AG, 4, T)
        kT = part(arena, AG + 2304, 4, T)
        prob = [part(arena, SC + 512 * i, 512) for i in range(2)]
        probT = [part(arena, SC + 1024 + 512 * i, 512) for i in range(2)]
        ob = part(arena, SC + 2048, NT, 512)
        qbd = part(arena, XR, NSEQ, BH, 16)
        keyT = [part(arena, XR + 1024 + 1024 * i, BH, 128) for i in range(2)]
        stS = [part(arena, XR + 3072 + 256 * i, 256) for i in range(2)]
        newT = part(arena, XR + 3584, 128)
        pnewT = part(arena, XR + 3712, 128)
        odiag = [part(arena, XR + 1024 + 128 * i, 128) for i in range(4)]
        orow = [part(arena, XR + 1536 + 128 * i, 128) for i in range(4)]
        snew = [part(arena, XR + 4096 + 64 * i, 64) for i in range(2)]
        qdup = part(arena, XR + 1024, BH, 128)
        gseq = [part(arena, SC + 4352, KD, NSMP), part(arena, BQ + 720, KD, NSMP)]
        S = [part(arena, SC + a, NBLK, 256) for a in (4608, 2048)]
        accS = [part(arena, SC + a, 4, P) for a in (6656, 7168, 7680, 4096)]
        probsT = part(arena, SC, NBLK, 2 * BH, 2, TS)
        merged = part(arena, BQ, KD, T)
        sig = [part(arena, SC + 576 * i, T) for i in range(4)]
        res = part(arena, AG, NT, D)
        gate1 = [part(arena, SC + 2304 + 1024 * i, D) for i in range(2)]
        xg = [part(arena, QF + 1024 * i, D) for i in range(2)]
        xgT = [part(arena, QF + 2048 + 1024 * i, KD, CAP) for i in range(2)]
        hs = part(arena, BQ, 4, CAP)
        hid = part(arena, BQ + 512, 4, CAP)
        yj = [part(arena, BQ + 1024 + 1024 * i, D) for i in range(2)]
        onehots = part(arena, BQ + 3072, 2, NT, NE)
        gate2 = [part(arena, BQ + 4096 + 1024 * i, D) for i in range(2)]

        cst = sb("cst", KEPT)
        C = {}
        for n, (a, k) in CONST.items():
            if a < KEPT:
                C[n] = cst[:, a:a + k]
            elif a < ATTN[1]:
                C[n] = part(arena, AG + 4608 + a - ATTN[0], k)
            elif a < ROUTE[1]:
                C[n] = part(arena, BQ + 400 + a - ROUTE[0], k)
        ident, ones, before = C["ident"], C["ones"], C["before"]
        reset = part(arena, SC + 6400, T)
        vecs = part(arena, SC + 3072, 128)
        colv = sb("colv", 80)
        gainv = part(arena, XR + 4992, 128)
        crow = part(arena, SC + 2048, D)
        cT = part(arena, SC + 3328, KD * NCOND)
        arow = [part(arena, SC + 3584 + 512 * i, 512) for i in range(2)]
        modT = sb("modT", 48 * NCOND)
        m3 = modT[:, :].rearrange("p (m n) -> p m n", n=NCOND)
        A1 = sb("A1", KD * NCOND)
        A2 = sb("A2", KD * NCOND)
        lb = sb("lb", 8)
        omlb = lb[:, 4:8]
        ssq = sb("ssq", 8)
        rstd = sb("rstd", 8)
        hss = sb("hss", NT * AH)
        ebl = sb("ebl", AH * 12)
        mx = sb("mx", 40)
        sm = sb("sm", 40)
        amx = part(arena, XR + 4480, 40)
        blk = sb("blk", 64)
        wr = part(arena, BQ, KD * 36)
        wr3 = wr.rearrange("p (k n) -> p k n", n=36)
        brow = part(arena, BQ + 320, 36)
        onerow = ones[0:1, 0:128]
        pages = sb("pages", 128, I32)
        soS = [part(arena, XR + 4864 + 64 * i, 64) for i in range(2)]
        jobs_i = sb("jobs_i", 2 * NJ + 4, I32)
        cur = sb("cur", 4, I32)
        ctl = sb("ctl", 16, I32)
        wts = sb("wts", 2 * NT)

        def S_(*names):
            return [sem(n) for n in names]

        c_in, xin, vec_in, lvl_in, cond_in, wr_in, attn_in = S_(
            "consts_in", "x_in", "vectors_in", "levels_in", "cond_in", "router_in", "attention_constants_in")
        fill = [sem(f"slot{s}_filled") for s in range(6)]
        used = [sem(f"slot{s}_used") for s in range(6)]

        plan = [("ada", n) for n in range(12)] + [("in", n) for n in range(7)]
        for kind, p in SAMPLE_PHASES:
            plan += [(kind, p, hb, n) for hb in range(2) for n in range(2)]
        plan += [("pa",), ("pb",), ("in", 7), ("in", 9), ("in", 8), ("in", 10), ("out", 0), ("out", 1)]
        slots = [n % 4 for n in range(len(plan) - 8)]
        first = len(slots) % 4
        slots += [(first + n) % 4 for n in (0, 1, 2, 3, 2, 3, 0, 1)]
        filled, taken = [0] * 6, [0] * 6
        loads, where = [], {}
        for what, slot in zip(plan, slots):
            filled[slot] += 128 if len(what) == 4 else 16
            where[what] = (slot, filled[slot], taken[slot])
            loads.append((what, *where[what]))
            taken[slot] += 1
        fill0, used0 = filled, taken

        mod_ready, cvec_t, cT_t, cT_r, silu_c = S_(
            "mod_ready", "vectors_transposed", "cond_transposed", "cond_ready", "silu_c")
        ssq_r, std_r, xn_r, xt_r, h_r = S_("row_squares", "row_std", "rows_normed", "rows_transposed", "hT_ready")
        in_mm, in_ev, zeroed = S_("in_proj_done", "in_proj_copied", "tails_zeroed")
        f_r, lnf_r = S_("f_ready", "log_f_ready")
        d_r, e_r, qd_r, kd_r, at_mm, at_ac = S_("diff_ready", "decay_ready", "q_decayed", "k_decayed",
                                              "attn_done", "attn_added")
        eb_r, dl_r, el_r, qk_r, kt_mm, kt_ev = S_("exp_b", "diff_last", "exp_last", "qk_ready", "kd_transposed",
                                                "kd_copied")
        o_mm, s_mm, s_up, o_ev = S_("o_done", "state_product", "state_ready", "o_copied")
        vb_r, so_mm, so_ev, sn_mm, sn_r, so_t = S_(
            "v_blocked", "so_done", "so_copied", "new_state_product",
            "new_state_ready", "so_turned_copied")
        hs_r, hq_r, oa_r, oat_mm, oat_r = S_("o_squares", "o_std", "oa_ready", "oa_transposed", "oaT_ready")
        rope_r, qkt_mm, qkt_r = S_("rope_ready", "qk_transposed", "qkT_ready")
        sc_mm, mx_r, ex_r, pt_mm, pt_r, pv_mm, ob_r = S_("scores_done", "max_ready", "probs_ready", "probs_transposed",
                                                       "probsT_ready", "pv_done", "ob_rows")
        qb_mm, qb_r, key_mm, keyA, keyD, sq_ev, ss_mm, ss_ev = S_(
            "qdup_done", "qblock_ready", "keys_transposed", "keysT_a", "keysT_b", "sscores_copied",
            "sscores_turned", "S_ready")
        nw_mm, nw_ev, nt_mm, sb_r, sp_r, sT_mm, sT_r, nT_mm, nT_r = S_(
            "new_scores", "new_copied", "new_turned", "sbias_ready", "sprobs_ready", "sprobs_turned", "sprobsT_ready",
            "newprobs_turned", "newprobsT_ready")
        spv, od_r, of_mm, or_r, ot_mm, ot_r = S_("spv_done", "odiag_ready", "ofold_done", "orow_ready",
                                               "orow_turned", "ob_sample_ready")
        obt_mm, obt_r = S_("ob_transposed", "obT_ready")
        g_mm, g_r, pr_mm, mg_r, bc_mm, bc_r, y_mm, x2_r, xin2 = S_(
            "gates_done", "gates_ready", "branch_done", "merged_ready", "gatebc_done", "gatebc_ready", "y_done",
            "x2_ready", "x_again")
        h2b_mm, h2b_r, h2_out, lg_mm = S_("h2_turned", "h2_rows_ready", "h2_stored", "logits_done")
        rt_a, rt_b, rk_mm, rk_r, oh_r, tb_mm, tb_r = S_("route_max", "route_exp", "ranks_done", "ranks_taken",
                                                      "onehot_ready", "table_done", "table_ready")
        cur_r, g_cl, xt2, xtA, xtD, sl, hd, yA, yD = S_(
            "index_ready", "gather_cleared", "job_transposed", "jobT_a", "jobT_b", "silu_done",
            "hid_ready", "job_y_a", "job_y_b")
        g_in2 = [sem(f"gathered{i}") for i in range(2)]
        sc2 = [sem(f"scattered{i}") for i in range(2)]
        s0_in2 = [sem(f"state_in{i}") for i in range(2)]
        sn_out2 = [sem(f"state_out{i}") for i in range(2)]
        kv_out, g2_mm, g2_r = S_("kv_stored", "gate2_done", "gate2_ready")
        so2_mm, lb_d, lb_r, nrm = S_("so_turn_done", "lb_diff", "lb_ready", "norm_scale")
        yin = [sem(f"y_in{i}") for i in range(2)]
        fin_a, fin_s, fin_v = S_("final_squares", "final_std", "final_rows")
        ofree = [sem(f"out_row{i}") for i in range(2)]
        gfin = sem("final_gain_in")

        acc_r, acc_t, sn_t = S_("outputs_copied", "outputs_turned", "snew_ready")
        ada_cp, ada_t = S_("mod_rows_copied", "mod_turned")
        qdup_r, gseq_r, y_r = S_("qdup_ready", "gates_spread", "y_taken")
        qks = sem("sample_scores_done")
        sbias, ssum, soff, bs8, bm8, rank8 = (blk[:, a:a + 9] for a in (0, 9, 18, 27, 36, 45))
        nm1, m1_ = (blk[:, a:a + 1] for a in (54, 55))
        rs1 = [blk[:, a:a + 1] for a in (56, 57, 58, 59)]
        gt8, eq8 = (part(arena, XR + 4352 + a, 8, 8) for a in (0, 64))
        ybuf = [part(arena, CHUNK * 3 * i, 2 * D) for i in range(2)]
        fgain = part(arena, CHUNK, D)
        fsq = part(arena, 2 * CHUNK, D)
        fss = sb("fss", 8)
        msum = part(arena, BQ + 3392, NT, NE)
        slot1 = [part(arena, BQ + 3552 + 128 * i, 128) for i in range(2)]
        job1 = [part(arena, BQ + 3808 + 48 * i, NJ + 2) for i in range(2)]
        rt_at = [BQ + 6144]

        def rt(*dims):
            n = 1
            for d in dims:
                n *= d
            rt_at[0] += n
            return part(arena, rt_at[0] - n, *dims)

        lg = rt(NT, 36)
        rexp = rt(NT, 5)

        def unit_of(v):
            return v // NL * (NL + 1) + v % NL + 1

        in_units = []
        for c, x in ((0, aq), (1, af)):
            for m in range(4):
                in_units += [(c, x[:, m, 0:SEQ]), (c, x[:, m, SEQ:T])]
        for c, x in ((2, ai), (3, ag), (4, bq), (5, bk), (6, bv)):
            in_units += [(c, x[0:(P if t < PT_ else NSMP), t, :]) for t in range(NT)]

        block = ctx.enter_context(nc.Block())

        def rows(t):
            return P if t < PT_ else NSMP

        def src_x(t):
            return x_prompt[0, t * P:(t + 1) * P, :] if t < PT_ else x_sample.rearrange("n t d -> (n t) d")

        def weights(w):
            return w.rearrange("(k p) n -> p k n", p=P)

        def slot_view(s, k, n):
            return ring[s].rearrange("p (k n) -> p k n", n=n)

        @block.sync
        def _(sp):
            sp.dma_start(cst[:, :], consts[:, 0:KEPT]).then_inc(c_in, 16)
            sp.dma_start(crow[0:1, :], c_prompt).then_inc(cond_in, 16)
            sp.dma_start(crow[1:NCOND, :], c_sample).then_inc(cond_in, 16)
            for at_, n, v in ((0, 48, b_ada[0]), (48, 8, norm_mix[0]), (56, 8, norm_ffn[0]),
                              (72, 1, hgrn_norm[0])):
                sp.dma_start(vecs[at_:at_ + n, :], v.rearrange("(a b) -> a b", b=P)).then_inc(vec_in, 16)
            sp.dma_start(vecs[64:72, :], lb_logits.rearrange("l (a b) -> (l a) b", b=P)).then_inc(vec_in, 16)
            for t in range(NT):
                sp.dma_start(xr[0:rows(t), t, :], src_x(t)).then_inc(xin, 16)
            sp.dma_start(reset, consts[:, CONST["reset"][0]:CONST["reset"][0] + T]).then_inc(lvl_in, 16)
            sp.dma_start(arena[:, SC + 7168:SC + 8192], consts[:, CONST["levels"][0]:NCONST]).then_inc(lvl_in, 16)
            sp.dma_start(pages[0:1, :], page_table.rearrange("n j -> (n j)").rearrange("(a b) -> a b", a=1)).then_inc(lvl_in, 16)
            sp.wait_ge(lvl_in, 48)
            for what, slot, f, n in loads:
                if n:
                    sp.wait_ge(used[slot], n)
                if what[0] == "ada":
                    src = weights(w_ada[0][:, what[1] * 512:(what[1] + 1) * 512])
                    sp.dma_start(slot_view(slot, 8, 512), src).then_inc(fill[slot], 16)
                elif what[0] == "in":
                    src = weights(w_in[0][:, what[1] * 512:(what[1] + 1) * 512])
                    sp.dma_start(slot_view(slot, 8, 512), src).then_inc(fill[slot], 16)
                elif what[0] in ("pa", "pb"):
                    src = weights((w_proj_a if what[0] == "pa" else w_proj_b)[0])
                    sp.dma_start(slot_view(slot, 4, D), src).then_inc(fill[slot], 16)
                elif what[0] == "out":
                    src = weights(w_out[0][:, what[1] * 512:(what[1] + 1) * 512])
                    sp.dma_start(slot_view(slot, 8, 512), src).then_inc(fill[slot], 16)
                else:
                    kind, p, hb, n01 = what
                    cache = cache_k if kind == "k" else cache_v
                    s_ = 2 * p + n01
                    dst = ring[slot].rearrange("p (b h c) -> p b h c", b=4, h=BH)
                    for b in range(4):
                        for pg in range(2):
                            j = s_ * 16 + (hb * 4 + b) * 2 + pg
                            page = sp.value_load(pages[0:1, j:j + 1], min_val=0, max_val=cache.shape[1] - 1)
                            src = cache[0, bass.ds(page, 1)].rearrange("o h (i r) d -> i (o h) (r d)", r=2)
                            sp.dma_start(dst[64 * pg:64 * pg + 64, b], src).then_inc(fill[slot], 16)
            def job_weights(j, e, par):
                for c, w in enumerate((w_gate, w_up, w_down)):
                    s_ = 3 * par + c
                    yield s_, w[0, bass.ds(e, 1)].rearrange("o (k p) n -> p (o k) n", p=P)

            for s_ in range(4):
                sp.wait_ge(used[s_], used0[s_])
            sp.wait_ge(bc_r, 4)
            sp.wait_ge(x2_r, NT)
            sp.wait_ge(ssq_r, 2 * NT)

            def pair(i, e0, e1, first=False):
                for par, e in ((0, e0), (1, e1)):
                    for s_, src in job_weights(None, e, par):
                        if not first:
                            sp.wait_ge(used[s_], used0[s_] + i)
                        sp.dma_start(slot_view(s_, 8 if s_ % 3 < 2 else 4, 512 if s_ % 3 < 2 else D), src)\
                            .then_inc(fill[s_], 16)
            pair(0, 0, 1, first=True)
            with sp.Fori(1, NE // 2) as i:
                pair(i, 2 * i, 2 * i + 1)
            sp.wait_ge(tb_r, 2)
            njobs = sp.value_load(ctl[0:1, 8:9], min_val=0, max_val=EXTRA)
            with sp.Fori(0, EXTRA // 2) as i:
                with sp.If(njobs > 2 * i):
                    e0 = sp.value_load(ctl[0:1, bass.ds(2 * i, 1)], min_val=0, max_val=NE - 1)
                    e1 = sp.value_load(ctl[0:1, bass.ds(2 * i + 1, 1)], min_val=0, max_val=NE - 1)
                    pair(i + NE // 2, e0, e1)

            npairs = sp.snap((njobs + 1) >> 1)
            for par in range(2):
                sp.wait_ge(sc2[par], (npairs + NE // 2) * 16)
            sp.dma_start(fgain, norm_final.unsqueeze(0).to_broadcast([P, D])).then_inc(gfin, 16)
            y_tok = y_rows.rearrange("(t k) d -> t (k d)", k=2)
            for t in range(NT):
                if t >= 2:
                    sp.wait_ge(ofree[t % 2], 16 * (t // 2))
                sp.dma_start(ybuf[t % 2][0:rows(t), :], y_tok[t * P:t * P + rows(t), :]).then_inc(yin[t % 2], 16)

        @block.gpsimd
        def _(g):
            g.wait_ge(h_r, KD)
            g.dma_start(gainv, hgrn_norm.to_broadcast([P, P])).then_inc(attn_in, 16)
            g.wait_ge(f_r, 1)
            for v in range(AH * NL):
                h, n = v // NL, LEVELS[v % NL]
                cols = T if n <= 4 else SEQ
                g.wait_ge(e_r, v + 1)
                if v >= 2:
                    g.wait_ge(at_mm, unit_of(v - 2) + 1)
                g.tensor_tensor(kdec[v % 2][:, 0:cols], af[:, h, 0:cols], diff[v % 2][:, 0:cols], ALU.mult)\
                    .then_inc(kd_r, 1)
            g.wait_ge(qk_r, 1)
            for h in range(AH + 1):
                if h < 2:
                    g.dma_start(st0[h], state_hgrn[0, :, h].rearrange("n k v -> k n v")).then_inc(s0_in2[h], 16)
                if h:
                    g.wait_ge(sn_r, h)
                    g.dma_start(s_sample[0, :, h - 1].rearrange("n k v -> k n v"), st1[(h - 1) % 2])\
                        .then_inc(sn_out2[(h - 1) % 2], 16)
                    if h + 1 < AH:
                        g.wait_ge(so_mm, h)
                        g.dma_start(st0[(h + 1) % 2], state_hgrn[0, :, h + 1].rearrange("n k v -> k n v"))\
                            .then_inc(s0_in2[(h + 1) % 2], 16)
            g.wait_ge(s_up, PT_)
            g.dma_start(s_prompt[0, 0].rearrange("h k v -> k h v"), stP).then_inc(kv_out, 16)
            g.wait_ge(oa_r, 1)
            g.dma_start(arena[:, AG + 4608:AG + 4608 + ATTN[1] - ATTN[0]], consts[:, ATTN[0]:ATTN[1]]).then_inc(attn_in, 16)
            g.memset(arena[:, XR:XR + 1024], 0.0).then_inc(zeroed, 1)
            g.wait_ge(ob_r, PT_)
            for par in range(2):
                g.wait_ge(sn_out2[par], 32)
            for x in accS:
                g.memset(x, 0.0).then_inc(zeroed, 1)
            g.wait_ge(in_ev, 41)
            g.wait_ge(rope_r, 2)
            for t in range(PT_):
                for dst, x in ((k_prompt, bk), (v_prompt, bv)):
                    g.dma_start(dst[0, 0, :, t * P:(t + 1) * P, :].rearrange("h t d -> t h d"),
                                x[:, t, :].rearrange("p (h d) -> p h d", d=DH)).then_inc(kv_out, 16)
            for n in range(NSEQ):
                for dst, x in ((k_sample, bk), (v_sample, bv)):
                    g.dma_start(dst[0, n].rearrange("h t d -> t h d"),
                                x[8 * n:8 * n + 8, PT_, :].rearrange("p (h d) -> p h d", d=DH)).then_inc(kv_out, 16)
            g.wait_ge(ot_r, 4)
            for t in range(NT):
                g.dma_start(res[0:rows(t), t, :], src_x(t)).then_inc(xin2, 16)
            g.wait_ge(y_mm, 2 * NT)
            g.wait_ge(kv_out, 16 * (2 * (PT_ + NSEQ) + 1))
            g.dma_start(arena[:, BQ + 400:BQ + 400 + ROUTE[1] - ROUTE[0]], consts[:, ROUTE[0]:ROUTE[1]]).then_inc(wr_in, 16)
            g.dma_start(wr3[:, :, 0:NG], weights(w_group[0])).then_inc(wr_in, 16)
            for gr in range(NG):
                g.dma_start(wr3[:, :, NG + gr * EPG:NG + (gr + 1) * EPG], weights(w_er[0, gr])).then_inc(wr_in, 16)
            g.dma_start(brow[0:1, 0:NG], b_group).then_inc(wr_in, 16)
            g.dma_start(brow[0:1, NG:36], b_er.rearrange("a g e -> a (g e)")).then_inc(wr_in, 16)

            for t in range(NT):
                g.wait_ge(h2b_r, 2 * t + 2)
                g.dma_start(h2_rows[t * P:t * P + rows(t), :], xr[0:rows(t), t, :]).then_inc(h2_out, 16)
            g.wait_ge(g2_r, 4)
            g.memset(arena[:, QF:QF + 2048], 0.0).then_inc(g_cl, 1)
            g.wait_ge(g_cl, 1)
            g.wait_ge(tb_r, 2)
            g.wait_ge(h2_out, 16 * NT)

            def gather(j, i, par, first=False):
                if not first:
                    g.wait_ge(xt2, 2 * i + par - 1)
                g.tensor_copy(cur[:, par:par + 1], jobs_i[:, bass.ds(j, 1)]).then_inc(cur_r, 1)
                g.drain()
                g.indirect_dma_start(out=xg[par], out_offset=None, in_=h2_rows,
                                     in_offset=bass.IndirectOffsetOnAxis(ap=cur[:, par:par + 1], axis=0),
                                     bounds_check=T - 1, oob_is_err=False).then_inc(g_in2[par], 16)

            def scatter(j, par):
                g.wait_ge(yA, j + 2)
                g.wait_ge(yD, j + 2)
                g.tensor_copy(cur[:, 2 + par:3 + par], jobs_i[:, bass.ds(j + NJ + 2, 1)]).then_inc(cur_r, 1)
                g.drain()
                g.indirect_dma_start(out=y_rows, in_=yj[par], in_offset=None,
                                     out_offset=bass.IndirectOffsetOnAxis(ap=cur[:, 2 + par:3 + par], axis=0),
                                     bounds_check=2 * T - 1, oob_is_err=False).then_inc(sc2[par], 16)

            def pool_pair(i):
                for par in range(2):
                    gather(2 * i + 2 + par, i + 1, par)
                    scatter(2 * i + par, par)

            gather(0, 0, 0, first=True)
            gather(1, 0, 1, first=True)
            with g.Fori(0, NE // 2) as i:
                pool_pair(i)
            njobs = g.value_load(ctl[0:1, 8:9], min_val=0, max_val=EXTRA)
            with g.Fori(0, EXTRA // 2) as i:
                with g.If(njobs > 2 * i):
                    pool_pair(i + NE // 2)
            npairs = g.snap((njobs + 1) >> 1)
            for par in range(2):
                g.wait_ge(g_in2[par], (npairs + NE // 2 + 1) * 16)
                g.sem_inc(g_cl, 1)
            for t in range(NT):
                g.wait_ge(fin_v, t + 1)
                dst = y_prompt[0, t * P:(t + 1) * P, :] if t < PT_ else y_sample.rearrange("n t d -> (n t) d")
                g.dma_start(dst, ybuf[t % 2][0:rows(t), 0:D]).then_inc(ofree[t % 2], 16)
            g.wait_ge(ofree[0], 48)
            g.wait_ge(ofree[1], 32)
            g.wait_ge(kv_out, 16 * (2 * (PT_ + NSEQ) + 1))
            for par in range(2):
                g.wait_ge(sn_out2[par], 32)

        @block.scalar
        def _(act):
            act.wait_ge(cond_in, 32)
            act.activation(crow[0:NCOND, :], crow[0:NCOND, :], ACT.Silu).then_inc(silu_c, 1)
            act.wait_ge(lb_d, 1)
            act.activation(lb[:, 0:4], lb[:, 0:4], ACT.Sigmoid).then_inc(lb_r, 1)

            def squares(x, n):
                act.wait_ge(nrm, 3 * n + 1)
                for t in range(NT):
                    act.activation(part(arena, SC, D)[0:rows(t), :], x[0:rows(t), t, :], ACT.Square,
                                   accum_out=ssq[0:rows(t), t:t + 1]).then_inc(ssq_r, 1)
                    act.drain()
                act.wait_ge(nrm, 3 * n + 2)
                act.activation(rstd[:, 0:NT], ssq[:, 0:NT], ACT.Sqrt).then_inc(std_r, 1)

            act.wait_ge(xin, 16 * NT)
            squares(xr, 0)
            for u, (c, dst) in enumerate(in_units):
                act.wait_ge(in_mm, u + 1)
                rr, cc = dst.shape[0], dst.shape[1]
                fn = {0: ACT.Silu, 1: ACT.Sigmoid, 3: ACT.Silu}.get(c, ACT.Copy)
                act.activation(dst, ps[u % 4][0:rr, 0:cc], fn).then_inc(in_ev, 1)
                if u == 20:
                    act.wait_ge(f_r, 1)
                    act.activation(logf, logf, ACT.Ln).then_inc(lnf_r, 1)
            for v in range(AH * NL):
                cols = T if LEVELS[v % NL] <= 4 else SEQ
                act.wait_ge(d_r, v + 1)
                d = diff[v % 2][:, 0:cols]
                act.activation(d, d, ACT.Abs)
                act.drain()
                act.activation(d, d, ACT.Exp, scale=-1.0).then_inc(e_r, 1)
            act.activation(logf, bsum, ACT.Exp).then_inc(eb_r, 1)
            act.wait_ge(dl_r, 1)
            act.activation(bsum, bsum, ACT.Exp).then_inc(el_r, 1)
            for h in range(AH):
                act.wait_ge(kt_mm, h + 1)
                act.activation(kdT[:, h, 0:PT_, :], ps[4 + h % 2][:, :].rearrange("p (t k) -> p t k", k=P), ACT.Copy)
                act.activation(kdT[0:NSMP, h, PT_, :], ps[6 + h % 2][0:NSMP, 0:P], ACT.Copy).then_inc(kt_ev, 1)
            for c in range(PT_):
                act.wait_ge(o_mm, c + 1)
                act.activation(oa[:, c, :], ps[c % 2][:, :], ACT.Copy).then_inc(o_ev, 1)
            for h in range(AH):
                act.wait_ge(so_mm, h + 1)
                act.activation(soS[h % 2], ps[4 + h % 2][:, 0:NSMP], ACT.Copy).then_inc(so_ev, 1)
                act.wait_ge(so2_mm, h + 1)
                act.activation(oa[0:NSMP, PT_, h * P:(h + 1) * P], ps[6 + h % 2][0:NSMP, 0:P], ACT.Copy).then_inc(so_t, 1)
            act.wait_ge(hs_r, 1)
            act.activation(hss[:, :], hss[:, :], ACT.Sqrt).then_inc(hq_r, 1)
            for t in range(NT):
                act.wait_ge(oat_mm, t + 1)
                r = rows(t)
                act.activation(oaT[:, :, t * P:t * P + r], ps[t % 2][:, 0:4 * r].rearrange("p (k t) -> p k t", t=r),
                               ACT.Copy).then_inc(oat_r, 1)
            for u in range(2 * NT):
                x, t = (qT, kT)[u // NT], u % NT
                r = rows(t)
                act.wait_ge(qkt_mm, u + 1)
                act.activation(x[:, :, t * P:t * P + r], ps[2 + u % 2][:, 0:4 * r].rearrange("p (k t) -> p k t", t=r),
                               ACT.Copy).then_inc(qkt_r, 1)
            for u in range(PT_ * BH):
                i = u // BH
                act.wait_ge(mx_r, u + 1)
                if u >= 2:
                    act.wait_ge(pt_mm, u - 1)
                act.activation(prob[u % 2][:, 0:(i + 1) * P], ps[u % 2][:, 0:(i + 1) * P], ACT.Exp,
                               bias=mx[:, u:u + 1], scale=0.125, accum_out=sm[:, u:u + 1])
                act.drain().then_inc(ex_r, 1)
            for t in range(PT_):
                act.wait_ge(obt_mm, t + 1)
                act.activation(obT[:, :, t * P:(t + 1) * P], ps[4 + t % 2][:, :].rearrange("p (k t) -> p k t", t=P),
                               ACT.Copy).then_inc(obt_r, 1)
            def take_scores(p, b):
                act.wait_ge(ss_mm, p * NBLK + b + 1)
                act.activation(S[p % 2][:, b, :], ps[6 + b % 2][:, 0:256], ACT.Copy).then_inc(ss_ev, 1)

            def exps(p, b0, b1):
                if b0 == 0:
                    act.wait_ge(sb_r, p + 1)
                for b in range(b0, b1):
                    act.activation(S[p % 2][:, b, :], S[p % 2][:, b, :], ACT.Exp, bias=sbias[:, b:b + 1], scale=0.125,
                                   accum_out=ssum[:, b:b + 1])
                    act.drain()
                if b1 == NBLK:
                    act.activation(snew[p % 2], snew[p % 2], ACT.Exp, bias=sbias[:, 8:9], scale=0.125,
                                   accum_out=ssum[:, 8:9])
                    act.drain().then_inc(sp_r, 1)

            for kind, p in SAMPLE_PHASES:
                if kind == "k":
                    for b in range(NBLK):
                        for n in range(2):
                            w = (p * NBLK + b) * 2 + n
                            act.wait_ge(key_mm, w + 1)
                            if w >= 2:
                                act.wait_ge(qks, w - 1)
                            act.activation(keyT[w % 2][:, 0:4, :],
                                           ps[2 * (w % 2)][:, :].rearrange("p (h k) -> p h k", k=P), ACT.Copy).then_inc(keyA, 1)
                        if b:
                            take_scores(p, b - 1)
                        q = p * NBLK + b
                        act.wait_ge(qks, 2 * q + 2)
                        if q >= 2:
                            act.wait_ge(ss_mm, q - 1)
                        act.activation(stS[b % 2], ps[4 + b % 2][:, 0:256], ACT.Copy).then_inc(sq_ev, 1)
                        if p and b >= 4:
                            exps(p - 1, 2 * b - 8, 2 * b - 6)
                    take_scores(p, NBLK - 1)
                    act.wait_ge(nw_mm, p + 1)
                    for r in range(2):
                        x4, y4 = (x[0:64, 0:128].rearrange("p (m r c) -> p m r c", r=2, c=TS)[:, :, r, :]
                                  for x in (newT, ps[4 + r]))
                        ins = act.activation(x4, y4, ACT.Copy)
                    ins.then_inc(nw_ev, 1)
                else:
                    if p == 3:
                        exps(p, 0, NBLK)
                    for q in range(4):
                        act.wait_ge(sT_mm, 4 * p + q + 1)
                        for r in range(2):
                            ins = act.activation(
                                probsT[:, 2 * q:2 * q + 2, :, r, :],
                                ps[q][:, :].rearrange("p (a r e t) -> p a r e t", a=2, r=2, t=TS)[:, :, r], ACT.Copy)
                        ins.then_inc(sT_r, 1)
                    act.wait_ge(nT_mm, p + 1)
                    act.activation(pnewT[0:64, :], ps[4][0:64, 256:384], ACT.Copy).then_inc(nT_r, 1)
            for m in range(KD):
                act.wait_ge(g_mm, m + 1)
                if m >= 2:
                    act.wait_ge(mg_r, m - 1)
                for k in range(2):
                    act.activation(sig[2 * (m % 2) + k][:, 0:SEQ], ps[k][:, :], ACT.Sigmoid)
                    ins = act.activation(sig[2 * (m % 2) + k][:, SEQ:T], ps[4 + k][:, 0:NSMP], ACT.Sigmoid)
                ins.then_inc(g_r, 1)

            def gate_rows(dst, mm, done):
                for q in range(4):
                    act.wait_ge(mm, q + 1)
                    k, r = q % 2, (P, NSMP)[q // 2]
                    act.activation(dst[q // 2][0:r, 512 * k:512 * k + 512], ps[q][0:r, :], ACT.Copy).then_inc(done, 1)

            gate_rows(gate1, bc_mm, bc_r)
            squares(res, 1)
            for t in range(NT):
                for k in range(2):
                    act.wait_ge(h2b_mm, 2 * t + k + 1)
                    act.activation(xr[0:rows(t), t, 512 * k:512 * k + 512], ps[2 + k][0:rows(t), :],
                                   ACT.Copy).then_inc(h2b_r, 1)
            act.wait_ge(rt_a, 1)
            act.activation(rexp, rexp, ACT.Exp).then_inc(rt_b, 1)
            gate_rows(gate2, g2_mm, g2_r)

            def act_rows(i, par):
                act.wait_ge(xt2, 2 * i + par + 1)
                act.activation(xgT[par][:, 0:4, :], ps[0][:, :].rearrange("p (k s) -> p k s", s=CAP), ACT.Copy).then_inc(xtA, 1)

            def act_job(i, par, first=False):
                act.wait_ge(used[3 * par], i + (used0[3 * par] + 1))
                act.activation(hs, ps[2][:, :].rearrange("p (k s) -> p k s", s=CAP), ACT.Silu).then_inc(sl, 1)
                act_rows(i + par, 1 - par)
                act.wait_ge(used[3 * par + 2], i + (used0[3 * par + 2] + 1))
                if not first:
                    act.wait_ge(sc2[par], i * 16)
                act.activation(yj[par][:, 0:512], ps[4][:, :], ACT.Copy).then_inc(yA, 1)

            act_rows(0, 0)
            act_job(0, 0, first=True)
            act_job(0, 1, first=True)
            with act.Fori(1, NE // 2) as i:
                act_job(i, 0)
                act_job(i, 1)
            njobs = act.value_load(ctl[0:1, 8:9], min_val=0, max_val=EXTRA)
            with act.Fori(0, EXTRA // 2) as i:
                with act.If(njobs > 2 * i):
                    act_job(i + NE // 2, 0)
                    act_job(i + NE // 2, 1)
            for t in range(NT):
                act.wait_ge(fin_a, 2 * t + 1)
                act.activation(fsq[0:rows(t), :], ybuf[t % 2][0:rows(t), 0:D], ACT.Square,
                               accum_out=fss[0:rows(t), t:t + 1])
                act.drain().then_inc(fin_s, 1)
                act.wait_ge(fin_a, 2 * t + 2)
                act.activation(fss[0:rows(t), t:t + 1], fss[0:rows(t), t:t + 1], ACT.Sqrt).then_inc(fin_s, 1)

        @block.tensor
        def _(pe):
            MM, TR = pe.matmul, pe.transpose
            pe.wait_ge(c_in, 16)
            pe.wait_ge(vec_in, 80)
            TR(ps[2][:, 0:73], vecs[0:73, :], ident[0:73, 0:73]).then_inc(cvec_t, 1)
            pe.wait_ge(silu_c, 1)
            for k in range(KD):
                ins = TR(ps[1][:, k * NCOND:(k + 1) * NCOND], crow[0:NCOND, k * P:(k + 1) * P], ident[0:NCOND, 0:NCOND])
            ins.then_inc(cT_t, 1)
            pe.wait_ge(cT_r, 1)

            def turn_mod(n):
                pe.wait_ge(ada_cp, n + 1)
                for m in range(4):
                    ins = TR(ps[0][:, (4 * n + m) * NCOND:(4 * n + m + 1) * NCOND], arow[n % 2][0:NCOND, m * P:(m + 1) * P],
                             ident[0:NCOND, 0:NCOND])
                ins.then_inc(ada_t, 1)

            for n in range(12):
                slot, f, u = where[("ada", n)]
                pe.wait_ge(fill[slot], f)
                w = slot_view(slot, 8, 512)
                if n >= 2:
                    pe.wait_ge(ada_cp, n - 1)
                for k in range(KD):
                    ins = MM(ps[6 + n % 2][0:NCOND, :], cT[:, k * NCOND:(k + 1) * NCOND], w[:, k, :],
                             start=(k == 0), stop=(k == KD - 1))
                ins.then_inc(used[slot], 1)
                if n:
                    turn_mod(n - 1)
            turn_mod(11)

            def turn_rows(x, n):
                pe.wait_ge(xn_r, NT * n + NT)
                for k in range(KD):
                    if n * KD + k >= 2:
                        pe.wait_ge(h_r, n * KD + k - 1)
                    for t in range(PT_):
                        TR(ps[2 + k % 2][:, t * P:(t + 1) * P], x[:, t, k * P:(k + 1) * P], ident)
                    TR(ps[4 + k % 2][:, 0:NSMP], x[0:NSMP, PT_, k * P:(k + 1) * P], ident[0:NSMP, 0:NSMP]).then_inc(xt_r, 1)

            turn_rows(xr, 0)
            pe.wait_ge(h_r, KD)
            u = 0
            for c in range(7):
                slot, f, n = where[("in", c)]
                pe.wait_ge(fill[slot], f)
                w = slot_view(slot, 8, 512)
                for v in range(8 if c < 2 else NT):
                    if u >= 4:
                        pe.wait_ge(in_ev, u - 3)
                    for k in range(KD):
                        if c < 2:
                            m, cols = v // 2, (slice(0, SEQ), slice(SEQ, T))[v % 2]
                            out = ps[u % 4][:, 0:(SEQ, NSMP)[v % 2]]
                            ins = MM(out, w[:, k, m * P:(m + 1) * P], hT[:, k, cols], start=(k == 0), stop=(k == KD - 1))
                        else:
                            ins = MM(ps[u % 4][0:rows(v), :], hT[:, k, v * P:v * P + rows(v)], w[:, k, :],
                                     start=(k == 0), stop=(k == KD - 1))
                    ins.then_inc(in_mm, 1)
                    u += 1
                pe.wait_ge(in_mm, u)
                pe.sem_inc(used[slot], 1)
            pe.wait_ge(in_ev, 41)
            for w_ in range(AH * (NL + 1)):
                h, l = w_ // (NL + 1), w_ % (NL + 1)
                v = h * NL + l - 1
                if w_ >= 2:
                    pe.wait_ge(at_ac, w_ - 1)
                if l:
                    pe.wait_ge(qd_r, v + 1)
                    pe.wait_ge(kd_r, v + 1)
                    q_, k_ = qdec[v % 2], kdec[v % 2]
                else:
                    pe.wait_ge(f_r, 1)
                    q_, k_ = aq[:, h, :], af[:, h, :]
                for t in range(PT_):
                    ins = MM(ps[w_ % 2][:, t * P:(t + 1) * P], k_[:, t * P:(t + 1) * P], q_[:, t * P:(t + 1) * P],
                             start=True, stop=True)
                if l == 0 or LEVELS[l - 1] <= 4:
                    ins = MM(ps[2 + w_ % 2][0:NSMP, 0:NSMP], k_[:, SEQ:T], q_[:, SEQ:T], start=True, stop=True)
                ins.then_inc(at_mm, 1)
            pe.wait_ge(qk_r, 1)
            for h in range(AH):
                if h >= 2:
                    pe.wait_ge(kt_ev, h - 1)
                for t in range(PT_):
                    TR(ps[4 + h % 2][:, t * P:(t + 1) * P], af[:, h, t * P:(t + 1) * P], ident)
                TR(ps[6 + h % 2][0:NSMP, 0:P], af[:, h, SEQ:T], ident).then_inc(kt_mm, 1)
            pe.wait_ge(kt_ev, AH)
            pe.wait_ge(at_ac, AH * (NL + 1))
            for c in range(PT_):
                if c >= 2:
                    pe.wait_ge(s_up, c - 1)
                for h in range(AH):
                    ins = MM(ps[2 + c % 2][:, h * P:(h + 1) * P], kdT[:, h, c, :], ai[:, c, h * P:(h + 1) * P],
                             start=True, stop=True)
                ins.then_inc(s_mm, 1)
                if c:
                    pe.wait_ge(s_up, c)
                if c >= 2:
                    pe.wait_ge(o_ev, c - 1)
                for h in range(AH):
                    o = ps[c % 2][:, h * P:(h + 1) * P]
                    ins = MM(o, attnT[:, h, c * P:(c + 1) * P], ai[:, c, h * P:(h + 1) * P], start=True, stop=(c == 0))
                    if c:
                        ins = MM(o, aq[:, h, c * P:(c + 1) * P], stP[:, h, :], start=False, stop=True)
                ins.then_inc(o_mm, 1)
            pe.wait_ge(s_up, PT_)
            for h in range(AH):
                pe.wait_ge(s0_in2[h % 2], 16 * (h // 2 + 1))
                if h >= 2:
                    pe.wait_ge(so_ev, h - 1)
                o = ps[4 + h % 2]
                MM(o[:, 0:NSMP], ai[0:NSMP, PT_, h * P:(h + 1) * P], attnT[0:NSMP, h, SEQ:T], start=True, stop=False,
                   skip_group_check=True)
                for n in range(NSEQ):
                    ins = MM(o[:, n * TS:(n + 1) * TS], st0[h % 2][:, n, :], aq[:, h, SEQ + n * TS:SEQ + (n + 1) * TS],
                             start=False, stop=(n == NSEQ - 1), skip_group_check=True)
                ins.then_inc(so_mm, 1)
                pe.wait_ge(so_ev, h + 1)
                if h >= 2:
                    pe.wait_ge(so_t, h - 1)
                TR(ps[6 + h % 2][0:NSMP, 0:P], soS[h % 2], ident).then_inc(so2_mm, 1)
                pe.wait_ge(vb_r, h + 1)
                if h:
                    pe.wait_ge(sn_r, h)
                for k in range(2):
                    ins = MM(ps[2 + k][:, :], kdT[0:NSMP, h, PT_, :], vbd[0:NSMP, 4 * k:4 * k + 4, :].rearrange("p n v -> p (n v)"),
                             start=True, stop=True)
                ins.then_inc(sn_mm, 1)
            pe.wait_ge(oa_r, 1)
            for t in range(NT):
                if t >= 2:
                    pe.wait_ge(oat_r, t - 1)
                r = rows(t)
                for k in range(4):
                    ins = TR(ps[t % 2][:, k * r:(k + 1) * r], oa[0:r, t, k * P:(k + 1) * P], ident[0:r, 0:r])
                ins.then_inc(oat_mm, 1)
            pe.wait_ge(rope_r, 2)
            for u in range(2 * NT):
                x, t = (bq, bk)[u // NT], u % NT
                r = rows(t)
                if u >= 2:
                    pe.wait_ge(qkt_r, u - 1)
                for k in range(4):
                    ins = TR(ps[2 + u % 2][:, k * r:(k + 1) * r], x[0:r, t, k * P:(k + 1) * P], ident[0:r, 0:r])
                ins.then_inc(qkt_mm, 1)
            pe.wait_ge(qkt_r, 2 * NT)
            pe.wait_ge(oat_r, NT)
            NU = PT_ * BH
            for s_ in range(NU + 2):
                if s_ < NU:
                    i, h = s_ // BH, s_ % BH
                    if s_ >= 2:
                        pe.wait_ge(ex_r, s_ - 1)
                    q0 = 64 * (h % 2)
                    MM(ps[s_ % 2][:, 0:(i + 1) * P], qT[q0:q0 + 64, h // 2, i * P:(i + 1) * P],
                       kT[q0:q0 + 64, h // 2, 0:(i + 1) * P], start=True, stop=True).then_inc(sc_mm, 1)
                if 1 <= s_ <= NU:
                    u = s_ - 1
                    pe.wait_ge(ex_r, u + 1)
                    if u >= 2:
                        pe.wait_ge(pt_r, u - 1)
                    for k in range(u // BH + 1):
                        ins = TR(ps[2 + u % 2][:, k * P:(k + 1) * P], prob[u % 2][:, k * P:(k + 1) * P], ident)
                    ins.then_inc(pt_mm, 1)
                if s_ >= 2:
                    u = s_ - 2
                    i, h = u // BH, u % BH
                    pe.wait_ge(pt_r, u + 1)
                    if h == 0 and i >= 2:
                        pe.wait_ge(ob_r, i - 1)
                    for k in range(i + 1):
                        ins = MM(ps[4 + i % 2][:, h * DH:(h + 1) * DH], probT[u % 2][:, k * P:(k + 1) * P],
                                 bv[:, k, h * DH:(h + 1) * DH], start=(k == 0), stop=(k == i))
                    ins.then_inc(pv_mm, 1)
            pe.wait_ge(ob_r, PT_)
            pe.wait_ge(attn_in, 32)
            for t in range(PT_):
                if t >= 2:
                    pe.wait_ge(obt_r, t - 1)
                for k in range(4):
                    ins = TR(ps[4 + t % 2][:, k * P:(k + 1) * P], ob[:, t, k * P:(k + 1) * P], ident)
                ins.then_inc(obt_mm, 1)
            pe.wait_ge(qdup_r, 1)
            for h in range(BH):
                ins = TR(ps[6][:, h * 64:(h + 1) * 64],
                         qdup[0:NSMP, h, :], ident[0:NSMP, 0:NSMP])
            ins.then_inc(qb_mm, 1)
            pe.wait_ge(qb_r, 1)
            pe.wait_ge(obt_r, PT_)
            def turn_scores(p, b):
                q = p * NBLK + b
                pe.wait_ge(sq_ev, q + 1)
                if q >= 2:
                    pe.wait_ge(ss_ev, q - 1)
                if b == 0 and p >= 2:
                    pe.wait_ge(acc_r, p - 1)
                for r in range(2):
                    ins = TR(ps[6 + b % 2][:, r * P:(r + 1) * P], stS[b % 2][:, r * P:(r + 1) * P], ident)
                ins.then_inc(ss_mm, 1)

            def score(w):
                p, n, b = w // (2 * NBLK), w % 2, w // 2 % NBLK
                pe.wait_ge(keyA, w + 1)
                pe.wait_ge(keyD, w + 1)
                if b >= 2 or p:
                    pe.wait_ge(sq_ev, p * NBLK + b - 1)
                if b == 1 and p:
                    pe.wait_ge(sn_t, p)
                st = ps[4 + b % 2][:, 0:256].rearrange("p (r c) -> p r c", r=2)
                for h in range(BH):
                    ins = MM(st[:, :, n * 64 + h * 8:n * 64 + h * 8 + 8], keyT[w % 2][:, h, :],
                             qbd[:, 2 * p + n, h, :], start=True, stop=True)
                ins.then_inc(qks, 1)

            def key_phase(p):
                for b in range(NBLK):
                    for n in range(2):
                        w = (p * NBLK + b) * 2 + n
                        slot, f, _u = where[("k", p, b // 4, n)]
                        pe.wait_ge(fill[slot], f)
                        if w >= 2:
                            pe.wait_ge(keyA, w - 1)
                            pe.wait_ge(keyD, w - 1)
                        blk_ = ring[slot].rearrange("p (b h c) -> p b h c", b=4, h=BH)
                        for h in range(BH):
                            ins = TR(ps[2 * (w % 2) + h // 4][:, (h % 4) * P:(h % 4 + 1) * P], blk_[:, b % 4, h, :], ident)
                        ins.then_inc(key_mm, 1)
                        if b % 4 == 3:
                            pe.wait_ge(key_mm, w + 1)
                            pe.sem_inc(used[slot], 1)
                        if w > p * 2 * NBLK:
                            score(w - 1)
                        if n == 1 and b:
                            turn_scores(p, b - 1)
                score((p * NBLK + NBLK - 1) * 2 + 1)
                turn_scores(p, NBLK - 1)
                pe.wait_ge(sq_ev, (p + 1) * NBLK)
                nw = [ps[4 + r][0:64, 0:128].rearrange("p (n c) -> p n c", n=2) for r in range(2)]
                for h in range(BH):
                    q0 = 64 * (h % 2)
                    ins = MM(nw[h % 2][:, :, h * 8:h * 8 + 8], kT[q0:q0 + 64, h // 2, SEQ:T],
                             qT[q0:q0 + 64, h // 2, SEQ + 16 * p:SEQ + 16 * p + 16], start=True, stop=True)
                ins.then_inc(nw_mm, 1)
                pe.wait_ge(nw_ev, p + 1)
                TR(ps[5][:, 0:64], newT[0:64, :], ident[0:64, 0:64]).then_inc(nt_mm, 1)

            def out_place(n, h):
                e = n * BH + h
                return 32 * (e % 4), P * (e // 4)

            def value_phase(p):
                pe.wait_ge(sp_r, p + 1)
                for q in range(4):
                    for k in range(4):
                        c = 4 * q + k
                        ins = TR(ps[q][:, k * P:(k + 1) * P], S[p % 2][:, c // 2, (c % 2) * P:(c % 2 + 1) * P], ident)
                    ins.then_inc(sT_mm, 1)
                TR(ps[4][0:64, 256:384], snew[p % 2], ident).then_inc(nT_mm, 1)
                pe.wait_ge(ss_ev, min(p + 2, 4) * NBLK)
                if p:
                    pe.wait_ge(acc_r, p)
                for b in range(NBLK):
                    pe.wait_ge(sT_r, 4 * p + b // 2 + 1)
                    for n in range(2):
                        slot, f, _u = where[("v", p, b // 4, n)]
                        pe.wait_ge(fill[slot], f)
                        vals = ring[slot].rearrange("p (b h c) -> p b h c", b=4, h=BH)
                        for h in range(BH):
                            r0, c0 = out_place(n, h)
                            ins = MM(ps[6][r0:r0 + 16, c0:c0 + P], probsT[:, b, n * BH + h].rearrange("p r t -> p (r t)"),
                                     vals[:, b % 4, h, :], start=(b == 0 and n == 0 and h < 4), stop=False,
                                     skip_group_check=True)
                        if b % 4 == 3:
                            ins.then_inc(used[slot], 1)
                pe.wait_ge(nT_r, p + 1)
                for n in range(2):
                    for h in range(BH):
                        r0, c0 = out_place(n, h)
                        ins = MM(ps[6][r0:r0 + 8, c0:c0 + DH], pnewT[0:64, n * 64 + h * 8:n * 64 + h * 8 + 8],
                                 bv[0:NSMP, PT_, h * DH:(h + 1) * DH], start=False, stop=(n == 1 and h == BH - 1),
                                 skip_group_check=True)
                ins.then_inc(spv, 1)

            for kind, p in SAMPLE_PHASES:
                (key_phase if kind == "k" else value_phase)(p)
            for p in range(4):
                pe.wait_ge(acc_r, p + 1)
                for k in range(4):
                    ins = TR(ps[p][:, k * P:(k + 1) * P], accS[p][:, k, :], ident)
                ins.then_inc(acc_t, 1)
            for p in range(4):
                pe.wait_ge(od_r, p + 1)
                MM(ps[4 + p][:, 0:DH], odiag[p], C["fold"], start=True, stop=True).then_inc(of_mm, 1)
            for p in range(4):
                pe.wait_ge(or_r, p + 1)
                TR(ps[p][:, 0:P], orow[p], ident).then_inc(ot_mm, 1)
            pe.wait_ge(ot_r, 4)
            pe.wait_ge(kv_out, 16 * (2 * (PT_ + NSEQ) + 1))
            for m in range(KD):
                if m:
                    pe.wait_ge(g_r, m)
                for k_, c in ((0, 7 + m // 4), (1, 9 + m // 4)):
                    slot, f, _u = where[("in", c)]
                    pe.wait_ge(fill[slot], f)
                    w = slot_view(slot, 8, 512)
                    for cols, bank in ((slice(0, SEQ), ps[k_][:, :]), (slice(SEQ, T), ps[4 + k_][:, 0:NSMP])):
                        for k in range(KD):
                            ins = MM(bank, w[:, k, (m % 4) * P:(m % 4 + 1) * P], hT[:, k, cols], start=(k == 0), stop=(k == KD - 1))
                    if k_:
                        ins.then_inc(g_mm, 1)
                    if m % 4 == 3:
                        if k_:
                            pe.wait_ge(g_mm, m + 1)
                            pe.sem_inc(used[slot], 1)
                        else:
                            ins.then_inc(used[slot], 1)
                if m:
                    pe.wait_ge(mg_r, m)
                for k_, (what, x) in enumerate(((("pa",), oaT), (("pb",), obT))):
                    slot, f, _u = where[what]
                    pe.wait_ge(fill[slot], f)
                    w = slot_view(slot, 4, D)
                    for cols, bank in ((slice(0, SEQ), ps[2 + k_][:, :]), (slice(SEQ, T), ps[6 + k_][:, 0:NSMP])):
                        for k in range(4):
                            ins = MM(bank, w[:, k, m * P:(m + 1) * P], x[:, k, cols], start=(k == 0), stop=(k == 3))
                    if k_:
                        ins.then_inc(pr_mm, 1)
            pe.wait_ge(pr_mm, KD)
            pe.sem_inc(used[where[("pa",)][0]], 1)
            pe.sem_inc(used[where[("pb",)][0]], 1)

            def gate_banks(m0, mm):
                pe.wait_ge(gseq_r, 1 + m0 // 40)
                for q in range(4):
                    for j in range(4):
                        m = m0 + 4 * (q % 2) + j
                        if q < 2:
                            ins = TR(ps[q][:, j * P:(j + 1) * P], m3[:, m, 0:1].to_broadcast([P, P]), ident)
                        else:
                            ins = TR(ps[q][0:NSMP, j * P:(j + 1) * P], gseq[m0 // 40][:, m - m0, :], ident)
                    ins.then_inc(mm, 1)

            pe.wait_ge(g_r, KD)
            pe.wait_ge(mg_r, KD)
            gate_banks(16, bc_mm)
            banks = (4, 5, 6, 7)
            for t in range(NT):
                for k_ in range(2):
                    u = 2 * t + k_
                    slot, f, _u = where[("out", k_)]
                    pe.wait_ge(fill[slot], f)
                    if u >= 4:
                        pe.wait_ge(y_r, u - 3)
                    w = slot_view(slot, 8, 512)
                    r = rows(t)
                    for k in range(KD):
                        ins = MM(ps[banks[u % 4]][0:r, :], merged[:, k, t * P:t * P + r], w[:, k, :], start=(k == 0), stop=(k == KD - 1))
                    ins.then_inc(y_mm, 1)
            pe.wait_ge(y_mm, 2 * NT)
            for k_ in range(2):
                pe.sem_inc(used[where[("out", k_)][0]], 1)
            pe.wait_ge(bc_r, 4)
            turn_rows(xr, 1)
            pe.wait_ge(h_r, 2 * KD)
            pe.wait_ge(wr_in, 16 * 8)
            for t in range(NT):
                r = rows(t)
                for k in range(KD):
                    MM(ps[0][0:r, t * 36:(t + 1) * 36], hT[:, k, t * P:t * P + r], wr3[:, k, :], start=(k == 0), stop=False)
                ins = MM(ps[0][0:r, t * 36:(t + 1) * 36], onerow[:, 0:r], brow[0:1, :], start=False, stop=True)
            ins.then_inc(lg_mm, 1)
            for t in range(NT):
                r = rows(t)
                for k_ in range(2):
                    if t:
                        pe.wait_ge(h2b_r, 2 * t + k_ - 1)
                    for k in range(4):
                        ins = TR(ps[2 + k_][0:r, k * P:(k + 1) * P], hT[:, 4 * k_ + k, t * P:t * P + r], ident)
                    ins.then_inc(h2b_mm, 1)
            pe.wait_ge(oh_r, 1)
            for t in range(NT):
                out = ps[1][:, t * NE:(t + 1) * NE]
                MM(out, before, msum[:, t, :], start=True, stop=(t == 0))
                for t2 in range(t):
                    MM(out, ones, msum[:, t2, :], start=False, stop=(t2 == t - 1))
            for t in range(NT):
                ins = MM(ps[1][:, NT * NE:(NT + 1) * NE], ones, msum[:, t, :], start=(t == 0), stop=(t == NT - 1))
            ins.then_inc(rk_mm, 1)
            for c in range(2 * NT):
                pe.wait_ge(oh_r, 2 + c)
                ins = MM(ps[4][:, 0:NJ + 2], slot1[c % 2], job1[c % 2], start=(c == 0), stop=(c == 2 * NT - 1))
                ins.then_inc(tb_mm, 1)
            pe.wait_ge(h2b_r, 2 * NT)
            pe.wait_ge(rk_r, 1)
            gate_banks(40, g2_mm)
            pe.wait_ge(g2_r, 4)
            pe.wait_ge(tb_r, 2)

            for free in (xtA, xtD, hd, yA, yD):
                pe.sem_inc(free, 1)

            def turn_job(i, par):
                j = 2 * i + par
                pe.wait_ge(g_in2[par], i * 16 + 16)
                pe.wait_ge(xtA, j + 1)
                pe.wait_ge(xtD, j + 1)
                for k in range(KD):
                    ins = TR(ps[k // 4][:, (k % 4) * P:(k % 4 + 1) * P], xg[par][:, k * P:(k + 1) * P], ident)
                ins.then_inc(xt2, 1)

            def pe_job(i, par):
                j = 2 * i + par
                pe.wait_ge(xtA, j + 2)
                pe.wait_ge(xtD, j + 2)
                pe.wait_ge(hd, j + 1)
                for c in range(2):
                    s_ = 3 * par + c
                    pe.wait_ge(fill[s_], i * 16 + (fill0[s_] + 16))
                    w = slot_view(s_, 8, 512)
                    for f in range(4):
                        for k in range(KD):
                            ins = MM(ps[2 + c][:, f * P:(f + 1) * P], w[:, k, f * P:(f + 1) * P], xgT[par][:, k, :],
                                     start=(k == 0), stop=(k == KD - 1))
                    ins.then_inc(used[s_], 1)
                turn_job(i + par, 1 - par)
                s_ = 3 * par + 2
                pe.wait_ge(fill[s_], i * 16 + (fill0[s_] + 16))
                pe.wait_ge(hd, j + 2)
                pe.wait_ge(yA, j + 1)
                pe.wait_ge(yD, j + 1)
                w = slot_view(s_, 4, D)
                for c in range(2):
                    for f in range(4):
                        ins = MM(ps[4 + c][:, :], hid[:, f, :], w[:, f, 512 * c:512 * c + 512], start=(f == 0), stop=(f == 3))
                ins.then_inc(used[s_], 1)

            turn_job(0, 0)
            with pe.Fori(0, NE // 2) as i:
                pe_job(i, 0)
                pe_job(i, 1)
            njobs = pe.value_load(ctl[0:1, 8:9], min_val=0, max_val=EXTRA)
            with pe.Fori(0, EXTRA // 2) as i:
                with pe.If(njobs > 2 * i):
                    pe_job(i + NE // 2, 0)
                    pe_job(i + NE // 2, 1)

        @block.vector
        def _(v):
            TT, TSC, STT, CP = v.tensor_tensor, v.tensor_scalar, v.scalar_tensor_tensor, v.tensor_copy
            RED = v.tensor_reduce
            v.wait_ge(c_in, 16)
            v.memset(ssq[:, :], 1.0).then_inc(nrm, 1)
            v.wait_ge(cvec_t, 1)
            CP(colv[:, 0:73], ps[2][:, 0:73])
            v.drain()
            TT(lb[:, 0:4], colv[:, 64:68], colv[:, 68:72], ALU.subtract).then_inc(lb_d, 1)
            v.wait_ge(cT_t, 1)
            CP(cT, ps[1][:, 0:KD * NCOND]).then_inc(cT_r, 1)
            v.wait_ge(lb_r, 1)
            TSC(omlb, lb[:, 0:4], -1.0, 1.0, ALU.mult, ALU.add)

            def norm_rows(x, dst, n):
                v.wait_ge(ssq_r, NT * (n + 1))
                TSC(ssq[:, 0:NT], ssq[:, 0:NT], 1.0 / D, EPS, ALU.mult, ALU.add).then_inc(nrm, 1)
                v.wait_ge(std_r, n + 1)
                v.reciprocal(rstd[:, 0:NT], rstd[:, 0:NT]).then_inc(nrm, 1)
                v.drain()
                for t in range(NT):
                    r = rows(t)
                    TSC(dst[0:r, t, :], x[0:r, t, :], rstd[0:r, t:t + 1], None, ALU.mult).then_inc(xn_r, 1)

            def modulate(A, shift, n):
                A3 = A[:, :].rearrange("p (k n) -> p k n", n=NCOND)
                for k in range(KD):
                    v.wait_ge(xt_r, n * KD + k + 1)
                    tail = hT[:, k, SEQ:T].rearrange("p (n t) -> p n t", t=TS)
                    TT(tail, ps[4 + k % 2][:, 0:NSMP].rearrange("p (n t) -> p n t", t=TS),
                       A3[:, k, 1:NCOND].unsqueeze(2).to_broadcast([P, NSEQ, TS]), ALU.mult)
                    TSC(hT[:, k, 0:SEQ], ps[2 + k % 2][:, :], A3[:, k, 0:1], m3[:, shift + k, 0:1], ALU.mult, ALU.add)
                    v.drain()
                    TT(tail, tail, m3[:, shift + k, 1:NCOND].unsqueeze(2).to_broadcast([P, NSEQ, TS]), ALU.add)\
                        .then_inc(h_r, 1)

            norm_rows(xr, xr, 0)
            for c in range(12):
                slot, _f, n = where[("ada", c)]
                v.wait_ge(used[slot], n + 1)
                if c >= 2:
                    v.wait_ge(ada_t, c - 1)
                CP(arow[c % 2][0:NCOND, :], ps[6 + c % 2][0:NCOND, :]).then_inc(ada_cp, 1)
            v.wait_ge(ada_t, 12)
            TT(m3, ps[0][:, 0:48 * NCOND].rearrange("p (m n) -> p m n", n=NCOND),
               colv[:, 0:48].unsqueeze(2).to_broadcast([P, 48, NCOND]), ALU.add)
            v.drain()
            for A, scale, gain in ((A1, 8, 48), (A2, 32, 56)):
                STT(A[:, :].rearrange("p (k n) -> p k n", n=NCOND), m3[:, scale:scale + KD, :], 1.0,
                    colv[:, gain:gain + KD].unsqueeze(2).to_broadcast([P, KD, NCOND]), ALU.add, ALU.mult)
            v.drain().then_inc(mod_ready, 1)
            modulate(A1, 0, 0)
            v.wait_ge(in_ev, 16)
            for h in range(AH):
                TSC(logf[:, h, :], af[:, h, :], omlb[:, h:h + 1], lb[:, h:h + 1], ALU.mult, ALU.add)
            v.drain()
            TSC(af, logf, -1.0, 1.0, ALU.mult, ALU.add).then_inc(f_r, 1)
            v.wait_ge(lnf_r, 1)
            v.wait_ge(lvl_in, 48)
            for h in range(AH):
                v.tensor_tensor_scan(bsum[:, h, :], reset, logf[:, h, :], 0.0, ALU.mult, ALU.add)
            v.drain()

            def difference(x):
                h, n = x // NL, LEVELS[x % NL]
                cols = T if n <= 4 else SEQ
                if x >= 2:
                    v.wait_ge(kd_r, x - 1)
                b = bsum[:, h, 0:cols].rearrange("p (j c) -> p j c", c=2 * n)
                TT(diff[x % 2][:, 0:cols].rearrange("p (j c) -> p j c", c=2 * n), b,
                   b[:, :, n - 1:n].to_broadcast([P, cols // (2 * n), 2 * n]), ALU.subtract).then_inc(d_r, 1)

            def accumulate(w):
                h, l = w // (NL + 1), w % (NL + 1)
                mask = level[:, NL if l == 0 else l - 1, :]
                v.wait_ge(at_mm, w + 1)
                acc = attnT[:, h, 0:SEQ]
                tail = attnT[0:NSMP, h, SEQ:T]
                m4 = mask.unsqueeze(1).to_broadcast([P, PT_, P])
                src = ps[w % 2][:, :].rearrange("p (t c) -> p t c", c=P)
                small = ps[2 + w % 2][0:NSMP, 0:NSMP]
                if l == 0:
                    TT(acc.rearrange("p (t c) -> p t c", c=P), src, m4, ALU.mult)
                    TT(tail, small, mask[0:NSMP, 0:NSMP], ALU.mult)
                else:
                    TT(atmp[:, 0:SEQ].rearrange("p (t c) -> p t c", c=P), src, m4, ALU.mult)
                    if LEVELS[l - 1] <= 4:
                        TT(atmp[0:NSMP, SEQ:T], small, mask[0:NSMP, 0:NSMP], ALU.mult)
                    v.drain()
                    TT(acc, acc, atmp[:, 0:SEQ], ALU.add)
                    if LEVELS[l - 1] <= 4:
                        TT(tail, tail, atmp[0:NSMP, SEQ:T], ALU.add)
                v.drain().then_inc(at_ac, 1)

            difference(0)
            done = 0
            for x in range(AH * NL):
                if x + 1 < AH * NL:
                    difference(x + 1)
                v.wait_ge(e_r, x + 1)
                if x >= 2:
                    v.wait_ge(at_mm, unit_of(x - 2) + 1)
                h, n = x // NL, LEVELS[x % NL]
                cols = T if n <= 4 else SEQ
                TT(qdec[x % 2][:, 0:cols], aq[:, h, 0:cols], diff[x % 2][:, 0:cols], ALU.mult).then_inc(qd_r, 1)
                while done < unit_of(x):
                    accumulate(done)
                    done += 1
            accumulate(done)
            v.wait_ge(eb_r, 1)
            last = blk[:, 0:48].rearrange("p (h c) -> p h c", c=12)
            e3 = ebl[:, :].rearrange("p (h c) -> p h c", c=12)
            for src, dst in ((logf, e3), (bsum, last)):
                CP(dst[:, :, 0:PT_], src[:, :, P - 1:SEQ:P])
                CP(dst[:, :, PT_:12], src[:, :, SEQ + TS - 1:T:TS])
            TT(aq, aq, logf, ALU.mult)
            v.drain()
            for h in range(AH):
                b = bsum[:, h, 0:SEQ].rearrange("p (j c) -> p j c", c=P)
                TT(b, last[:, h, 0:PT_].unsqueeze(2).to_broadcast([P, PT_, P]), b, ALU.subtract)
                b = bsum[:, h, SEQ:T].rearrange("p (j c) -> p j c", c=TS)
                TT(b, last[:, h, PT_:12].unsqueeze(2).to_broadcast([P, NSEQ, TS]), b, ALU.subtract)
            v.drain().then_inc(dl_r, 1)
            v.wait_ge(el_r, 1)
            TT(af, af, bsum, ALU.mult).then_inc(qk_r, 1)
            for c in range(PT_):
                v.wait_ge(s_mm, c + 1)
                if c:
                    v.wait_ge(o_mm, c + 1)
                for h in range(AH):
                    new = ps[2 + c % 2][:, h * P:(h + 1) * P]
                    if c:
                        ins = STT(stP[:, h, :], stP[:, h, :], e3[:, h, c:c + 1], new, ALU.mult, ALU.add)
                    else:
                        ins = CP(stP[:, h, :], new)
                v.drain().then_inc(s_up, 1)
            for h in range(AH):
                if h:
                    v.wait_ge(sn_mm, h)
                TT(vbd[0:NSMP, :, :], ai[0:NSMP, PT_, h * P:(h + 1) * P].unsqueeze(1).to_broadcast([NSMP, NSEQ, P]),
                   C["seqmask"][0:NSMP, :].unsqueeze(2).to_broadcast([NSMP, NSEQ, P]), ALU.mult).then_inc(vb_r, 1)
                v.wait_ge(s0_in2[h % 2], 16 * (h // 2 + 1))
                if h >= 2:
                    v.wait_ge(sn_out2[h % 2], 16 * (h // 2))
                TT(st1[h % 2], st0[h % 2], e3[:, h, PT_:12].unsqueeze(2).to_broadcast([P, NSEQ, P]), ALU.mult)
                v.drain()
                v.wait_ge(sn_mm, h + 1)
                for k in range(2):
                    x = st1[h % 2][:, 4 * k:4 * k + 4, :]
                    ins = TT(x, x, ps[2 + k][:, :].rearrange("p (n c) -> p n c", c=P), ALU.add)
                ins.then_inc(sn_r, 1)
            v.wait_ge(o_ev, PT_)
            v.wait_ge(so_t, AH)
            v.wait_ge(attn_in, 16)
            tiles = ((P, 0, PT_), (NSMP, PT_, NT))

            def heads(x, r, t0, t1):
                return x[0:r, t0:t1, :].rearrange("p t (h c) -> p (t h) c", c=P)

            v.memset(hss[:, :], 1.0)
            v.drain()
            for r, t0, t1 in tiles:
                o = heads(oa, r, t0, t1)
                TT(osqr[0:r, t0 * AH:t1 * AH, :], o, o, ALU.mult)
                v.drain()
                RED(hss[0:r, t0 * AH:t1 * AH], osqr[0:r, t0 * AH:t1 * AH, :], AX, ALU.add)
            v.drain()
            TSC(hss[:, :], hss[:, :], 1.0 / P, EPS, ALU.mult, ALU.add).then_inc(hs_r, 1)
            v.wait_ge(hq_r, 1)
            v.reciprocal(hss[:, :], hss[:, :])
            v.drain()
            for r, t0, t1 in tiles:
                o = heads(oa, r, t0, t1)
                n = (t1 - t0) * AH
                TT(o, o, hss[0:r, t0 * AH:t1 * AH].unsqueeze(2).to_broadcast([r, n, P]), ALU.mult)
                v.drain()
                TT(o, o, gainv[0:r, :].unsqueeze(1).to_broadcast([r, n, P]), ALU.mult)
                v.drain()
                TT(o, o, heads(ag, r, t0, t1), ALU.mult)
            v.drain().then_inc(oa_r, 1)
            v.wait_ge(attn_in, 32)
            cos = C["cos"].rearrange("p (t f) -> p t f", f=8)
            sin = C["sin"].rearrange("p (t f) -> p t f", f=8)
            v.wait_ge(in_ev, 41)
            for x in (bq, bk):
                for r, t0, t1 in tiles:
                    n = t1 - t0
                    for t in range(t0, t1):
                        x3 = x[0:r, t, :].rearrange("p (h c) -> p h c", c=DH)
                        x1, x2 = x3[:, :, 0:8], x3[:, :, 8:16]
                        cb = cos[0:r, t, :].unsqueeze(1).to_broadcast([r, BH, 8])
                        sb_ = sin[0:r, t, :].unsqueeze(1).to_broadcast([r, BH, 8])
                        q4 = [part(arena, XR + 4864 + 64 * k, 64)[0:r].rearrange("p (h c) -> p h c", c=8) for k in range(4)]
                        TT(q4[0], x1, cb, ALU.mult)
                        TT(q4[1], x2, sb_, ALU.mult)
                        TT(q4[2], x1, sb_, ALU.mult)
                        TT(q4[3], x2, cb, ALU.mult)
                        v.drain()
                        TT(x1, q4[0], q4[1], ALU.subtract)
                        TT(x2, q4[2], q4[3], ALU.add)
                        v.drain()
                v.drain().then_inc(rope_r, 1)
            NU = PT_ * BH
            for s_ in range(NU + 3):
                if s_ < NU:
                    i = s_ // BH
                    v.wait_ge(sc_mm, s_ + 1)
                    own = ps[s_ % 2][:, i * P:(i + 1) * P]
                    TT(own, own, C["causal"], ALU.add)
                    v.drain()
                    RED(amx[:, s_:s_ + 1], ps[s_ % 2][:, 0:(i + 1) * P], AX, ALU.max)
                    v.drain()
                    TSC(mx[:, s_:s_ + 1], amx[:, s_:s_ + 1], -0.125, None, ALU.mult).then_inc(mx_r, 1)
                if 1 <= s_ <= NU:
                    u = s_ - 1
                    v.wait_ge(pt_mm, u + 1)
                    if u >= 2:
                        v.wait_ge(pv_mm, u - 1)
                    n = (u // BH + 1) * P
                    CP(probT[u % 2][:, 0:n], ps[2 + u % 2][:, 0:n]).then_inc(pt_r, 1)
                if s_ >= 2 and (s_ - 2) % BH == BH - 1:
                    i = (s_ - 2) // BH
                    v.wait_ge(pv_mm, BH * (i + 1))
                    v.reciprocal(amx[:, 32:40], sm[:, BH * i:BH * (i + 1)])
                    v.drain()
                    TT(ob[:, i, :].rearrange("p (h c) -> p h c", c=DH), ps[4 + i % 2][:, :].rearrange("p (h c) -> p h c", c=DH),
                       amx[:, 32:40].unsqueeze(2).to_broadcast([P, BH, DH]), ALU.mult).then_inc(ob_r, 1)
                    v.drain()
            q3 = bq[0:NSMP, PT_, :].rearrange("p (h d) -> p h d", d=DH)
            for k in range(2):
                CP(qdup[0:NSMP, :, k * DH:(k + 1) * DH], q3)
            v.drain().then_inc(qdup_r, 1)
            v.wait_ge(qb_mm, 1)
            v.wait_ge(zeroed, 1)
            src = ps[6][:, :].rearrange("p (h n t) -> p n h t", h=BH, t=TS)
            CP(qbd[0:64, :, :, 0:8], src[0:64])
            CP(qbd[64:128, :, :, 8:16], src[64:128])
            v.drain().then_inc(qb_r, 1)
            def choose_blocks(p, step):
                Sp, sn = S[p % 2], snew[p % 2]
                if step == 0:
                    v.wait_ge(nt_mm, p + 1)
                    m0 = 8 * (6 - 2 * p)
                    TT(sn, ps[5][:, 0:64], C["newmask"][:, m0:m0 + 64], ALU.add)
                    v.drain().then_inc(sn_t, 1)
                    v.wait_ge(ss_ev, NBLK * (p + 1))
                    RED(bs8[:, 0:8], Sp, AX, ALU.add)
                    v.drain()
                if step == 1:
                    RED(bm8[:, 0:8], Sp, AX, ALU.max)
                    RED(nm1, sn, AX, ALU.max)
                    v.drain()
                    bj = bs8[:, 0:8].unsqueeze(1).to_broadcast([P, 8, 8])
                    bi = bs8[:, 0:8].unsqueeze(2).to_broadcast([P, 8, 8])
                    TT(gt8, bj, bi, ALU.is_gt)
                    TT(eq8, bj, bi, ALU.is_equal)
                    v.drain()
                    TT(eq8, eq8, C["tie"].rearrange("p (i j) -> p i j", j=8), ALU.mult)
                    v.drain()
                    TT(gt8, gt8, eq8, ALU.add)
                    v.drain()
                if step == 2:
                    RED(rank8[:, 0:8], gt8, AX, ALU.add)
                    v.drain()
                    TSC(soff[:, 0:8], rank8[:, 0:8], float(TOPK), -BIG, ALU.is_ge, ALU.mult)
                    v.drain()
                    TT(bm8[:, 0:8], bm8[:, 0:8], soff[:, 0:8], ALU.add)
                    v.drain()
                    RED(m1_, bm8[:, 0:8], AX, ALU.max)
                    v.drain()
                if step == 3:
                    TT(m1_, m1_, nm1, ALU.max)
                    v.drain()
                    TSC(sbias[:, 8:9], m1_, -0.125, None, ALU.mult)
                    v.drain()
                    TSC(sbias[:, 0:8], soff[:, 0:8], sbias[:, 8:9], None, ALU.add).then_inc(sb_r, 1)

            v.wait_ge(zeroed, 5)
            for kind, p in SAMPLE_PHASES:
                if kind == "k":
                    for b in range(NBLK):
                        for n in range(2):
                            w = (p * NBLK + b) * 2 + n
                            v.wait_ge(key_mm, w + 1)
                            if w >= 2:
                                v.wait_ge(qks, w - 1)
                            CP(keyT[w % 2][:, 4:8, :], ps[2 * (w % 2) + 1][:, :].rearrange("p (h k) -> p h k", k=P))\
                                .then_inc(keyD, 1)
                        if p and b < 4:
                            choose_blocks(p - 1, b)
                else:
                    if p == 3:
                        for step in range(4):
                            choose_blocks(p, step)
                    v.wait_ge(sp_r, p + 1)
                    RED(rs1[p], ssum, AX, ALU.add)
                    v.drain()
                    v.reciprocal(rs1[p], rs1[p])
                    v.wait_ge(spv, p + 1)
                    for r0 in (0, 32, 64, 96):
                        CP(accS[p][r0:r0 + 16], ps[6][r0:r0 + 16, :].rearrange("p (k c) -> p k c", c=P))
                    v.drain().then_inc(acc_r, 1)
            for p in range(4):
                v.wait_ge(acc_t, p + 1)
                a3 = ps[p][:, :].rearrange("p (e c) -> p e c", c=32)
                o3 = odiag[p].rearrange("p (e t) -> p e t", t=TS)
                CP(o3[0:64], a3[0:64, :, 0:TS])
                CP(o3[64:128], a3[64:128, :, TS:2 * TS])
                v.drain().then_inc(od_r, 1)
            for p in range(4):
                v.wait_ge(of_mm, p + 1)
                for k in range(2):
                    TSC(orow[p][:, k * DH:(k + 1) * DH], ps[4 + p][:, 0:DH], rs1[p], None, ALU.mult)
                v.drain().then_inc(or_r, 1)
            for p in range(4):
                v.wait_ge(ot_mm, p + 1)
                for par in range(2):
                    s4 = ps[p][64 * par:64 * par + 64, 0:P]\
                        .rearrange("p (n k r t) -> p k n r t", n=2, r=2, t=TS)[:, :, :, par, :]
                    d4 = obT[64 * par:64 * par + 64, :, SEQ + 16 * p:SEQ + 16 * p + 16].rearrange("p k (n t) -> p k n t", t=TS)
                    CP(d4, s4)
                v.drain().then_inc(ot_r, 1)
            v.wait_ge(kv_out, 16 * (2 * (PT_ + NSEQ) + 1))
            for m in range(KD):
                v.wait_ge(g_r, m + 1)
                v.wait_ge(pr_mm, m + 1)
                for k in range(2):
                    x = sig[2 * (m % 2) + k]
                    TT(x[:, 0:SEQ], x[:, 0:SEQ], ps[2 + k][:, :], ALU.mult)
                    TT(x[:, SEQ:T], x[:, SEQ:T], ps[6 + k][:, 0:NSMP], ALU.mult)
                v.drain()
                TT(merged[:, m, :], sig[2 * (m % 2)], sig[2 * (m % 2) + 1], ALU.add).then_inc(mg_r, 1)
            def spread_gates(k, m0):
                for m in range(KD):
                    CP(gseq[k][:, m, :].rearrange("p (n t) -> p n t", t=TS),
                       m3[:, m0 + m, 1:NCOND].unsqueeze(2).to_broadcast([P, NSEQ, TS]))
                v.drain().then_inc(gseq_r, 1)

            spread_gates(0, 16)
            v.wait_ge(xin2, 16 * NT)
            v.wait_ge(bc_r, 4)
            banks = (4, 5, 6, 7)
            for t in range(NT):
                r = rows(t)
                gt = gate1[0 if t < PT_ else 1]
                for k in range(2):
                    u = 2 * t + k
                    cols = slice(512 * k, 512 * k + 512)
                    v.wait_ge(y_mm, u + 1)
                    TT(xr[0:r, t, cols], ps[banks[u % 4]][0:r, :], gt[0:r, cols], ALU.mult).then_inc(y_r, 1)
                v.drain()
                TT(res[0:r, t, :], res[0:r, t, :], xr[0:r, t, :], ALU.add).then_inc(x2_r, 1)
            spread_gates(1, 40)
            v.memset(ssq[:, :], 1.0).then_inc(nrm, 1)
            norm_rows(res, xr, 1)
            modulate(A2, 24, 1)
            v.wait_ge(wr_in, 16 * 8)
            v.memset(lg, 0.0)
            v.drain()
            v.wait_ge(lg_mm, 1)
            l3 = ps[0][:, 0:NT * 36].rearrange("p (t n) -> p t n", n=36)
            CP(lg[:, 0:PT_, :], l3[:, 0:PT_, :])
            CP(lg[0:NSMP, PT_, :], l3[0:NSMP, PT_, :])
            v.drain()
            rank_of = C["ranks8"]

            def first_max(x, n, oh):
                mxv, vm = rt(NT), rt(NT)
                RED(mxv, x, AX, ALU.max)
                v.drain()
                TT(oh, x, mxv.unsqueeze(2).to_broadcast([P, NT, n]), ALU.is_equal)
                v.drain()
                TT(oh, oh, rank_of[:, 0:n].unsqueeze(1).to_broadcast([P, NT, n]), ALU.mult)
                v.drain()
                RED(vm, oh, AX, ALU.max)
                v.drain()
                TT(oh, oh, vm.unsqueeze(2).to_broadcast([P, NT, n]), ALU.is_equal)
                v.drain()
                return mxv

            def bc(x, n):
                return x.unsqueeze(2).to_broadcast([P, NT, n])

            G, E3 = lg[:, :, 0:NG], lg[:, :, NG:36]
            ohg = rt(NT, NG)
            gm = first_max(G, NG, ohg)
            TT(rexp[:, :, 0:NG], G, bc(gm, NG), ALU.subtract)
            pick = rt(NT, NE)
            for t in range(NT):
                TT(pick[:, t, :].rearrange("p (g e) -> p g e", e=EPG), E3[:, t, :].rearrange("p (g e) -> p g e", e=EPG),
                   ohg[:, t, :].unsqueeze(2).to_broadcast([P, NG, EPG]), ALU.mult)
            v.drain()
            esel = rt(NT, EPG)
            for t in range(NT):
                RED(esel[:, t, :], pick[:, t, :].rearrange("p (g e) -> p e g", e=EPG), AX, ALU.add)
            v.drain()
            oh = [rt(NT, EPG), rt(NT, EPG)]
            top1 = first_max(esel, EPG, oh[0])
            esel2 = rt(NT, EPG)
            STT(esel2, oh[0], -BIG, esel, ALU.mult, ALU.add)
            v.drain()
            top2 = first_max(esel2, EPG, oh[1])
            TT(rexp[:, :, NG], top2, top1, ALU.subtract)
            v.drain().then_inc(rt_a, 1)
            valid = C["valid"]
            for k in range(2):
                for t in range(NT):
                    TT(onehots[:, k, t, :].rearrange("p (g e) -> p g e", e=EPG), ohg[:, t, :].unsqueeze(2).to_broadcast([P, NG, EPG]),
                       oh[k][:, t, :].unsqueeze(1).to_broadcast([P, NG, EPG]), ALU.mult)
                v.drain()
                TT(onehots[:, k, :, :], onehots[:, k, :, :], bc(valid, NE), ALU.mult)
            v.drain()
            TT(msum, onehots[:, 0, :, :], onehots[:, 1, :, :], ALU.add).then_inc(oh_r, 1)
            v.wait_ge(rt_b, 1)
            den, e21 = rt(NT), rt(NT)
            RED(den, rexp[:, :, 0:NG], AX, ALU.add)
            TSC(e21, rexp[:, :, NG], 1.0, None, ALU.add)
            v.drain()
            TT(den, den, e21, ALU.mult)
            v.drain()
            v.reciprocal(wts[:, 0:NT], den)
            v.drain()
            TT(wts[:, NT:2 * NT], wts[:, 0:NT], rexp[:, :, NG], ALU.mult)
            v.wait_ge(rk_mm, 1)
            rt_at[0] = HT
            cnt, extra, cum, obase = rt(NE), rt(NE), rt(NE), rt(NE)
            ranks = rt(NT, NE)
            CP(ranks, ps[1][:, 0:NT * NE].rearrange("p (t e) -> p t e", e=NE))
            CP(cnt, ps[1][:, NT * NE:(NT + 1) * NE])
            v.drain().then_inc(rk_r, 1)
            TSC(extra, cnt, float(CAP) + 0.5, None, ALU.is_ge)
            v.drain()
            for m in range(2, T // CAP + 1):
                STT(extra, cnt, float(m * CAP) + 0.5, extra, ALU.is_ge, ALU.add)
                v.drain()
            v.tensor_tensor_scan(cum, ones[:, 0:NE], extra, 0.0, ALU.mult, ALU.add)
            v.drain()
            TT(obase, cum, extra, ALU.subtract)
            v.drain()
            rk, ex, ob_, jq, sl_, jb, pay, tm5 = (rt(2, NT) for _ in range(8))
            tmpE = pick
            for k in range(2):
                for dst, row in ((rk, ranks), (ex, C["iotaE"].unsqueeze(1).to_broadcast([P, NT, NE])),
                                 (ob_, obase.unsqueeze(1).to_broadcast([P, NT, NE]))):
                    TT(tmpE, onehots[:, k, :, :], row, ALU.mult)
                    v.drain()
                    RED(dst[:, k, :], tmpE, AX, ALU.add)
                    v.drain()
            TSC(jq, rk, float(CAP) - 0.5, None, ALU.is_ge)
            v.drain()
            for m in range(2, T // CAP + 1):
                STT(jq, rk, float(m * CAP) - 0.5, jq, ALU.is_ge, ALU.add)
                v.drain()
            STT(sl_, jq, -float(CAP), rk, ALU.mult, ALU.add)
            TSC(tm5, jq, 0.5, None, ALU.is_ge)
            TT(jb, ob_, jq, ALU.add)
            v.drain()
            STT(jb, jb, float(NE - 1), ex, ALU.add, ALU.subtract)
            v.drain()
            TT(jb, jb, tm5, ALU.mult)
            v.drain()
            TT(jb, jb, ex, ALU.add)
            for k in range(2):
                STT(pay[:, k, :], valid, float(k), C["payload"], ALU.mult, ALU.add)
            v.drain()
            for c in range(2 * NT):
                k, t = c // NT, c % NT
                if c >= 2:
                    v.wait_ge(tb_mm, c - 1)
                TSC(slot1[c % 2], C["iota"], sl_[:, k, t:t + 1], None, ALU.is_equal)
                TSC(job1[c % 2], C["iota"][:, 0:NJ + 2], jb[:, k, t:t + 1], pay[:, k, t:t + 1], ALU.is_equal, ALU.mult)
                v.drain().then_inc(oh_r, 1)
            je, jw = rt(EXTRA), rt(EXTRA, NE)
            big = [rt(EXTRA, NE), rt(EXTRA, NE)]
            jrow = C["iota"][:, 0:EXTRA].unsqueeze(2).to_broadcast([P, EXTRA, NE])
            TT(big[0], jrow, obase.unsqueeze(1).to_broadcast([P, EXTRA, NE]), ALU.is_ge)
            TT(big[1], jrow, cum.unsqueeze(1).to_broadcast([P, EXTRA, NE]), ALU.is_lt)
            v.drain()
            TT(jw, big[0], big[1], ALU.mult)
            v.drain()
            TT(jw, jw, C["iotaE"].unsqueeze(1).to_broadcast([P, EXTRA, NE]), ALU.mult)
            v.drain()
            RED(je, jw, AX, ALU.add)
            v.drain()
            CP(ctl[:, 0:EXTRA], je)
            CP(ctl[:, 8:9], cum[:, NE - 1:NE])
            v.drain().then_inc(tb_r, 1)
            v.wait_ge(tb_mm, 2 * NT)
            tab, emp = rt(NJ + 2), rt(NJ + 2)
            TSC(emp, ps[4][:, 0:NJ + 2], 0.5, ABSENT, ALU.is_lt, ALU.mult)
            v.drain()
            STT(tab, ps[4][:, 0:NJ + 2], -1.0, emp, ALU.add, ALU.add)
            v.drain()
            CP(jobs_i[:, NJ + 2:2 * NJ + 4], tab)
            v.drain()
            TSC(jobs_i[:, 0:NJ + 2], jobs_i[:, NJ + 2:2 * NJ + 4], 1, None, ALU.arith_shift_right).then_inc(tb_r, 1)

            def dve_rows(i, par):
                v.wait_ge(xt2, 2 * i + par + 1)
                CP(xgT[par][:, 4:8, :], ps[1][:, :].rearrange("p (k s) -> p k s", s=CAP)).then_inc(xtD, 1)

            def dve_job(i, par, first=False):
                j = 2 * i + par
                v.wait_ge(sl, j + 1)
                v.wait_ge(used[3 * par + 1], i + (used0[3 * par + 1] + 1))
                TT(hid, hs, ps[3][:, :].rearrange("p (k s) -> p k s", s=CAP), ALU.mult).then_inc(hd, 1)
                dve_rows(i + par, 1 - par)
                v.wait_ge(used[3 * par + 2], i + (used0[3 * par + 2] + 1))
                if not first:
                    v.wait_ge(sc2[par], i * 16)
                CP(yj[par][:, 512:1024], ps[5][:, :]).then_inc(yD, 1)

            dve_rows(0, 0)
            dve_job(0, 0, first=True)
            dve_job(0, 1, first=True)
            with v.Fori(1, NE // 2) as i:
                dve_job(i, 0)
                dve_job(i, 1)
            njobs = v.value_load(ctl[0:1, 8:9], min_val=0, max_val=EXTRA)
            with v.Fori(0, EXTRA // 2) as i:
                with v.If(njobs > 2 * i):
                    dve_job(i + NE // 2, 0)
                    dve_job(i + NE // 2, 1)
            v.wait_ge(gfin, 16)
            for t in range(NT):
                r = rows(t)
                y = ybuf[t % 2]
                v.wait_ge(yin[t % 2], 16 * (t // 2 + 1))
                y0, y1 = y[0:r, 0:D], y[0:r, D:2 * D]
                TSC(y0, y0, wts[0:r, t:t + 1], None, ALU.mult)
                v.drain()
                STT(y0, y1, wts[0:r, NT + t:NT + t + 1], y0, ALU.mult, ALU.add)
                v.drain()
                TT(y0, y0, gate2[0 if t < PT_ else 1][0:r, :], ALU.mult)
                v.drain()
                TT(y0, y0, res[0:r, t, :], ALU.add).then_inc(fin_a, 1)
                v.wait_ge(fin_s, 2 * t + 1)
                TSC(fss[0:r, t:t + 1], fss[0:r, t:t + 1], 1.0 / D, EPS, ALU.mult, ALU.add).then_inc(fin_a, 1)
                v.wait_ge(fin_s, 2 * t + 2)
                v.reciprocal(fss[0:r, t:t + 1], fss[0:r, t:t + 1])
                v.drain()
                STT(y0, y0, fss[0:r, t:t + 1], fgain[0:r, :], ALU.mult, ALU.mult).then_inc(fin_v, 1)


def shape_constants():
    import numpy as np
    c = np.zeros((P, NCONST), np.float32)

    def put(name, a):
        at, n = CONST[name]
        c[:, at:at + n] = np.asarray(a, np.float32).reshape(P, n)

    p, q = np.arange(P)[:, None], np.arange(P)[None, :]
    put("ident", p == q)
    put("before", p < q)
    put("ones", np.ones((P, P)))
    put("causal", np.where(q <= p, 0.0, -BIG))
    m, s = np.arange(14)[None, :, None], np.arange(8)[None, None, :]
    n2, t = (np.arange(P) // 64)[:, None, None], (np.arange(P) % 8)[:, None, None]
    put("newmask", np.where((m == n2 + 6) & (s <= t), 0.0, -BIG))
    put("fold", (p % 64) == np.arange(64)[None, :])
    half = 8
    inv = np.power(np.float32(500000.0), -(np.arange(half, dtype=np.float32) * np.float32(2.0) / np.float32(16)))
    pos = np.zeros((P, NT), np.float32)
    pos[:, 0:PT_] = np.arange(P)[:, None] + P * np.arange(PT_)[None, :]
    pos[:, PT_] = 2048 + np.arange(P) % TS
    ang = (pos[:, :, None] * inv[None, None, :]).astype(np.float32)
    put("cos", np.cos(ang))
    put("sin", np.sin(ang))
    put("iota", np.broadcast_to(q, (P, P)))
    put("ranks8", np.broadcast_to(8 - np.arange(8), (P, 8)))
    put("iotaE", np.broadcast_to(np.arange(NE), (P, NE)))
    put("seqmask", (p // TS) == np.arange(8)[None, :])
    put("tie", np.broadcast_to(np.arange(8)[None, :] < np.arange(8)[:, None], (P, 8, 8)))
    row = np.arange(P)[:, None] + P * np.arange(NT)[None, :]
    put("valid", row < T)
    put("payload", np.where(row < T, 2 * row + 1, 0))
    col = np.arange(T)
    put("reset", np.broadcast_to(np.where(col < SEQ, col % P != 0, col % TS != 0), (P, T)))
    lv = np.zeros((P, 8, P))
    for i, n in enumerate(LEVELS):
        lv[:, i] = (p // (2 * n) == q // (2 * n)) & (p % (2 * n) < n) & (q % (2 * n) >= n)
    lv[:, 7] = p == q
    put("levels", lv)
    return c


_INS = ["x_prompt", "x_sample", "c_prompt", "c_sample", "cache_k", "cache_v", "state_hgrn", "page_table", "w_ada",
        "b_ada", "norm_mix", "norm_ffn", "w_in", "hgrn_lb_logits", "hgrn_norm", "w_proj_a", "w_proj_b", "w_out",
        "w_group", "b_group", "w_expert_router", "b_expert_router", "w_gate", "w_up", "w_down", "norm_final"]
_OUTS = [(1, SEQ, D), (NSEQ, TS, D), (1, 1, BH, SEQ, DH), (1, 1, BH, SEQ, DH), (1, 1, AH, P, P),
         (1, NSEQ, BH, TS, DH), (1, NSEQ, BH, TS, DH), (1, NSEQ, AH, P, P)]


def kernel(**inputs):
    import numpy as _np
    import concourse.bacc as _bacc
    from concourse import mybir as _mybir
    from concourse.bass_utils import run_bass_kernel_spmd as _run

    nc = _bacc.Bacc("TRN2", target_bir_lowering=False, num_devices=1)
    arrays, args = {}, []
    given = [(name, _np.ascontiguousarray(inputs[name])) for name in _INS] + [("shape_constants", shape_constants())]
    for name, a in given:
        arrays[f"in_{name}_dram"] = a
        args.append(nc.dram_tensor(f"in_{name}_dram", a.shape, _mybir.dt.from_np(a.dtype), kind="ExternalInput").ap())
    for i, shape in enumerate(_OUTS):
        args.append(nc.dram_tensor(f"out_{i}_dram", shape, F32, kind="ExternalOutput").ap())
    bass_hybrid_step(nc, *args)
    r = _run(nc, [arrays], core_ids=[0])
    return tuple(r.results[0][f"out_{i}_dram"] for i in range(len(_OUTS)))
```

```python
from contextlib import ExitStack

import concourse.bass as bass
from concourse import mybir

F32 = mybir.dt.float32
I32 = mybir.dt.int32
ALU = mybir.AluOpType
ACT = mybir.ActivationFunctionType
AX = mybir.AxisListType.X

P = 128
D = 1024
KD = D // P
SEQ = 512
NSEQ = 8
TS = 8
NSMP = NSEQ * TS
T = SEQ + NSMP
PT_ = SEQ // P
NT = PT_ + 1
NCOND = 1 + NSEQ
AH = 4
BH = 8
DH = 64
BLK = 256
NBLK = 8
PAGE = 128
TOPK = 3
EPS = 1e-6
NG, EPG = 4, 8
NE = NG * EPG
DE = 512
CAP = 128
EXTRA = 8
NJ = NE + EXTRA
BIG = 1.0e30
ABSENT = 8192.0
CHUNK = 4096
SAMPLE_PHASES = (("k", 0), ("k", 1), ("v", 0), ("k", 2), ("v", 1), ("k", 3), ("v", 2), ("v", 3))
IN_ORDER = (0, 1, 4, 5, 2, 3, 6)
LEVELS = (64, 32, 16, 8, 4, 2, 1)
NL = len(LEVELS)

CONST = {}
_at = 0
for _name, _n in (("ident", 128), ("ones", 128), ("seqmask", 8), ("cos", NT * 8), ("sin", NT * 8),
                  ("causal", 128), ("newmask", 112), ("fold", 64), ("tie", 64),
                  ("before", 128), ("iota", 128), ("iotaE", NE), ("ranks8", 8), ("valid", NT), ("payload", NT),
                  ("reset", T), ("levels", 8 * 128)):
    CONST[_name] = (_at, _n)
    _at += _n
NCONST = _at
KEPT = CONST["causal"][0]
ATTN = (KEPT, CONST["before"][0])
ROUTE = (ATTN[1], CONST["reset"][0])


def part(t, at, *dims):
    n = 1
    for d in dims:
        n *= d
    v = t[:, at:at + n]
    if len(dims) == 1:
        return v
    names = "abcde"[:len(dims)]
    return v.rearrange("p (" + " ".join(names) + ") -> p " + " ".join(names), **dict(zip(names, dims)))


def bass_hybrid_step(nc, x_prompt, x_sample, c_prompt, c_sample, cache_k, cache_v, state_hgrn, page_table,
                     w_ada, b_ada, norm_mix, norm_ffn, w_in, lb_logits, hgrn_norm, w_proj_a, w_proj_b, w_out,
                     w_group, b_group, w_er, b_er, w_gate, w_up, w_down, norm_final, consts,
                     y_prompt, y_sample, k_prompt, v_prompt, s_prompt, k_sample, v_sample, s_sample):
    h2_rows = nc.dram_tensor("h2_rows", (T, D), F32, kind="Internal").ap()
    y_rows = nc.dram_tensor("y_rows", (2 * T, D), F32, kind="Internal").ap()

    with ExitStack() as ctx:
        def sb(name, cols, dt=F32):
            return ctx.enter_context(nc.sbuf_tensor(name, [P, cols], dt))

        def sem(name):
            return ctx.enter_context(nc.semaphore(name))

        ps = [ctx.enter_context(nc.psum_tensor(f"bank{i}", [P, 512], F32)) for i in range(8)]

        arena = sb("arena", 6 * CHUNK + 4608 + 5120 + 17408)
        ringA = 0
        SC = 4 * CHUNK
        HT = 6 * CHUNK
        XR = HT + 4608
        QF = XR + 5120
        AG = QF + 4608
        BQ = AG + 5120
        ring = [part(arena, ringA + s * CHUNK, CHUNK) for s in range(6)]
        hT = part(arena, HT, KD, T)
        xr = part(arena, XR, NT, D)
        aq = part(arena, QF, AH, T)
        af = part(arena, QF + 2304, AH, T)
        ai = part(arena, AG, NT, 512)
        ag = part(arena, AG + 2560, NT, 512)
        bqkv = [part(arena, BQ + 2560 * i, NT, 512) for i in range(3)]
        bq, bk, bv = bqkv
        bsum = part(arena, SC, AH, T)
        diff = [part(arena, SC + 2304 + 576 * i, T) for i in range(2)]
        qdec = [part(arena, SC + 3456 + 576 * i, T) for i in range(2)]
        kdec = [part(arena, SC + 4608 + 576 * i, T) for i in range(2)]
        atmp = part(arena, SC + 5760, T)
        level = part(arena, SC + 7168, 8, 128)
        attnT = part(arena, XR, AH, T)
        logf = part(arena, XR + 2304, AH, T)
        kdT = part(arena, XR + 2304, AH, NT, 128)
        oa = part(arena, SC, NT, 512)
        stP = part(arena, SC + 2560, AH, 128)
        st0 = [part(arena, SC + 3072 + 1024 * i, NSEQ, 128) for i in range(2)]
        st1 = [part(arena, SC + 5120 + 1024 * i, NSEQ, 128) for i in range(2)]
        vbd = part(arena, SC + 7168, NSEQ, 128)
        oaT = part(arena, QF, AH, T)
        obT = part(arena, QF + 2304, AH, T)
        qT = part(arena, AG, 4, T)
        qT_odd = part(arena, XR + 1024, 4, SEQ)
        kT = part(arena, AG + 2304, 4, T)
        prob = [part(arena, SC + 512 * i, 512) for i in range(2)]
        probT = [part(arena, SC + 1024 + 512 * i, 512) for i in range(2)]
        ob = part(arena, SC + 2048, NT, 512)
        qbd = part(arena, XR, NSEQ, BH, 16)
        keyT = [part(arena, XR + 1024 + 1024 * i, BH, 128) for i in range(2)]
        stS = [part(arena, XR + 3072 + 256 * i, 256) for i in range(2)]
        newT = part(arena, XR + 3584, 128)
        pnewT = part(arena, XR + 3712, 128)
        odiag = [part(arena, XR + 1024 + 128 * i, 128) for i in range(4)]
        orow = [part(arena, XR + 1536 + 128 * i, 128) for i in range(4)]
        snew = [part(arena, XR + 4096 + 64 * i, 64) for i in range(2)]
        qdup = part(arena, XR + 1024, BH, 128)
        gseq = [part(arena, SC + 4352, KD, NSMP), part(arena, BQ + 720, KD, NSMP)]
        S = [part(arena, SC + a, NBLK, 256) for a in (4608, 2048)]
        accS = [part(arena, SC + a, 4, P) for a in (6656, 7168, 7680, 4096)]
        probsT = part(arena, SC, NBLK, 2 * BH, 2, TS)
        merged = part(arena, BQ, KD, T)
        sig = [part(arena, SC + 576 * i, T) for i in range(4)]
        res = part(arena, AG, NT, D)
        gate1 = [part(arena, SC + 2304 + 1024 * i, D) for i in range(2)]
        xg = [part(arena, QF + 1024 * i, D) for i in range(2)]
        xgT = [part(arena, QF + 2048 + 1024 * i, KD, CAP) for i in range(2)]
        hs = part(arena, BQ, 4, CAP)
        hid = part(arena, BQ + 512, 4, CAP)
        yj = [part(arena, BQ + 1024 + 1024 * i, D) for i in range(2)]
        onehots = part(arena, BQ + 3072, 2, NT, NE)
        gate2 = [part(arena, BQ + 4096 + 1024 * i, D) for i in range(2)]

        ROUTER = BQ + 7680 - 324 - (ROUTE[1] - ROUTE[0])
        cst = sb("cst", KEPT)
        C = {}
        for n, (a, k) in CONST.items():
            if a < KEPT:
                C[n] = cst[:, a:a + k]
            elif a < ATTN[1]:
                C[n] = part(arena, AG + 4608 + a - ATTN[0], k)
            elif a < ROUTE[1]:
                C[n] = part(arena, ROUTER + 324 + a - ROUTE[0], k)
        ident, ones, before = C["ident"], C["ones"], C["before"]
        reset = part(arena, SC + 6400, T)
        vecs = part(arena, SC + 3072, 128)
        colv = sb("colv", 80)
        gainv = part(arena, XR + 4992, 128)
        crow = part(arena, SC + 2048, D)
        cT = part(arena, SC + 3328, KD * NCOND)
        arow = [part(arena, SC + 3584 + 512 * i, 512) for i in range(2)]
        modT = sb("modT", 48 * NCOND)
        m3 = modT[:, :].rearrange("p (m n) -> p m n", n=NCOND)
        A1 = sb("A1", KD * NCOND)
        A2 = sb("A2", KD * NCOND)
        lb = sb("lb", 8)
        omlb = lb[:, 4:8]
        ssq = sb("ssq", 8)
        rstd = sb("rstd", 8)
        hss = sb("hss", NT * AH)
        ebl = sb("ebl", AH * 12)
        mx = sb("mx", 40)
        sm = sb("sm", 40)
        amx = part(arena, XR + 4480, 40)
        blk = sb("blk", 64)
        wr = part(arena, ROUTER, KD * 36)
        wr3 = wr.rearrange("p (k n) -> p k n", n=36)
        brow = part(arena, ROUTER + 288, 36)
        onerow = ones[0:1, 0:128]
        pages = sb("pages", 128, I32)
        soS = [part(arena, XR + 4864 + 64 * i, 64) for i in range(2)]
        jobs_i = sb("jobs_i", 2 * NJ + 4, I32)
        cur = sb("cur", 4, I32)
        ctl = sb("ctl", 16, I32)
        wts = sb("wts", 2 * NT)

        def S_(*names):
            return [sem(n) for n in names]

        c_in, xin, lvl_in, wr_in, attn_in = S_(
            "consts_in", "x_in", "levels_in", "router_in", "attention_constants_in")
        fill = [sem(f"slot{s}_filled") for s in range(6)]
        used = [sem(f"slot{s}_used") for s in range(6)]

        plan = [("ada", n) for n in range(12)] + [("in", n) for n in IN_ORDER]
        for kind, p in SAMPLE_PHASES:
            plan += [(kind, p, c) for c in range(4)]
        plan += [("pa",), ("pb",), ("in", 7), ("in", 9), ("in", 8), ("in", 10), ("out", 0), ("out", 1)]
        slots = [n % 4 for n in range(len(plan) - 8)]
        first = len(slots) % 4
        slots += [(first + n) % 4 for n in (0, 1, 2, 3, 2, 3, 0, 1)]
        filled, taken = [0] * 6, [0] * 6
        loads, where = [], {}
        for what, slot in zip(plan, slots):
            filled[slot] += 128 if what[0] in ("k", "v") else 16
            where[what] = (slot, filled[slot], taken[slot])
            loads.append((what, *where[what]))
            taken[slot] += 1
        fill0, used0 = filled, taken

        cvec_t, cT_t, cT_r, silu_c = S_(
            "vectors_transposed", "cond_transposed", "cond_ready", "silu_c")
        ssq_r, std_r, xn_r, xt_r, h_r = S_("row_squares", "row_std", "rows_normed", "rows_transposed", "hT_ready")
        in_mm, in_ev, zeroed = S_("in_proj_done", "in_proj_copied", "tails_zeroed")
        f_r, lnf_r = S_("f_ready", "log_f_ready")
        d_r, e_r, qd_r, kd_r, at_mm, at_ac = S_("diff_ready", "decay_ready", "q_decayed", "k_decayed",
                                              "attn_done", "attn_added")
        eb_r, dl_r, el_r, qk_r, kt_mm, kt_ev = S_("exp_b", "diff_last", "exp_last", "qk_ready", "kd_transposed",
                                                "kd_copied")
        o_mm, s_mm, s_up, o_ev = S_("o_done", "state_product", "state_ready", "o_copied")
        vb_r, so_mm, so_ev, sn_mm, sn_r, so_t = S_(
            "v_blocked", "so_done", "so_copied", "new_state_product",
            "new_state_ready", "so_turned_copied")
        hs_r, hq_r, oa_r, oat_mm, oat_r = S_("o_squares", "o_std", "oa_ready", "oa_transposed", "oaT_ready")
        rope_r, qkt_mm, qkt_r = S_("rope_ready", "qk_transposed", "qkT_ready")
        sc_mm, mx_r, ex_r, pt_mm, pt_r, pv_mm, ob_r = S_("scores_done", "max_ready", "probs_ready", "probs_transposed",
                                                       "probsT_ready", "pv_done", "ob_rows")
        qb_mm, qb_r, key_mm, keyA, keyD, sq_ev, ss_mm, ss_ev = S_(
            "qdup_done", "qblock_ready", "keys_transposed", "keysT_a", "keysT_b", "sscores_copied",
            "sscores_turned", "S_ready")
        nw_mm, nw_ev, nt_mm, sb_r, sp_r, sT_mm, sT_r, nT_mm, nT_r = S_(
            "new_scores", "new_copied", "new_turned", "sbias_ready", "sprobs_ready", "sprobs_turned", "sprobsT_ready",
            "newprobs_turned", "newprobsT_ready")
        spv, od_r, of_mm, or_r, ot_mm, ot_r = S_("spv_done", "odiag_ready", "ofold_done", "orow_ready",
                                               "orow_turned", "ob_sample_ready")
        obt_mm, obt_r = S_("ob_transposed", "obT_ready")
        g_mm, g_r, pr_mm, mg_r, bc_mm, bc_r, y_mm, x2_r, xin2 = S_(
            "gates_done", "gates_ready", "branch_done", "merged_ready", "gatebc_done", "gatebc_ready", "y_done",
            "x2_ready", "x_again")
        h2b_mm, h2b_r, h2_out, lg_mm = S_("h2_turned", "h2_rows_ready", "h2_stored", "logits_done")
        rt_a, rt_b, rk_mm, rk_r, oh_r, tb_mm, tb_r = S_("route_max", "route_exp", "ranks_done", "ranks_taken",
                                                      "onehot_ready", "table_done", "table_ready")
        g_cl, xt2, xtA, xtD, sl, hd, yA, yD = S_(
            "gather_cleared", "job_transposed", "jobT_a", "jobT_b", "silu_done",
            "hid_ready", "job_y_a", "job_y_b")
        g_in2 = [sem(f"gathered{i}") for i in range(2)]
        sc2 = [sem(f"scattered{i}") for i in range(2)]
        s0_in2 = [sem(f"state_in{i}") for i in range(2)]
        sn_out2 = [sem(f"state_out{i}") for i in range(2)]
        kv_out, g2_mm, g2_r = S_("kv_stored", "gate2_done", "gate2_ready")
        so2_mm, lb_r, nrm = S_("so_turn_done", "lb_ready", "norm_scale")
        yin = [sem(f"y_in{t}") for t in range(NT)]
        fin_w, fin_a, fin_s, fin_v = S_("second_choice_weighed", "final_sums", "final_std", "final_rows")
        epsv = sm[:, 0:1]
        rows_out = sem("final_rows_stored")

        acc_r, acc_t, sn_t = S_("outputs_copied", "outputs_turned", "snew_ready")
        h_a, mod_r = S_("hT_prompt_ready", "modulation_ready")
        ada_cp, ada_t = S_("mod_rows_copied", "mod_turned")
        qdup_r, gseq_r, y_r = S_("qdup_ready", "gates_spread", "y_taken")
        qks = sem("sample_scores_done")
        sbias, ssum, soff, bs8, bm8, rank8 = (blk[:, a:a + 9] for a in (0, 9, 18, 27, 36, 45))
        nm1, m1_ = (blk[:, a:a + 1] for a in (54, 55))
        rs1 = [blk[:, a:a + 1] for a in (56, 57, 58, 59)]
        gt8, eq8 = (part(arena, XR + 4352 + a, 8, 8) for a in (0, 64))
        ybuf = [part(arena, 2 * D * t, 2 * D) for t in range(NT)]
        fgain = part(arena, 2 * D * NT, D)
        fsq = part(arena, 2 * D * NT + D, D)
        fss = ssq
        msum = part(arena, BQ + 3392, NT, NE)
        slot1 = [part(arena, BQ + 3552 + 128 * i, 128) for i in range(2)]
        job1 = [part(arena, BQ + 3808 + 48 * i, NJ + 2) for i in range(2)]
        rt_at = [BQ + 6144]

        def rt(*dims):
            n = 1
            for d in dims:
                n *= d
            rt_at[0] += n
            assert rt_at[0] <= ROUTER or rt_at[0] <= HT + 4608
            return part(arena, rt_at[0] - n, *dims)

        lg = rt(NT, 36)
        rexp = rt(NT, 5)

        def unit_of(v):
            return v // NL * (NL + 1) + v % NL + 1

        HALVES = (slice(0, T // 2), slice(T // 2, T))
        in_units = []
        for c, x in ((0, aq), (1, af)):
            for m in range(4):
                in_units += [(c, x[:, m, cols]) for cols in HALVES]
        for c, x in ((4, bq), (5, bk), (2, ai), (3, ag), (6, bv)):
            in_units += [(c, x[0:(P if t < PT_ else NSMP), t, :]) for t in range(NT)]

        in_bank = [u % 4 + (4 if u >= 16 else 0) for u in range(len(in_units))]
        EARLY, PRODUCTS = 19, AH * (NL + 1)
        in_after = [[] for _ in range(PRODUCTS)]
        for u in range(EARLY, len(in_units)):
            in_after[(u - EARLY) * PRODUCTS // (len(in_units) - EARLY)].append(u)

        shared = {what for what in where if what[:2] in (("k", 2), ("k", 3), ("v", 3)) and what[2] < 2}

        def load_pages(eng, what, pgs):
            kind, p, c = what
            slot, cache = where[what][0], cache_k if kind == "k" else cache_v
            dst = ring[slot].rearrange("p (b h c) -> p b h c", b=4, h=BH)
            for at in range(4):
                for pg in pgs:
                    j = (2 * p + at // 2) * 16 + (2 * c + at % 2) * 2 + pg
                    page = eng.value_load(pages[0:1, j:j + 1], min_val=0, max_val=cache.shape[1] - 1)
                    src = cache[0, bass.ds(page, 1)].rearrange("o h (i r) d -> i (o h) (r d)", r=2)
                    eng.dma_start(dst[64 * pg:64 * pg + 64, at], src).then_inc(fill[slot], 16)

        block = ctx.enter_context(nc.Block())

        def rows(t):
            return P if t < PT_ else NSMP

        def src_x(t):
            return x_prompt[0, t * P:(t + 1) * P, :] if t < PT_ else x_sample.rearrange("n t d -> (n t) d")

        def weights(w):
            return w.rearrange("(k p) n -> p k n", p=P)

        def slot_view(s, k, n):
            return ring[s].rearrange("p (k n) -> p k n", n=n)

        @block.sync
        def _(sp):
            sp.dma_start(cst[:, :], consts[:, 0:KEPT]).then_inc(c_in, 16)
            sp.dma_start(crow[0:1, :], c_prompt).then_inc(c_in, 16)
            sp.dma_start(crow[1:NCOND, :], c_sample).then_inc(c_in, 16)
            for at_, n, v in ((0, 48, b_ada[0]), (48, 8, norm_mix[0]), (56, 8, norm_ffn[0]),
                              (72, 1, hgrn_norm[0])):
                sp.dma_start(vecs[at_:at_ + n, :], v.rearrange("(a b) -> a b", b=P)).then_inc(c_in, 16)
            sp.dma_start(vecs[64:72, :], lb_logits.rearrange("l (a b) -> (l a) b", b=P)).then_inc(c_in, 16)
            for c in range(2):
                slot = where[("ada", c)][0]
                sp.dma_start(slot_view(slot, 8, 512), weights(w_ada[0][:, c * 512:(c + 1) * 512])).then_inc(fill[slot], 16)
            for t in range(NT):
                sp.dma_start(xr[0:rows(t), t, :], src_x(t)).then_inc(xin, 16)
            sp.dma_start(reset, consts[:, CONST["reset"][0]:CONST["reset"][0] + T]).then_inc(lvl_in, 16)
            sp.dma_start(arena[:, SC + 7168:SC + 8192], consts[:, CONST["levels"][0]:NCONST]).then_inc(lvl_in, 16)
            sp.dma_start(pages[0:1, :], page_table.rearrange("n j -> (n j)").rearrange("(a b) -> a b", a=1)).then_inc(lvl_in, 16)
            sp.wait_ge(lvl_in, 48)
            for what, slot, f, n in loads[2:]:
                if n:
                    sp.wait_ge(used[slot], n)
                if what[0] == "ada":
                    src = weights(w_ada[0][:, what[1] * 512:(what[1] + 1) * 512])
                    sp.dma_start(slot_view(slot, 8, 512), src).then_inc(fill[slot], 16)
                elif what[0] == "in":
                    src = weights(w_in[0][:, what[1] * 512:(what[1] + 1) * 512])
                    sp.dma_start(slot_view(slot, 8, 512), src).then_inc(fill[slot], 16)
                elif what[0] in ("pa", "pb"):
                    src = weights((w_proj_a if what[0] == "pa" else w_proj_b)[0])
                    sp.dma_start(slot_view(slot, 4, D), src).then_inc(fill[slot], 16)
                elif what[0] == "out":
                    src = weights(w_out[0][:, what[1] * 512:(what[1] + 1) * 512])
                    sp.dma_start(slot_view(slot, 8, 512), src).then_inc(fill[slot], 16)
                else:
                    load_pages(sp, what, (0,) if what in shared else (0, 1))
            def job_weights(j, e, par):
                for c, w in enumerate((w_gate, w_up, w_down)):
                    s_ = 3 * par + c
                    yield s_, w[0, bass.ds(e, 1)].rearrange("o (k p) n -> p (o k) n", p=P)

            for s_ in range(4):
                sp.wait_ge(used[s_], used0[s_])
            sp.wait_ge(bc_r, 4)
            sp.wait_ge(x2_r, NT)
            sp.wait_ge(ssq_r, 2 * NT)

            def pair(i, e0, e1, first=False):
                for par, e in ((0, e0), (1, e1)):
                    for s_, src in job_weights(None, e, par):
                        if not first:
                            sp.wait_ge(used[s_], used0[s_] + i)
                        sp.dma_start(slot_view(s_, 8 if s_ % 3 < 2 else 4, 512 if s_ % 3 < 2 else D), src)\
                            .then_inc(fill[s_], 16)
            pair(0, 0, 1, first=True)
            with sp.Fori(1, NE // 2) as i:
                pair(i, 2 * i, 2 * i + 1)
            sp.wait_ge(tb_r, 2)
            njobs = sp.value_load(ctl[0:1, 8:9], min_val=0, max_val=EXTRA)
            with sp.Fori(0, EXTRA // 2) as i:
                with sp.If(njobs > 2 * i):
                    e0 = sp.value_load(ctl[0:1, bass.ds(2 * i, 1)], min_val=0, max_val=NE - 1)
                    e1 = sp.value_load(ctl[0:1, bass.ds(2 * i + 1, 1)], min_val=0, max_val=NE - 1)
                    pair(i + NE // 2, e0, e1)

            npairs = sp.snap((njobs + 1) >> 1)
            for par in range(2):
                sp.wait_ge(sc2[par], (npairs + NE // 2) * 16)
            y_tok = y_rows.rearrange("(t k) d -> t (k d)", k=2)
            for t in range(NT):
                sp.dma_start(ybuf[t][0:rows(t), :], y_tok[t * P:t * P + rows(t), :]).then_inc(yin[t], 16)
            sp.dma_start(fgain, norm_final.unsqueeze(0).to_broadcast([P, D])).then_inc(c_in, 16)

        @block.gpsimd
        def _(g):
            g.wait_ge(h_r, KD)
            g.wait_ge(h_a, KD)
            g.dma_start(gainv, hgrn_norm.to_broadcast([P, P])).then_inc(attn_in, 16)
            cos = C["cos"].rearrange("p (t f) -> p t f", f=8)
            sin = C["sin"].rearrange("p (t f) -> p t f", f=8)

            def rotate(x, t):
                r, gtt = rows(t), g.tensor_tensor
                x3 = x[0:r, t, :].rearrange("p (h c) -> p h c", c=DH)
                x1, x2 = x3[:, :, 0:8], x3[:, :, 8:16]
                cb = cos[0:r, t, :].unsqueeze(1).to_broadcast([r, BH, 8])
                sb_ = sin[0:r, t, :].unsqueeze(1).to_broadcast([r, BH, 8])
                q4 = [part(arena, SC + a, 64)[0:r].rearrange("p (h c) -> p h c", c=8) for a in (6336, 6976, 7040, 7104)]
                gtt(q4[0], x1, cb, ALU.mult)
                gtt(q4[1], x2, sb_, ALU.mult)
                gtt(q4[2], x1, sb_, ALU.mult)
                gtt(q4[3], x2, cb, ALU.mult)
                g.drain()
                gtt(x1, q4[0], q4[1], ALU.subtract)
                gtt(x2, q4[2], q4[3], ALU.add)
                g.drain()

            g.wait_ge(f_r, 1)
            for v in range(AH * NL):
                h, n = v // NL, LEVELS[v % NL]
                cols = T if n <= 4 else SEQ
                g.wait_ge(e_r, v + 1)
                if v >= 2:
                    g.wait_ge(at_mm, unit_of(v - 2) + 1)
                g.tensor_tensor(kdec[v % 2][:, 0:cols], af[:, h, 0:cols], diff[v % 2][:, 0:cols], ALU.mult)\
                    .then_inc(kd_r, 1)
                x = v - (AH * NL - 2 * NT)
                if x >= 0:
                    g.wait_ge(in_ev, 16 + 2 * NT)
                    rotate((bq, bk)[x // NT], x % NT)
            g.drain().then_inc(rope_r, 2)
            g.wait_ge(in_ev, 16 + 4 * NT)
            g.wait_ge(attn_in, 16)
            for r, t0, t1 in ((P, 0, PT_), (NSMP, PT_, NT)):
                o = ag[0:r, t0:t1, :].rearrange("p t (h c) -> p (t h) c", c=P)
                g.tensor_tensor(o, o, gainv[0:r, :].unsqueeze(1).to_broadcast([r, (t1 - t0) * AH, P]), ALU.mult)
            g.drain().then_inc(rope_r, 1)
            g.wait_ge(qk_r, AH)
            for h in range(AH + 1):
                if h < 2:
                    g.dma_start(st0[h], state_hgrn[0, :, h].rearrange("n k v -> k n v")).then_inc(s0_in2[h], 16)
                if h:
                    g.wait_ge(sn_r, h)
                    g.dma_start(s_sample[0, :, h - 1].rearrange("n k v -> k n v"), st1[(h - 1) % 2])\
                        .then_inc(sn_out2[(h - 1) % 2], 16)
                    if h + 1 < AH:
                        g.wait_ge(so_mm, h)
                        g.dma_start(st0[(h + 1) % 2], state_hgrn[0, :, h + 1].rearrange("n k v -> k n v"))\
                            .then_inc(s0_in2[(h + 1) % 2], 16)
            g.wait_ge(s_up, PT_)
            g.dma_start(s_prompt[0, 0].rearrange("h k v -> k h v"), stP).then_inc(kv_out, 16)
            g.wait_ge(oa_r, 1)
            g.memset(qT[64:128, :, 0:SEQ], 0.0).then_inc(zeroed, 1)
            g.drain()
            g.memset(qT_odd[0:64], 0.0).then_inc(zeroed, 1)
            g.drain()
            g.dma_start(arena[:, AG + 4608:AG + 4608 + ATTN[1] - ATTN[0]], consts[:, ATTN[0]:ATTN[1]]).then_inc(attn_in, 16)
            g.memset(arena[:, XR:XR + 1024], 0.0).then_inc(zeroed, 1)
            g.wait_ge(ob_r, PT_)
            for par in range(2):
                g.wait_ge(sn_out2[par], 32)
            for x in accS:
                g.memset(x, 0.0).then_inc(zeroed, 1)
            g.wait_ge(in_ev, 41)
            g.wait_ge(rope_r, 2)
            for t in range(PT_):
                for dst, x in ((k_prompt, bk), (v_prompt, bv)):
                    g.dma_start(dst[0, 0, :, t * P:(t + 1) * P, :].rearrange("h t d -> t h d"),
                                x[:, t, :].rearrange("p (h d) -> p h d", d=DH)).then_inc(kv_out, 16)
            for n in range(NSEQ):
                for dst, x in ((k_sample, bk), (v_sample, bv)):
                    g.dma_start(dst[0, n].rearrange("h t d -> t h d"),
                                x[8 * n:8 * n + 8, PT_, :].rearrange("p (h d) -> p h d", d=DH)).then_inc(kv_out, 16)
            g.wait_ge(ot_r, 4)
            for t in range(NT):
                g.dma_start(res[0:rows(t), t, :], src_x(t)).then_inc(xin2, 16)
            g.wait_ge(kv_out, 16 * (2 * (PT_ + NSEQ) + 1))
            g.dma_start(arena[:, ROUTER + 324:BQ + 7680], consts[:, ROUTE[0]:ROUTE[1]]).then_inc(wr_in, 16)
            g.dma_start(wr3[:, :, 0:NG], weights(w_group[0])).then_inc(wr_in, 16)
            for gr in range(NG):
                g.dma_start(wr3[:, :, NG + gr * EPG:NG + (gr + 1) * EPG], weights(w_er[0, gr])).then_inc(wr_in, 16)
            g.dma_start(brow[0:1, 0:NG], b_group).then_inc(wr_in, 16)
            g.dma_start(brow[0:1, NG:36], b_er.rearrange("a g e -> a (g e)")).then_inc(wr_in, 16)

            g.wait_ge(pr_mm, KD)
            g.memset(arena[:, QF:QF + 2048], 0.0).then_inc(g_cl, 1)
            g.wait_ge(g_cl, 1)
            for t in range(NT):
                g.wait_ge(h2b_r, 2 * t + 2)
                g.dma_start(h2_rows[t * P:t * P + rows(t), :], xr[0:rows(t), t, :]).then_inc(h2_out, 16)
            g.wait_ge(tb_r, 2)
            g.wait_ge(h2_out, 16 * NT)

            def gather(j, i, par, first=False):
                if not first:
                    g.wait_ge(xt2, 2 * i + par - 1)
                g.tensor_copy(cur[:, par:par + 1], jobs_i[:, bass.ds(j, 1)])
                g.drain()
                g.indirect_dma_start(out=xg[par], out_offset=None, in_=h2_rows,
                                     in_offset=bass.IndirectOffsetOnAxis(ap=cur[:, par:par + 1], axis=0),
                                     bounds_check=T - 1, oob_is_err=False).then_inc(g_in2[par], 16)

            def scatter(j, par):
                g.wait_ge(yA, j + 2)
                g.wait_ge(yD, j + 2)
                g.tensor_copy(cur[:, 2 + par:3 + par], jobs_i[:, bass.ds(j + NJ + 2, 1)])
                g.drain()
                g.indirect_dma_start(out=y_rows, in_=yj[par], in_offset=None,
                                     out_offset=bass.IndirectOffsetOnAxis(ap=cur[:, 2 + par:3 + par], axis=0),
                                     bounds_check=2 * T - 1, oob_is_err=False).then_inc(sc2[par], 16)

            def pool_pair(i):
                for par in range(2):
                    gather(2 * i + 2 + par, i + 1, par)
                    scatter(2 * i + par, par)

            gather(0, 0, 0, first=True)
            gather(1, 0, 1, first=True)
            with g.Fori(0, NE // 2) as i:
                pool_pair(i)
            njobs = g.value_load(ctl[0:1, 8:9], min_val=0, max_val=EXTRA)
            with g.Fori(0, EXTRA // 2) as i:
                with g.If(njobs > 2 * i):
                    pool_pair(i + NE // 2)
            npairs = g.snap((njobs + 1) >> 1)
            for par in range(2):
                g.wait_ge(g_in2[par], (npairs + NE // 2 + 1) * 16)
                g.sem_inc(g_cl, 1)
            for t in range(NT):
                g.wait_ge(fin_v, t + 1)
                dst = y_prompt[0, t * P:(t + 1) * P, :] if t < PT_ else y_sample.rearrange("n t d -> (n t) d")
                g.dma_start(dst, ybuf[t][0:rows(t), 0:D]).then_inc(rows_out, 16)
            g.wait_ge(rows_out, 16 * NT)
            g.wait_ge(kv_out, 16 * (2 * (PT_ + NSEQ) + 1))
            for par in range(2):
                g.wait_ge(sn_out2[par], 32)

        @block.scalar
        def _(act):
            act.wait_ge(c_in, 16 * 8)
            act.activation(crow[0:NCOND, :], crow[0:NCOND, :], ACT.Silu).then_inc(silu_c, 1)
            act.wait_ge(cT_r, 1)
            act.activation(lb[:, 0:4], lb[:, 0:4], ACT.Sigmoid).then_inc(lb_r, 1)

            def square(x, t):
                act.activation(part(arena, SC, D)[0:rows(t), :], x[0:rows(t), t, :], ACT.Square,
                               accum_out=ssq[0:rows(t), t:t + 1]).then_inc(ssq_r, 1)
                act.drain()

            def modulate_prompt(A, shift, n):
                A3 = A[:, :].rearrange("p (k n) -> p k n", n=NCOND)
                for k in range(KD):
                    act.wait_ge(xt_r, n * KD + k + 1)
                    act.activation(hT[:, k, 0:SEQ], ps[2 + k % 2][:, :], ACT.Identity, scale=A3[:, k, 0:1],
                                   bias=m3[:, shift + k, 0:1]).then_inc(h_a, 1)

            act.wait_ge(xin, 16 * NT)
            act.wait_ge(lvl_in, 48)
            act.wait_ge(nrm, 1)
            for t in range(NT):
                square(xr, t)
            act.wait_ge(nrm, 2)
            act.activation(rstd[:, 0:NT], ssq[:, 0:NT], ACT.Sqrt).then_inc(std_r, 1)
            act.wait_ge(mod_r, 1)
            modulate_prompt(A1, 0, 0)
            def take_projected(u):
                c, dst = in_units[u]
                act.wait_ge(in_mm, u + 1)
                rr, cc = dst.shape[0], dst.shape[1]
                fn = {0: ACT.Silu, 1: ACT.Sigmoid, 3: ACT.Silu}.get(c, ACT.Copy)
                act.activation(dst, ps[in_bank[u]][0:rr, 0:cc], fn).then_inc(in_ev, 1)

            def decay(w):
                if w < PRODUCTS and w % (NL + 1):
                    v = w // (NL + 1) * NL + w % (NL + 1) - 1
                    cols = T if LEVELS[v % NL] <= 4 else SEQ
                    act.wait_ge(d_r, v + 1)
                    d = diff[v % 2][:, 0:cols]
                    act.activation(d, d, ACT.Abs)
                    act.drain()
                    act.activation(d, d, ACT.Exp, scale=-1.0).then_inc(e_r, 1)

            for u in range(17):
                take_projected(u)
            act.wait_ge(f_r, 1)
            act.activation(logf, logf, ACT.Ln).then_inc(lnf_r, 1)
            for u in range(17, EARLY):
                take_projected(u)
            decay(0)
            decay(1)
            for w in range(PRODUCTS):
                decay(w + 2)
                for u in in_after[w]:
                    take_projected(u)
                h = w // (NL + 1)
                if w % (NL + 1) == 0:
                    act.activation(logf[:, h, :], bsum[:, h, :], ACT.Exp).then_inc(eb_r, 1)
                if h and w % (NL + 1) == 3 or w == PRODUCTS - 1:
                    last_of = AH - 1 if w == PRODUCTS - 1 else h - 1
                    act.wait_ge(dl_r, last_of + 1)
                    act.activation(bsum[:, last_of, :], bsum[:, last_of, :], ACT.Exp).then_inc(el_r, 1)
            for h in range(AH):
                act.wait_ge(kt_mm, h + 1)
                act.activation(kdT[:, h, 0:PT_, :], ps[4 + h % 2][:, :].rearrange("p (t k) -> p t k", k=P), ACT.Copy)
                act.activation(kdT[0:NSMP, h, PT_, :], ps[6 + h % 2][0:NSMP, 0:P], ACT.Copy).then_inc(kt_ev, 1)
            def head_squares(r, t, heads):
                for h in heads:
                    act.activation(kdT[0:r, h, t % PT_, :], oa[0:r, t, h * P:(h + 1) * P], ACT.Square,
                                   accum_out=hss[0:r, t * AH + h:t * AH + h + 1])
                    act.drain()

            for c in range(PT_):
                act.wait_ge(o_mm, c + 1)
                act.activation(oa[:, c, :], ps[c % 2][:, :], ACT.Copy).then_inc(o_ev, 1)
                act.drain()
                head_squares(P, c, range(AH))
            for h in range(AH):
                act.wait_ge(so_mm, h + 1)
                act.activation(soS[h % 2], ps[4 + h % 2][:, 0:NSMP], ACT.Copy).then_inc(so_ev, 1)
                act.wait_ge(so2_mm, h + 1)
                act.activation(oa[0:NSMP, PT_, h * P:(h + 1) * P], ps[6 + h % 2][0:NSMP, 0:P], ACT.Copy).then_inc(so_t, 1)
                act.drain()
                head_squares(NSMP, PT_, (h,))
            act.drain().then_inc(hs_r, 1)
            act.wait_ge(hq_r, 1)
            act.activation(hss[:, :], hss[:, :], ACT.Sqrt).then_inc(hq_r, 1)
            for t in range(NT):
                act.wait_ge(oat_mm, t + 1)
                r = rows(t)
                act.activation(oaT[:, :, t * P:t * P + r], ps[t % 2][:, 0:4 * r].rearrange("p (k t) -> p k t", t=r),
                               ACT.Copy).then_inc(oat_r, 1)
            for u in range(2 * NT):
                x, t = (qT, kT)[u // NT], u % NT
                r = rows(t)
                act.wait_ge(qkt_mm, u + 1)
                cols = slice(t * P, t * P + r)
                src = ps[2 + u % 2][:, 0:4 * r].rearrange("p (k t) -> p k t", t=r)
                if u < PT_:
                    act.activation(qT[0:64, :, cols], src[0:64], ACT.Copy)
                    act.activation(qT_odd[64:128, :, cols], src[64:128], ACT.Copy).then_inc(qkt_r, 1)
                else:
                    act.activation(x[:, :, cols], src, ACT.Copy).then_inc(qkt_r, 1)
            for u in range(PT_ * BH):
                i = u // BH
                act.wait_ge(mx_r, u + 1)
                if u >= 2:
                    act.wait_ge(pt_mm, u - 1)
                act.activation(prob[u % 2][:, 0:(i + 1) * P], ps[u % 2][:, 0:(i + 1) * P], ACT.Exp,
                               bias=mx[:, u:u + 1], scale=0.125, accum_out=sm[:, u:u + 1])
                act.drain().then_inc(ex_r, 1)
            for t in range(PT_):
                act.wait_ge(obt_mm, t + 1)
                act.activation(obT[:, :, t * P:(t + 1) * P], ps[4 + t % 2][:, :].rearrange("p (k t) -> p k t", t=P),
                               ACT.Copy).then_inc(obt_r, 1)
            def take_scores(p, b):
                act.wait_ge(ss_mm, p * NBLK + b + 1)
                act.activation(S[p % 2][:, b, :], ps[6 + b % 2][:, 0:256], ACT.Copy).then_inc(ss_ev, 1)

            def exps(p, b0, b1):
                if b0 == 0:
                    act.wait_ge(sb_r, p + 1)
                for b in range(b0, b1):
                    act.activation(S[p % 2][:, b, :], S[p % 2][:, b, :], ACT.Exp, bias=sbias[:, b:b + 1], scale=0.125,
                                   accum_out=ssum[:, b:b + 1])
                    act.drain()
                if b1 == NBLK:
                    act.activation(snew[p % 2], snew[p % 2], ACT.Exp, bias=sbias[:, 8:9], scale=0.125,
                                   accum_out=ssum[:, 8:9])
                    act.drain().then_inc(sp_r, 1)

            for kind, p in SAMPLE_PHASES:
                if kind == "k":
                    for b in range(NBLK):
                        for n in range(2):
                            w = (p * NBLK + b) * 2 + n
                            act.wait_ge(key_mm, w + 1)
                            if w >= 2:
                                act.wait_ge(qks, w - 1)
                            act.activation(keyT[w % 2][:, 0:4, :],
                                           ps[2 * (w % 2)][:, :].rearrange("p (h k) -> p h k", k=P), ACT.Copy).then_inc(keyA, 1)
                        if b:
                            take_scores(p, b - 1)
                        q = p * NBLK + b
                        act.wait_ge(qks, 2 * q + 2)
                        if q >= 2:
                            act.wait_ge(ss_mm, q - 1)
                        act.activation(stS[b % 2], ps[4 + b % 2][:, 0:256], ACT.Copy).then_inc(sq_ev, 1)
                        if p and b >= 4:
                            exps(p - 1, 2 * b - 8, 2 * b - 6)
                    take_scores(p, NBLK - 1)
                    act.wait_ge(nw_mm, p + 1)
                    for r in range(2):
                        x4, y4 = (x[0:64, 0:128].rearrange("p (m r c) -> p m r c", r=2, c=TS)[:, :, r, :]
                                  for x in (newT, ps[4 + r]))
                        ins = act.activation(x4, y4, ACT.Copy)
                    ins.then_inc(nw_ev, 1)
                else:
                    for q in range(4):
                        act.wait_ge(sT_mm, 4 * p + q + 1)
                        for r in range(2):
                            ins = act.activation(
                                probsT[:, 2 * q:2 * q + 2, :, r, :],
                                ps[q][:, :].rearrange("p (a r e t) -> p a r e t", a=2, r=2, t=TS)[:, :, r], ACT.Copy)
                        ins.then_inc(sT_r, 1)
                    act.wait_ge(nT_mm, p + 1)
                    act.activation(pnewT[0:64, :], ps[4][0:64, 256:384], ACT.Copy).then_inc(nT_r, 1)
                    if p == 2:
                        exps(3, 0, NBLK)
                    for m in [m for m, (what, *_) in enumerate(loads) if what[:2] == ("v", p)]:
                        what, slot, _f, n = loads[m + 4]
                        if what in shared:
                            act.wait_ge(used[slot], n)
                            load_pages(act, what, (1,))
            for m in range(KD):
                act.wait_ge(g_mm, m + 1)
                if m >= 2:
                    act.wait_ge(mg_r, m - 1)
                for k in range(2):
                    for cols, bank in zip(HALVES, (ps[k], ps[4 + k])):
                        ins = act.activation(sig[2 * (m % 2) + k][:, cols], bank[:, 0:T // 2], ACT.Sigmoid)
                ins.then_inc(g_r, 1)

            def gate_rows(dst, mm, done):
                for q in range(4):
                    act.wait_ge(mm, q + 1)
                    k, r = q % 2, (P, NSMP)[q // 2]
                    act.activation(dst[q // 2][0:r, 512 * k:512 * k + 512], ps[q][0:r, :], ACT.Copy).then_inc(done, 1)

            gate_rows(gate1, bc_mm, bc_r)
            for t in range(NT):
                act.wait_ge(x2_r, t + 1)
                square(res, t)
                r = rows(t)
                act.activation(rstd[0:r, t:t + 1], ssq[0:r, t:t + 1], ACT.Sqrt, scale=1.0 / D, bias=epsv[0:r])\
                    .then_inc(std_r, 1)
            modulate_prompt(A2, 24, 1)
            for t in range(NT):
                for k in range(2):
                    act.wait_ge(h2b_mm, 2 * t + k + 1)
                    act.activation(xr[0:rows(t), t, 512 * k:512 * k + 512], ps[2 + k][0:rows(t), :],
                                   ACT.Copy).then_inc(h2b_r, 1)
            act.wait_ge(rt_a, 1)
            act.activation(rexp, rexp, ACT.Exp).then_inc(rt_b, 1)
            gate_rows(gate2, g2_mm, g2_r)

            def act_rows(i, par):
                act.wait_ge(xt2, 2 * i + par + 1)
                act.activation(xgT[par][:, 0:4, :], ps[0][:, :].rearrange("p (k s) -> p k s", s=CAP), ACT.Copy).then_inc(xtA, 1)

            def act_job(i, par, first=False):
                act.wait_ge(used[3 * par], i + (used0[3 * par] + 1))
                act.activation(hs, ps[2][:, :].rearrange("p (k s) -> p k s", s=CAP), ACT.Silu).then_inc(sl, 1)
                act_rows(i + par, 1 - par)
                act.wait_ge(used[3 * par + 2], i + (used0[3 * par + 2] + 1))
                if not first:
                    act.wait_ge(sc2[par], i * 16)
                act.activation(yj[par][:, 0:512], ps[4][:, :], ACT.Copy).then_inc(yA, 1)

            act_rows(0, 0)
            act_job(0, 0, first=True)
            act_job(0, 1, first=True)
            with act.Fori(1, NE // 2) as i:
                act_job(i, 0)
                act_job(i, 1)
            njobs = act.value_load(ctl[0:1, 8:9], min_val=0, max_val=EXTRA)
            with act.Fori(0, EXTRA // 2) as i:
                with act.If(njobs > 2 * i):
                    act_job(i + NE // 2, 0)
                    act_job(i + NE // 2, 1)
            def weigh(t):
                act.wait_ge(yin[t], 16)
                y1 = ybuf[t][0:rows(t), D:2 * D]
                act.activation(y1, y1, ACT.Copy, scale=wts[0:rows(t), NT + t:NT + t + 1]).then_inc(fin_w, 1)

            weigh(0)
            weigh(1)
            for t in range(NT):
                act.wait_ge(fin_a, t + 1)
                act.activation(fsq[0:rows(t), :], ybuf[t][0:rows(t), 0:D], ACT.Square,
                               accum_out=fss[0:rows(t), t:t + 1])
                act.drain()
                act.activation(fss[0:rows(t), t:t + 1], fss[0:rows(t), t:t + 1], ACT.Sqrt, scale=1.0 / D,
                               bias=epsv[0:rows(t)]).then_inc(fin_s, 1)
                if t + 2 < NT:
                    weigh(t + 2)

        @block.tensor
        def _(pe):
            MM, TR = pe.matmul, pe.transpose
            pe.wait_ge(c_in, 16 * 8)
            TR(ps[2][:, 0:73], vecs[0:73, :], ident[0:73, 0:73]).then_inc(cvec_t, 1)
            pe.wait_ge(silu_c, 1)
            for k in range(KD):
                ins = TR(ps[1][:, k * NCOND:(k + 1) * NCOND], crow[0:NCOND, k * P:(k + 1) * P], ident[0:NCOND, 0:NCOND])
            ins.then_inc(cT_t, 1)
            pe.wait_ge(cT_r, 1)

            def turn_mod(n):
                pe.wait_ge(ada_cp, n + 1)
                for m in range(4):
                    ins = TR(ps[0][:, (4 * n + m) * NCOND:(4 * n + m + 1) * NCOND], arow[n % 2][0:NCOND, m * P:(m + 1) * P],
                             ident[0:NCOND, 0:NCOND])
                ins.then_inc(ada_t, 1)

            for n in range(12):
                slot, f, u = where[("ada", n)]
                pe.wait_ge(fill[slot], f)
                w = slot_view(slot, 8, 512)
                if n >= 2:
                    pe.wait_ge(ada_cp, n - 1)
                for k in range(KD):
                    ins = MM(ps[6 + n % 2][0:NCOND, :], cT[:, k * NCOND:(k + 1) * NCOND], w[:, k, :],
                             start=(k == 0), stop=(k == KD - 1))
                ins.then_inc(used[slot], 1)
                if n:
                    turn_mod(n - 1)
            turn_mod(11)

            def turn_rows(x, n):
                pe.wait_ge(xn_r, NT * n + NT)
                for k in range(KD):
                    if n * KD + k >= 2:
                        pe.wait_ge(h_r, n * KD + k - 1)
                        pe.wait_ge(h_a, n * KD + k - 1)
                    for t in range(PT_):
                        TR(ps[2 + k % 2][:, t * P:(t + 1) * P], x[:, t, k * P:(k + 1) * P], ident)
                    TR(ps[4 + k % 2][:, 0:NSMP], x[0:NSMP, PT_, k * P:(k + 1) * P], ident[0:NSMP, 0:NSMP]).then_inc(xt_r, 1)

            turn_rows(xr, 0)
            pe.wait_ge(h_r, KD)
            pe.wait_ge(h_a, KD)
            def project(u):
                c = in_units[u][0]
                v = u % 8 if c < 2 else (u - 16) % NT
                slot, f, n = where[("in", c)]
                w = slot_view(slot, 8, 512)
                if v == 0:
                    pe.wait_ge(fill[slot], f)
                if u >= 4:
                    pe.wait_ge(in_ev, u - 3)
                for k in range(KD):
                    if c < 2:
                        m, cols = v // 2, HALVES[v % 2]
                        ins = MM(ps[in_bank[u]][:, 0:T // 2], w[:, k, m * P:(m + 1) * P], hT[:, k, cols],
                                 start=(k == 0), stop=(k == KD - 1))
                    else:
                        ins = MM(ps[in_bank[u]][0:rows(v), :], hT[:, k, v * P:v * P + rows(v)], w[:, k, :],
                                 start=(k == 0), stop=(k == KD - 1))
                ins.then_inc(in_mm, 1)
                if v == (7 if c < 2 else NT - 1):
                    pe.wait_ge(in_mm, u + 1)
                    pe.sem_inc(used[slot], 1)

            for u in range(EARLY):
                project(u)
            pe.wait_ge(in_ev, 16)
            for w_ in range(PRODUCTS):
                h, l = w_ // (NL + 1), w_ % (NL + 1)
                v = h * NL + l - 1
                if w_ >= 2:
                    pe.wait_ge(at_ac, w_ - 1)
                if l:
                    pe.wait_ge(qd_r, v + 1)
                    pe.wait_ge(kd_r, v + 1)
                    q_, k_ = qdec[v % 2], kdec[v % 2]
                else:
                    pe.wait_ge(f_r, 1)
                    q_, k_ = aq[:, h, :], af[:, h, :]
                for t in range(PT_):
                    ins = MM(ps[w_ % 2][:, t * P:(t + 1) * P], k_[:, t * P:(t + 1) * P], q_[:, t * P:(t + 1) * P],
                             start=True, stop=True)
                if l == 0 or LEVELS[l - 1] <= 4:
                    ins = MM(ps[2 + w_ % 2][0:NSMP, 0:NSMP], k_[:, SEQ:T], q_[:, SEQ:T], start=True, stop=True)
                ins.then_inc(at_mm, 1)
                for u in in_after[w_]:
                    project(u)
            pe.wait_ge(in_ev, len(in_units))
            for h in range(AH):
                pe.wait_ge(qk_r, h + 1)
                if h >= 2:
                    pe.wait_ge(kt_ev, h - 1)
                for t in range(PT_):
                    TR(ps[4 + h % 2][:, t * P:(t + 1) * P], af[:, h, t * P:(t + 1) * P], ident)
                TR(ps[6 + h % 2][0:NSMP, 0:P], af[:, h, SEQ:T], ident).then_inc(kt_mm, 1)
            pe.wait_ge(kt_ev, AH)
            pe.wait_ge(at_ac, AH * (NL + 1))
            for c in range(PT_):
                if c >= 2:
                    pe.wait_ge(s_up, c - 1)
                for h in range(AH):
                    ins = MM(ps[2 + c % 2][:, h * P:(h + 1) * P], kdT[:, h, c, :], ai[:, c, h * P:(h + 1) * P],
                             start=True, stop=True)
                ins.then_inc(s_mm, 1)
                if c:
                    pe.wait_ge(s_up, c)
                if c >= 2:
                    pe.wait_ge(o_ev, c - 1)
                for h in range(AH):
                    o = ps[c % 2][:, h * P:(h + 1) * P]
                    ins = MM(o, attnT[:, h, c * P:(c + 1) * P], ai[:, c, h * P:(h + 1) * P], start=True, stop=(c == 0))
                    if c:
                        ins = MM(o, aq[:, h, c * P:(c + 1) * P], stP[:, h, :], start=False, stop=True)
                ins.then_inc(o_mm, 1)
            pe.wait_ge(s_up, PT_)
            for h in range(AH):
                pe.wait_ge(s0_in2[h % 2], 16 * (h // 2 + 1))
                if h >= 2:
                    pe.wait_ge(so_ev, h - 1)
                o = ps[4 + h % 2]
                MM(o[:, 0:NSMP], ai[0:NSMP, PT_, h * P:(h + 1) * P], attnT[0:NSMP, h, SEQ:T], start=True, stop=False,
                   skip_group_check=True)
                for n in range(NSEQ):
                    ins = MM(o[:, n * TS:(n + 1) * TS], st0[h % 2][:, n, :], aq[:, h, SEQ + n * TS:SEQ + (n + 1) * TS],
                             start=False, stop=(n == NSEQ - 1), skip_group_check=True)
                ins.then_inc(so_mm, 1)
                pe.wait_ge(so_ev, h + 1)
                if h >= 2:
                    pe.wait_ge(so_t, h - 1)
                TR(ps[6 + h % 2][0:NSMP, 0:P], soS[h % 2], ident).then_inc(so2_mm, 1)
                pe.wait_ge(vb_r, h + 1)
                if h:
                    pe.wait_ge(sn_r, h)
                for k in range(2):
                    ins = MM(ps[2 + k][:, :], kdT[0:NSMP, h, PT_, :], vbd[0:NSMP, 4 * k:4 * k + 4, :].rearrange("p n v -> p (n v)"),
                             start=True, stop=True)
                ins.then_inc(sn_mm, 1)
            pe.wait_ge(oa_r, 1)
            for t in range(NT):
                if t >= 2:
                    pe.wait_ge(oat_r, t - 1)
                r = rows(t)
                for k in range(4):
                    ins = TR(ps[t % 2][:, k * r:(k + 1) * r], oa[0:r, t, k * P:(k + 1) * P], ident[0:r, 0:r])
                ins.then_inc(oat_mm, 1)
            pe.wait_ge(rope_r, 2)
            for u in range(2 * NT):
                x, t = (bq, bk)[u // NT], u % NT
                r = rows(t)
                if u >= 2:
                    pe.wait_ge(qkt_r, u - 1)
                for k in range(4):
                    ins = TR(ps[2 + u % 2][:, k * r:(k + 1) * r], x[0:r, t, k * P:(k + 1) * P], ident[0:r, 0:r])
                ins.then_inc(qkt_mm, 1)
            pe.wait_ge(qkt_r, 2 * NT)
            pe.wait_ge(oat_r, NT)
            pe.wait_ge(zeroed, 2)
            NU = PT_ * BH
            for s_ in range(NU + 2):
                if s_ < NU:
                    i, h = s_ // BH, s_ % BH
                    if s_ >= 2:
                        pe.wait_ge(ex_r, s_ - 1)
                    MM(ps[s_ % 2][:, 0:(i + 1) * P], (qT, qT_odd)[h % 2][:, h // 2, i * P:(i + 1) * P],
                       kT[:, h // 2, 0:(i + 1) * P], start=True, stop=True).then_inc(sc_mm, 1)
                if 1 <= s_ <= NU:
                    u = s_ - 1
                    pe.wait_ge(ex_r, u + 1)
                    if u >= 2:
                        pe.wait_ge(pt_r, u - 1)
                    for k in range(u // BH + 1):
                        ins = TR(ps[2 + u % 2][:, k * P:(k + 1) * P], prob[u % 2][:, k * P:(k + 1) * P], ident)
                    ins.then_inc(pt_mm, 1)
                if s_ >= 2:
                    u = s_ - 2
                    i, h = u // BH, u % BH
                    pe.wait_ge(pt_r, u + 1)
                    if h == 0 and i >= 2:
                        pe.wait_ge(ob_r, i - 1)
                    for k in range(i + 1):
                        ins = MM(ps[4 + i % 2][:, h * DH:(h + 1) * DH], probT[u % 2][:, k * P:(k + 1) * P],
                                 bv[:, k, h * DH:(h + 1) * DH], start=(k == 0), stop=(k == i))
                    ins.then_inc(pv_mm, 1)
            pe.wait_ge(ob_r, PT_)
            pe.wait_ge(attn_in, 32)
            for t in range(PT_):
                if t >= 2:
                    pe.wait_ge(obt_r, t - 1)
                for k in range(4):
                    ins = TR(ps[4 + t % 2][:, k * P:(k + 1) * P], ob[:, t, k * P:(k + 1) * P], ident)
                ins.then_inc(obt_mm, 1)
            pe.wait_ge(qdup_r, 1)
            for h in range(BH):
                ins = TR(ps[6][:, h * 64:(h + 1) * 64],
                         qdup[0:NSMP, h, :], ident[0:NSMP, 0:NSMP])
            ins.then_inc(qb_mm, 1)
            pe.wait_ge(qb_r, 1)
            pe.wait_ge(obt_r, PT_)
            def turn_scores(p, b):
                q = p * NBLK + b
                pe.wait_ge(sq_ev, q + 1)
                if q >= 2:
                    pe.wait_ge(ss_ev, q - 1)
                if b == 0 and p >= 2:
                    pe.wait_ge(acc_r, p - 1)
                for r in range(2):
                    ins = TR(ps[6 + b % 2][:, r * P:(r + 1) * P], stS[b % 2][:, r * P:(r + 1) * P], ident)
                ins.then_inc(ss_mm, 1)

            def score(w):
                p, n, b = w // (2 * NBLK), w % 2, w // 2 % NBLK
                pe.wait_ge(keyA, w + 1)
                pe.wait_ge(keyD, w + 1)
                if b >= 2 or p:
                    pe.wait_ge(sq_ev, p * NBLK + b - 1)
                if b == 1 and p:
                    pe.wait_ge(sn_t, p)
                st = ps[4 + b % 2][:, 0:256].rearrange("p (r n h t) -> p n h r t", r=2, n=2, h=BH)[:, n]
                for h in range(BH):
                    ins = MM(st[:, h:BH], keyT[w % 2][:, h, :],
                             qbd[:, 2 * p + n, h:BH, :].rearrange("p h (r t) -> p h r t", r=2), start=True, stop=True)
                ins.then_inc(qks, 1)

            def key_phase(p):
                for b in range(NBLK):
                    for n in range(2):
                        w = (p * NBLK + b) * 2 + n
                        slot, f, _u = where[("k", p, b // 2)]
                        pe.wait_ge(fill[slot], f)
                        if w >= 2:
                            pe.wait_ge(keyA, w - 1)
                            pe.wait_ge(keyD, w - 1)
                        blk_ = ring[slot].rearrange("p (b h c) -> p b h c", b=4, h=BH)
                        for h in range(BH):
                            ins = TR(ps[2 * (w % 2) + h // 4][:, (h % 4) * P:(h % 4 + 1) * P], blk_[:, 2 * n + b % 2, h, :], ident)
                        ins.then_inc(key_mm, 1)
                        if b % 2 and n:
                            pe.wait_ge(key_mm, w + 1)
                            pe.sem_inc(used[slot], 1)
                        if w > p * 2 * NBLK:
                            score(w - 1)
                        if n == 1 and b:
                            turn_scores(p, b - 1)
                score((p * NBLK + NBLK - 1) * 2 + 1)
                turn_scores(p, NBLK - 1)
                pe.wait_ge(sq_ev, (p + 1) * NBLK)
                nw = [ps[4 + r][0:64, 0:128].rearrange("p (n c) -> p n c", n=2) for r in range(2)]
                for h in range(BH):
                    q0 = 64 * (h % 2)
                    ins = MM(nw[h % 2][:, :, h * 8:h * 8 + 8], kT[q0:q0 + 64, h // 2, SEQ:T],
                             qT[q0:q0 + 64, h // 2, SEQ + 16 * p:SEQ + 16 * p + 16], start=True, stop=True)
                ins.then_inc(nw_mm, 1)
                pe.wait_ge(nw_ev, p + 1)
                TR(ps[5][:, 0:64], newT[0:64, :], ident[0:64, 0:64]).then_inc(nt_mm, 1)

            def out_place(n, h):
                e = n * BH + h
                return 32 * (e % 4), P * (e // 4)

            def value_phase(p):
                pe.wait_ge(sp_r, p + 1)
                for q in range(4):
                    for k in range(4):
                        c = 4 * q + k
                        ins = TR(ps[q][:, k * P:(k + 1) * P], S[p % 2][:, c // 2, (c % 2) * P:(c % 2 + 1) * P], ident)
                    ins.then_inc(sT_mm, 1)
                TR(ps[4][0:64, 256:384], snew[p % 2], ident).then_inc(nT_mm, 1)
                pe.wait_ge(ss_ev, min(p + 2, 4) * NBLK)
                if p:
                    pe.wait_ge(acc_r, p)
                for b in range(NBLK):
                    pe.wait_ge(sT_r, 4 * p + b // 2 + 1)
                    for n in range(2):
                        slot, f, _u = where[("v", p, b // 2)]
                        pe.wait_ge(fill[slot], f)
                        vals = ring[slot].rearrange("p (b h c) -> p b h c", b=4, h=BH)
                        for h in range(BH):
                            r0, c0 = out_place(n, h)
                            ins = MM(ps[6][r0:r0 + 16, c0:c0 + P], probsT[:, b, n * BH + h].rearrange("p r t -> p (r t)"),
                                     vals[:, 2 * n + b % 2, h, :], start=(b == 0 and n == 0 and h < 4), stop=False,
                                     skip_group_check=True)
                        if b % 2 and n:
                            ins.then_inc(used[slot], 1)
                pe.wait_ge(nT_r, p + 1)
                for n in range(2):
                    for h in range(BH):
                        r0, c0 = out_place(n, h)
                        ins = MM(ps[6][r0:r0 + 8, c0:c0 + DH], pnewT[0:64, n * 64 + h * 8:n * 64 + h * 8 + 8],
                                 bv[0:NSMP, PT_, h * DH:(h + 1) * DH], start=False, stop=(n == 1 and h == BH - 1),
                                 skip_group_check=True)
                ins.then_inc(spv, 1)

            for kind, p in SAMPLE_PHASES:
                (key_phase if kind == "k" else value_phase)(p)
            for p in range(4):
                pe.wait_ge(acc_r, p + 1)
                for k in range(4):
                    ins = TR(ps[p][:, k * P:(k + 1) * P], accS[p][:, k, :], ident)
                ins.then_inc(acc_t, 1)
            for p in range(4):
                pe.wait_ge(od_r, p + 1)
                MM(ps[4 + p][:, 0:DH], odiag[p], C["fold"], start=True, stop=True).then_inc(of_mm, 1)
            for p in range(4):
                pe.wait_ge(or_r, p + 1)
                TR(ps[p][:, 0:P], orow[p], ident).then_inc(ot_mm, 1)
            pe.wait_ge(ot_r, 4)
            pe.wait_ge(kv_out, 16 * (2 * (PT_ + NSEQ) + 1))
            for m in range(KD):
                if m:
                    pe.wait_ge(g_r, m)
                for k_, c in ((0, 7 + m // 4), (1, 9 + m // 4)):
                    slot, f, _u = where[("in", c)]
                    pe.wait_ge(fill[slot], f)
                    w = slot_view(slot, 8, 512)
                    for cols, bank in zip(HALVES, (ps[k_][:, 0:T // 2], ps[4 + k_][:, 0:T // 2])):
                        for k in range(KD):
                            ins = MM(bank, w[:, k, (m % 4) * P:(m % 4 + 1) * P], hT[:, k, cols], start=(k == 0), stop=(k == KD - 1))
                    if k_:
                        ins.then_inc(g_mm, 1)
                    if m % 4 == 3:
                        if k_:
                            pe.wait_ge(g_mm, m + 1)
                            pe.sem_inc(used[slot], 1)
                        else:
                            ins.then_inc(used[slot], 1)
                if m:
                    pe.wait_ge(mg_r, m)
                for k_, (what, x) in enumerate(((("pa",), oaT), (("pb",), obT))):
                    slot, f, _u = where[what]
                    pe.wait_ge(fill[slot], f)
                    w = slot_view(slot, 4, D)
                    for cols, bank in zip(HALVES, (ps[2 + k_][:, 0:T // 2], ps[6 + k_][:, 0:T // 2])):
                        for k in range(4):
                            ins = MM(bank, w[:, k, m * P:(m + 1) * P], x[:, k, cols], start=(k == 0), stop=(k == 3))
                    if k_:
                        ins.then_inc(pr_mm, 1)
            pe.wait_ge(pr_mm, KD)
            pe.sem_inc(used[where[("pa",)][0]], 1)
            pe.sem_inc(used[where[("pb",)][0]], 1)

            def gate_banks(m0, mm):
                pe.wait_ge(gseq_r, 1 + m0 // 40)
                for q in range(4):
                    for j in range(4):
                        m = m0 + 4 * (q % 2) + j
                        if q < 2:
                            ins = TR(ps[q][:, j * P:(j + 1) * P], m3[:, m, 0:1].to_broadcast([P, P]), ident)
                        else:
                            ins = TR(ps[q][0:NSMP, j * P:(j + 1) * P], gseq[m0 // 40][:, m - m0, :], ident)
                    ins.then_inc(mm, 1)

            pe.wait_ge(g_r, KD)
            pe.wait_ge(mg_r, KD)
            gate_banks(16, bc_mm)
            banks = (4, 5, 6, 7)
            for t in range(NT):
                for k_ in range(2):
                    u = 2 * t + k_
                    slot, f, _u = where[("out", k_)]
                    pe.wait_ge(fill[slot], f)
                    if u >= 4:
                        pe.wait_ge(y_r, u - 3)
                    w = slot_view(slot, 8, 512)
                    r = rows(t)
                    for k in range(KD):
                        ins = MM(ps[banks[u % 4]][0:r, :], merged[:, k, t * P:t * P + r], w[:, k, :], start=(k == 0), stop=(k == KD - 1))
                    ins.then_inc(y_mm, 1)
            pe.wait_ge(y_mm, 2 * NT)
            for k_ in range(2):
                pe.sem_inc(used[where[("out", k_)][0]], 1)
            pe.wait_ge(bc_r, 4)
            turn_rows(xr, 1)
            pe.wait_ge(h_r, 2 * KD)
            pe.wait_ge(h_a, 2 * KD)
            pe.wait_ge(wr_in, 16 * 8)
            for t in range(NT):
                r = rows(t)
                for k in range(KD):
                    MM(ps[0][0:r, t * 36:(t + 1) * 36], hT[:, k, t * P:t * P + r], wr3[:, k, :], start=(k == 0), stop=False)
                ins = MM(ps[0][0:r, t * 36:(t + 1) * 36], onerow[:, 0:r], brow[0:1, :], start=False, stop=True)
            ins.then_inc(lg_mm, 1)
            for t in range(NT):
                r = rows(t)
                for k_ in range(2):
                    if t:
                        pe.wait_ge(h2b_r, 2 * t + k_ - 1)
                    for k in range(4):
                        ins = TR(ps[2 + k_][0:r, k * P:(k + 1) * P], hT[:, 4 * k_ + k, t * P:t * P + r], ident)
                    ins.then_inc(h2b_mm, 1)
            pe.wait_ge(oh_r, 1)
            for t in range(NT):
                out = ps[1][:, t * NE:(t + 1) * NE]
                MM(out, before, msum[:, t, :], start=True, stop=(t == 0))
                for t2 in range(t):
                    MM(out, ones, msum[:, t2, :], start=False, stop=(t2 == t - 1))
            for t in range(NT):
                ins = MM(ps[1][:, NT * NE:(NT + 1) * NE], ones, msum[:, t, :], start=(t == 0), stop=(t == NT - 1))
            ins.then_inc(rk_mm, 1)
            for c in range(2 * NT):
                pe.wait_ge(oh_r, 2 + c)
                ins = MM(ps[4][:, 0:NJ + 2], slot1[c % 2], job1[c % 2], start=(c == 0), stop=(c == 2 * NT - 1))
                ins.then_inc(tb_mm, 1)
            pe.wait_ge(h2b_r, 2 * NT)
            pe.wait_ge(rk_r, 1)
            gate_banks(40, g2_mm)
            pe.wait_ge(g2_r, 4)
            pe.wait_ge(tb_r, 2)

            for free in (xtA, xtD, hd, yA, yD):
                pe.sem_inc(free, 1)

            def turn_job(i, par):
                j = 2 * i + par
                pe.wait_ge(g_in2[par], i * 16 + 16)
                pe.wait_ge(xtA, j + 1)
                pe.wait_ge(xtD, j + 1)
                for k in range(KD):
                    ins = TR(ps[k // 4][:, (k % 4) * P:(k % 4 + 1) * P], xg[par][:, k * P:(k + 1) * P], ident)
                ins.then_inc(xt2, 1)

            def pe_job(i, par):
                j = 2 * i + par
                pe.wait_ge(xtA, j + 2)
                pe.wait_ge(xtD, j + 2)
                pe.wait_ge(hd, j + 1)
                for c in range(2):
                    s_ = 3 * par + c
                    pe.wait_ge(fill[s_], i * 16 + (fill0[s_] + 16))
                    w = slot_view(s_, 8, 512)
                    for f in range(4):
                        for k in range(KD):
                            ins = MM(ps[2 + c][:, f * P:(f + 1) * P], w[:, k, f * P:(f + 1) * P], xgT[par][:, k, :],
                                     start=(k == 0), stop=(k == KD - 1))
                    ins.then_inc(used[s_], 1)
                turn_job(i + par, 1 - par)
                s_ = 3 * par + 2
                pe.wait_ge(fill[s_], i * 16 + (fill0[s_] + 16))
                pe.wait_ge(hd, j + 2)
                pe.wait_ge(yA, j + 1)
                pe.wait_ge(yD, j + 1)
                w = slot_view(s_, 4, D)
                for c in range(2):
                    for f in range(4):
                        ins = MM(ps[4 + c][:, :], hid[:, f, :], w[:, f, 512 * c:512 * c + 512], start=(f == 0), stop=(f == 3))
                ins.then_inc(used[s_], 1)

            turn_job(0, 0)
            with pe.Fori(0, NE // 2) as i:
                pe_job(i, 0)
                pe_job(i, 1)
            njobs = pe.value_load(ctl[0:1, 8:9], min_val=0, max_val=EXTRA)
            with pe.Fori(0, EXTRA // 2) as i:
                with pe.If(njobs > 2 * i):
                    pe_job(i + NE // 2, 0)
                    pe_job(i + NE // 2, 1)

        @block.vector
        def _(v):
            TT, TSC, STT, CP = v.tensor_tensor, v.tensor_scalar, v.scalar_tensor_tensor, v.tensor_copy
            RED = v.tensor_reduce
            v.wait_ge(c_in, 16 * 8)
            v.memset(hss[:, :], 1.0)
            v.memset(ssq[:, :], 1.0).then_inc(nrm, 1)
            v.wait_ge(cvec_t, 1)
            CP(colv[:, 0:73], ps[2][:, 0:73])
            v.drain()
            TT(lb[:, 0:4], colv[:, 64:68], colv[:, 68:72], ALU.subtract)
            v.wait_ge(cT_t, 1)
            CP(cT, ps[1][:, 0:KD * NCOND]).then_inc(cT_r, 1)
            v.wait_ge(lb_r, 1)
            TSC(omlb, lb[:, 0:4], -1.0, 1.0, ALU.mult, ALU.add)

            def norm_rows(x, dst):
                v.wait_ge(ssq_r, NT)
                TSC(ssq[:, 0:NT], ssq[:, 0:NT], 1.0 / D, EPS, ALU.mult, ALU.add).then_inc(nrm, 1)
                v.wait_ge(std_r, 1)
                v.reciprocal(rstd[:, 0:NT], rstd[:, 0:NT]).then_inc(nrm, 1)
                v.drain()
                for t in range(NT):
                    r = rows(t)
                    TSC(dst[0:r, t, :], x[0:r, t, :], rstd[0:r, t:t + 1], None, ALU.mult).then_inc(xn_r, 1)

            def modulate(A, shift, n):
                A3 = A[:, :].rearrange("p (k n) -> p k n", n=NCOND)
                for k in range(KD):
                    v.wait_ge(xt_r, n * KD + k + 1)
                    tail = hT[:, k, SEQ:T].rearrange("p (n t) -> p n t", t=TS)
                    TT(tail, ps[4 + k % 2][:, 0:NSMP].rearrange("p (n t) -> p n t", t=TS),
                       A3[:, k, 1:NCOND].unsqueeze(2).to_broadcast([P, NSEQ, TS]), ALU.mult)
                    v.drain()
                    TT(tail, tail, m3[:, shift + k, 1:NCOND].unsqueeze(2).to_broadcast([P, NSEQ, TS]), ALU.add)\
                        .then_inc(h_r, 1)

            for c in range(12):
                slot, _f, n = where[("ada", c)]
                v.wait_ge(used[slot], n + 1)
                if c >= 2:
                    v.wait_ge(ada_t, c - 1)
                CP(arow[c % 2][0:NCOND, :], ps[6 + c % 2][0:NCOND, :]).then_inc(ada_cp, 1)
                if c == 3:
                    norm_rows(xr, xr)
            v.wait_ge(ada_t, 12)
            TT(m3, ps[0][:, 0:48 * NCOND].rearrange("p (m n) -> p m n", n=NCOND),
               colv[:, 0:48].unsqueeze(2).to_broadcast([P, 48, NCOND]), ALU.add)
            v.drain()
            for A, scale, gain in ((A1, 8, 48), (A2, 32, 56)):
                STT(A[:, :].rearrange("p (k n) -> p k n", n=NCOND), m3[:, scale:scale + KD, :], 1.0,
                    colv[:, gain:gain + KD].unsqueeze(2).to_broadcast([P, KD, NCOND]), ALU.add, ALU.mult)
            v.drain().then_inc(mod_r, 1)
            modulate(A1, 0, 0)
            v.wait_ge(in_ev, 16)
            for h in range(AH):
                TSC(logf[:, h, :], af[:, h, :], omlb[:, h:h + 1], lb[:, h:h + 1], ALU.mult, ALU.add)
            v.drain()
            TSC(af, logf, -1.0, 1.0, ALU.mult, ALU.add).then_inc(f_r, 1)
            v.wait_ge(lnf_r, 1)
            v.wait_ge(lvl_in, 48)
            for h in range(AH):
                v.tensor_tensor_scan(bsum[:, h, :], reset, logf[:, h, :], 0.0, ALU.mult, ALU.add)
            v.drain()

            def difference(x):
                h, n = x // NL, LEVELS[x % NL]
                cols = T if n <= 4 else SEQ
                if x >= 2:
                    v.wait_ge(kd_r, x - 1)
                b = bsum[:, h, 0:cols].rearrange("p (j c) -> p j c", c=2 * n)
                TT(diff[x % 2][:, 0:cols].rearrange("p (j c) -> p j c", c=2 * n), b,
                   b[:, :, n - 1:n].to_broadcast([P, cols // (2 * n), 2 * n]), ALU.subtract).then_inc(d_r, 1)

            def accumulate(w):
                h, l = w // (NL + 1), w % (NL + 1)
                mask = level[:, NL if l == 0 else l - 1, :]
                v.wait_ge(at_mm, w + 1)
                acc = attnT[:, h, 0:SEQ]
                tail = attnT[0:NSMP, h, SEQ:T]
                m4 = mask.unsqueeze(1).to_broadcast([P, PT_, P])
                src = ps[w % 2][:, :].rearrange("p (t c) -> p t c", c=P)
                small = ps[2 + w % 2][0:NSMP, 0:NSMP]
                if l == 0:
                    TT(acc.rearrange("p (t c) -> p t c", c=P), src, m4, ALU.mult)
                    TT(tail, small, mask[0:NSMP, 0:NSMP], ALU.mult)
                else:
                    TT(atmp[:, 0:SEQ].rearrange("p (t c) -> p t c", c=P), src, m4, ALU.mult)
                    if LEVELS[l - 1] <= 4:
                        TT(atmp[0:NSMP, SEQ:T], small, mask[0:NSMP, 0:NSMP], ALU.mult)
                    v.drain()
                    TT(acc, acc, atmp[:, 0:SEQ], ALU.add)
                    if LEVELS[l - 1] <= 4:
                        TT(tail, tail, atmp[0:NSMP, SEQ:T], ALU.add)
                v.drain().then_inc(at_ac, 1)

            last = blk[:, 0:48].rearrange("p (h c) -> p h c", c=12)
            e3 = ebl[:, :].rearrange("p (h c) -> p h c", c=12)

            def end_decays(h):
                v.wait_ge(eb_r, h + 1)
                for src, dst in ((logf, e3), (bsum, last)):
                    CP(dst[:, h, 0:PT_], src[:, h, P - 1:SEQ:P])
                    CP(dst[:, h, PT_:12], src[:, h, SEQ + TS - 1:T:TS])
                TT(aq[:, h, :], aq[:, h, :], logf[:, h, :], ALU.mult)
                v.drain()
                b = bsum[:, h, 0:SEQ].rearrange("p (j c) -> p j c", c=P)
                TT(b, last[:, h, 0:PT_].unsqueeze(2).to_broadcast([P, PT_, P]), b, ALU.subtract)
                b = bsum[:, h, SEQ:T].rearrange("p (j c) -> p j c", c=TS)
                TT(b, last[:, h, PT_:12].unsqueeze(2).to_broadcast([P, NSEQ, TS]), b, ALU.subtract)
                v.drain().then_inc(dl_r, 1)

            def decayed_keys(h):
                v.wait_ge(el_r, h + 1)
                TT(af[:, h, :], af[:, h, :], bsum[:, h, :], ALU.mult).then_inc(qk_r, 1)

            difference(0)
            done = 0
            for x in range(AH * NL):
                if x + 1 < AH * NL:
                    difference(x + 1)
                v.wait_ge(e_r, x + 1)
                if x >= 2:
                    v.wait_ge(at_mm, unit_of(x - 2) + 1)
                h, n = x // NL, LEVELS[x % NL]
                cols = T if n <= 4 else SEQ
                TT(qdec[x % 2][:, 0:cols], aq[:, h, 0:cols], diff[x % 2][:, 0:cols], ALU.mult).then_inc(qd_r, 1)
                while done < unit_of(x):
                    accumulate(done)
                    if done % (NL + 1) == NL:
                        end_decays(done // (NL + 1))
                    if done % (NL + 1) == 5 and done > NL:
                        decayed_keys(done // (NL + 1) - 1)
                    done += 1
            accumulate(done)
            end_decays(AH - 1)
            decayed_keys(AH - 1)
            for c in range(PT_):
                v.wait_ge(s_mm, c + 1)
                if c:
                    v.wait_ge(o_mm, c + 1)
                for h in range(AH):
                    new = ps[2 + c % 2][:, h * P:(h + 1) * P]
                    if c:
                        ins = STT(stP[:, h, :], stP[:, h, :], e3[:, h, c:c + 1], new, ALU.mult, ALU.add)
                    else:
                        ins = CP(stP[:, h, :], new)
                v.drain().then_inc(s_up, 1)
            for h in range(AH):
                if h:
                    v.wait_ge(sn_mm, h)
                TT(vbd[0:NSMP, :, :], ai[0:NSMP, PT_, h * P:(h + 1) * P].unsqueeze(1).to_broadcast([NSMP, NSEQ, P]),
                   C["seqmask"][0:NSMP, :].unsqueeze(2).to_broadcast([NSMP, NSEQ, P]), ALU.mult).then_inc(vb_r, 1)
                v.wait_ge(s0_in2[h % 2], 16 * (h // 2 + 1))
                if h >= 2:
                    v.wait_ge(sn_out2[h % 2], 16 * (h // 2))
                TT(st1[h % 2], st0[h % 2], e3[:, h, PT_:12].unsqueeze(2).to_broadcast([P, NSEQ, P]), ALU.mult)
                v.drain()
                v.wait_ge(sn_mm, h + 1)
                for k in range(2):
                    x = st1[h % 2][:, 4 * k:4 * k + 4, :]
                    ins = TT(x, x, ps[2 + k][:, :].rearrange("p (n c) -> p n c", c=P), ALU.add)
                ins.then_inc(sn_r, 1)
            v.wait_ge(o_ev, PT_)
            v.wait_ge(so_t, AH)
            v.wait_ge(hs_r, 1)
            TSC(hss[:, :], hss[:, :], 1.0 / P, EPS, ALU.mult, ALU.add).then_inc(hq_r, 1)
            v.wait_ge(hq_r, 2)
            v.reciprocal(hss[:, :], hss[:, :])
            v.drain()
            v.wait_ge(rope_r, 3)
            for t in range(NT):
                for h in range(AH):
                    r, cols = rows(t), slice(h * P, (h + 1) * P)
                    STT(oa[0:r, t, cols], oa[0:r, t, cols], hss[0:r, t * AH + h:t * AH + h + 1], ag[0:r, t, cols],
                        ALU.mult, ALU.mult)
            v.drain().then_inc(oa_r, 1)
            v.wait_ge(attn_in, 32)
            NU = PT_ * BH
            for s_ in range(NU + 3):
                if s_ < NU:
                    i = s_ // BH
                    v.wait_ge(sc_mm, s_ + 1)
                    own = ps[s_ % 2][:, i * P:(i + 1) * P]
                    TT(own, own, C["causal"], ALU.add)
                    v.drain()
                    RED(amx[:, s_:s_ + 1], ps[s_ % 2][:, 0:(i + 1) * P], AX, ALU.max)
                    v.drain()
                    TSC(mx[:, s_:s_ + 1], amx[:, s_:s_ + 1], -0.125, None, ALU.mult).then_inc(mx_r, 1)
                if 1 <= s_ <= NU:
                    u = s_ - 1
                    v.wait_ge(pt_mm, u + 1)
                    if u >= 2:
                        v.wait_ge(pv_mm, u - 1)
                    n = (u // BH + 1) * P
                    CP(probT[u % 2][:, 0:n], ps[2 + u % 2][:, 0:n]).then_inc(pt_r, 1)
                if s_ >= 2 and (s_ - 2) % BH == BH - 1:
                    i = (s_ - 2) // BH
                    v.wait_ge(pv_mm, BH * (i + 1))
                    v.reciprocal(amx[:, 32:40], sm[:, BH * i:BH * (i + 1)])
                    v.drain()
                    TT(ob[:, i, :].rearrange("p (h c) -> p h c", c=DH), ps[4 + i % 2][:, :].rearrange("p (h c) -> p h c", c=DH),
                       amx[:, 32:40].unsqueeze(2).to_broadcast([P, BH, DH]), ALU.mult).then_inc(ob_r, 1)
                    v.drain()
            v.wait_ge(rope_r, 2)
            q3 = bq[0:NSMP, PT_, :].rearrange("p (h d) -> p h d", d=DH)
            for k in range(2):
                CP(qdup[0:NSMP, :, k * DH:(k + 1) * DH], q3)
            v.drain().then_inc(qdup_r, 1)
            v.wait_ge(qb_mm, 1)
            v.wait_ge(zeroed, 3)
            src = ps[6][:, :].rearrange("p (h n t) -> p n h t", h=BH, t=TS)
            CP(qbd[0:64, :, :, 0:8], src[0:64])
            CP(qbd[64:128, :, :, 8:16], src[64:128])
            v.drain().then_inc(qb_r, 1)
            def choose_blocks(p, step):
                Sp, sn = S[p % 2], snew[p % 2]
                if step == 0:
                    v.wait_ge(nt_mm, p + 1)
                    m0 = 8 * (6 - 2 * p)
                    TT(sn, ps[5][:, 0:64], C["newmask"][:, m0:m0 + 64], ALU.add)
                    v.drain().then_inc(sn_t, 1)
                    v.wait_ge(ss_ev, NBLK * (p + 1))
                    RED(bs8[:, 0:8], Sp, AX, ALU.add)
                    v.drain()
                if step == 1:
                    RED(bm8[:, 0:8], Sp, AX, ALU.max)
                    RED(nm1, sn, AX, ALU.max)
                    v.drain()
                    bj = bs8[:, 0:8].unsqueeze(1).to_broadcast([P, 8, 8])
                    bi = bs8[:, 0:8].unsqueeze(2).to_broadcast([P, 8, 8])
                    TT(gt8, bj, bi, ALU.is_gt)
                    TT(eq8, bj, bi, ALU.is_equal)
                    v.drain()
                    TT(eq8, eq8, C["tie"].rearrange("p (i j) -> p i j", j=8), ALU.mult)
                    v.drain()
                    TT(gt8, gt8, eq8, ALU.add)
                    v.drain()
                if step == 2:
                    RED(rank8[:, 0:8], gt8, AX, ALU.add)
                    v.drain()
                    TSC(soff[:, 0:8], rank8[:, 0:8], float(TOPK), -BIG, ALU.is_ge, ALU.mult)
                    v.drain()
                    TT(bm8[:, 0:8], bm8[:, 0:8], soff[:, 0:8], ALU.add)
                    v.drain()
                    RED(m1_, bm8[:, 0:8], AX, ALU.max)
                    v.drain()
                if step == 3:
                    TT(m1_, m1_, nm1, ALU.max)
                    v.drain()
                    TSC(sbias[:, 8:9], m1_, -0.125, None, ALU.mult)
                    v.drain()
                    TSC(sbias[:, 0:8], soff[:, 0:8], sbias[:, 8:9], None, ALU.add).then_inc(sb_r, 1)

            v.wait_ge(zeroed, 7)
            for kind, p in SAMPLE_PHASES:
                if kind == "k":
                    for b in range(NBLK):
                        for n in range(2):
                            w = (p * NBLK + b) * 2 + n
                            v.wait_ge(key_mm, w + 1)
                            if w >= 2:
                                v.wait_ge(qks, w - 1)
                            CP(keyT[w % 2][:, 4:8, :], ps[2 * (w % 2) + 1][:, :].rearrange("p (h k) -> p h k", k=P))\
                                .then_inc(keyD, 1)
                        if p and b < 4:
                            choose_blocks(p - 1, b)
                else:
                    v.wait_ge(sp_r, p + 1)
                    RED(rs1[p], ssum, AX, ALU.add)
                    v.drain()
                    v.reciprocal(rs1[p], rs1[p])
                    if p == 2:
                        for step in range(4):
                            choose_blocks(3, step)
                    v.wait_ge(spv, p + 1)
                    for r0 in (0, 32, 64, 96):
                        CP(accS[p][r0:r0 + 16], ps[6][r0:r0 + 16, :].rearrange("p (k c) -> p k c", c=P))
                    v.drain().then_inc(acc_r, 1)
            for p in range(4):
                v.wait_ge(acc_t, p + 1)
                a3 = ps[p][:, :].rearrange("p (e c) -> p e c", c=32)
                o3 = odiag[p].rearrange("p (e t) -> p e t", t=TS)
                CP(o3[0:64], a3[0:64, :, 0:TS])
                CP(o3[64:128], a3[64:128, :, TS:2 * TS])
                v.drain().then_inc(od_r, 1)
            for p in range(4):
                v.wait_ge(of_mm, p + 1)
                for k in range(2):
                    TSC(orow[p][:, k * DH:(k + 1) * DH], ps[4 + p][:, 0:DH], rs1[p], None, ALU.mult)
                v.drain().then_inc(or_r, 1)
            for p in range(4):
                v.wait_ge(ot_mm, p + 1)
                for par in range(2):
                    s4 = ps[p][64 * par:64 * par + 64, 0:P]\
                        .rearrange("p (n k r t) -> p k n r t", n=2, r=2, t=TS)[:, :, :, par, :]
                    d4 = obT[64 * par:64 * par + 64, :, SEQ + 16 * p:SEQ + 16 * p + 16].rearrange("p k (n t) -> p k n t", t=TS)
                    CP(d4, s4)
                v.drain().then_inc(ot_r, 1)
            v.wait_ge(kv_out, 16 * (2 * (PT_ + NSEQ) + 1))
            for m in range(KD):
                v.wait_ge(g_r, m + 1)
                v.wait_ge(pr_mm, m + 1)
                for k in range(2):
                    x = sig[2 * (m % 2) + k]
                    for cols, bank in zip(HALVES, (ps[2 + k], ps[6 + k])):
                        TT(x[:, cols], x[:, cols], bank[:, 0:T // 2], ALU.mult)
                v.drain()
                TT(merged[:, m, :], sig[2 * (m % 2)], sig[2 * (m % 2) + 1], ALU.add).then_inc(mg_r, 1)
            def spread_gates(k, m0):
                for m in range(KD):
                    CP(gseq[k][:, m, :].rearrange("p (n t) -> p n t", t=TS),
                       m3[:, m0 + m, 1:NCOND].unsqueeze(2).to_broadcast([P, NSEQ, TS]))
                v.drain().then_inc(gseq_r, 1)

            spread_gates(0, 16)
            def norm_tile(t):
                r = rows(t)
                v.wait_ge(std_r, 2 + t)
                v.reciprocal(rstd[0:r, t:t + 1], rstd[0:r, t:t + 1])
                v.drain()
                TSC(xr[0:r, t, :], res[0:r, t, :], rstd[0:r, t:t + 1], None, ALU.mult).then_inc(xn_r, 1)

            v.memset(epsv, EPS)
            v.drain()
            v.wait_ge(xin2, 16 * NT)
            v.wait_ge(bc_r, 4)
            banks = (4, 5, 6, 7)
            for t in range(NT):
                r = rows(t)
                gt = gate1[0 if t < PT_ else 1]
                for k in range(2):
                    u = 2 * t + k
                    cols = slice(512 * k, 512 * k + 512)
                    v.wait_ge(y_mm, u + 1)
                    TT(xr[0:r, t, cols], ps[banks[u % 4]][0:r, :], gt[0:r, cols], ALU.mult).then_inc(y_r, 1)
                v.drain()
                TT(res[0:r, t, :], res[0:r, t, :], xr[0:r, t, :], ALU.add).then_inc(x2_r, 1)
                if t:
                    norm_tile(t - 1)
            spread_gates(1, 40)
            norm_tile(PT_)
            modulate(A2, 24, 1)
            v.wait_ge(wr_in, 16 * 8)
            v.memset(lg, 0.0)
            v.drain()
            v.wait_ge(lg_mm, 1)
            l3 = ps[0][:, 0:NT * 36].rearrange("p (t n) -> p t n", n=36)
            CP(lg[:, 0:PT_, :], l3[:, 0:PT_, :])
            CP(lg[0:NSMP, PT_, :], l3[0:NSMP, PT_, :])
            v.drain()
            rank_of = C["ranks8"]

            def first_max(x, n, oh):
                mxv, vm = rt(NT), rt(NT)
                RED(mxv, x, AX, ALU.max)
                v.drain()
                TT(oh, x, mxv.unsqueeze(2).to_broadcast([P, NT, n]), ALU.is_equal)
                v.drain()
                TT(oh, oh, rank_of[:, 0:n].unsqueeze(1).to_broadcast([P, NT, n]), ALU.mult)
                v.drain()
                RED(vm, oh, AX, ALU.max)
                v.drain()
                TT(oh, oh, vm.unsqueeze(2).to_broadcast([P, NT, n]), ALU.is_equal)
                v.drain()
                return mxv

            def bc(x, n):
                return x.unsqueeze(2).to_broadcast([P, NT, n])

            G, E3 = lg[:, :, 0:NG], lg[:, :, NG:36]
            ohg = rt(NT, NG)
            gm = first_max(G, NG, ohg)
            TT(rexp[:, :, 0:NG], G, bc(gm, NG), ALU.subtract)
            pick = rt(NT, NE)
            for t in range(NT):
                TT(pick[:, t, :].rearrange("p (g e) -> p g e", e=EPG), E3[:, t, :].rearrange("p (g e) -> p g e", e=EPG),
                   ohg[:, t, :].unsqueeze(2).to_broadcast([P, NG, EPG]), ALU.mult)
            v.drain()
            esel = rt(NT, EPG)
            for t in range(NT):
                RED(esel[:, t, :], pick[:, t, :].rearrange("p (g e) -> p e g", e=EPG), AX, ALU.add)
            v.drain()
            oh = [rt(NT, EPG), rt(NT, EPG)]
            top1 = first_max(esel, EPG, oh[0])
            esel2 = rt(NT, EPG)
            STT(esel2, oh[0], -BIG, esel, ALU.mult, ALU.add)
            v.drain()
            top2 = first_max(esel2, EPG, oh[1])
            TT(rexp[:, :, NG], top2, top1, ALU.subtract)
            v.drain().then_inc(rt_a, 1)
            valid = C["valid"]
            for k in range(2):
                for t in range(NT):
                    TT(onehots[:, k, t, :].rearrange("p (g e) -> p g e", e=EPG), ohg[:, t, :].unsqueeze(2).to_broadcast([P, NG, EPG]),
                       oh[k][:, t, :].unsqueeze(1).to_broadcast([P, NG, EPG]), ALU.mult)
                v.drain()
                TT(onehots[:, k, :, :], onehots[:, k, :, :], bc(valid, NE), ALU.mult)
            v.drain()
            TT(msum, onehots[:, 0, :, :], onehots[:, 1, :, :], ALU.add).then_inc(oh_r, 1)
            v.wait_ge(rt_b, 1)
            den, e21 = rt(NT), rt(NT)
            RED(den, rexp[:, :, 0:NG], AX, ALU.add)
            TSC(e21, rexp[:, :, NG], 1.0, None, ALU.add)
            v.drain()
            TT(den, den, e21, ALU.mult)
            v.drain()
            v.reciprocal(wts[:, 0:NT], den)
            v.drain()
            TT(wts[:, NT:2 * NT], wts[:, 0:NT], rexp[:, :, NG], ALU.mult)
            v.wait_ge(rk_mm, 1)
            rt_at[0] = HT
            cnt, extra, cum, obase = rt(NE), rt(NE), rt(NE), rt(NE)
            ranks = rt(NT, NE)
            CP(ranks, ps[1][:, 0:NT * NE].rearrange("p (t e) -> p t e", e=NE))
            CP(cnt, ps[1][:, NT * NE:(NT + 1) * NE])
            v.drain().then_inc(rk_r, 1)
            TSC(extra, cnt, float(CAP) + 0.5, None, ALU.is_ge)
            v.drain()
            for m in range(2, T // CAP + 1):
                STT(extra, cnt, float(m * CAP) + 0.5, extra, ALU.is_ge, ALU.add)
                v.drain()
            v.tensor_tensor_scan(cum, ones[:, 0:NE], extra, 0.0, ALU.mult, ALU.add)
            v.drain()
            TT(obase, cum, extra, ALU.subtract)
            v.drain()
            rk, ex, ob_, jq, sl_, jb, pay, tm5 = (rt(2, NT) for _ in range(8))
            tmpE = pick
            for k in range(2):
                for dst, row in ((rk, ranks), (ex, C["iotaE"].unsqueeze(1).to_broadcast([P, NT, NE])),
                                 (ob_, obase.unsqueeze(1).to_broadcast([P, NT, NE]))):
                    TT(tmpE, onehots[:, k, :, :], row, ALU.mult)
                    v.drain()
                    RED(dst[:, k, :], tmpE, AX, ALU.add)
                    v.drain()
            TSC(jq, rk, float(CAP) - 0.5, None, ALU.is_ge)
            v.drain()
            for m in range(2, T // CAP + 1):
                STT(jq, rk, float(m * CAP) - 0.5, jq, ALU.is_ge, ALU.add)
                v.drain()
            STT(sl_, jq, -float(CAP), rk, ALU.mult, ALU.add)
            TSC(tm5, jq, 0.5, None, ALU.is_ge)
            TT(jb, ob_, jq, ALU.add)
            v.drain()
            STT(jb, jb, float(NE - 1), ex, ALU.add, ALU.subtract)
            v.drain()
            TT(jb, jb, tm5, ALU.mult)
            v.drain()
            TT(jb, jb, ex, ALU.add)
            for k in range(2):
                STT(pay[:, k, :], valid, float(k), C["payload"], ALU.mult, ALU.add)
            v.drain()
            for c in range(2 * NT):
                k, t = c // NT, c % NT
                if c >= 2:
                    v.wait_ge(tb_mm, c - 1)
                TSC(slot1[c % 2], C["iota"], sl_[:, k, t:t + 1], None, ALU.is_equal)
                TSC(job1[c % 2], C["iota"][:, 0:NJ + 2], jb[:, k, t:t + 1], pay[:, k, t:t + 1], ALU.is_equal, ALU.mult)
                v.drain().then_inc(oh_r, 1)
            je, jw = rt(EXTRA), rt(EXTRA, NE)
            big = [rt(EXTRA, NE), rt(EXTRA, NE)]
            jrow = C["iota"][:, 0:EXTRA].unsqueeze(2).to_broadcast([P, EXTRA, NE])
            TT(big[0], jrow, obase.unsqueeze(1).to_broadcast([P, EXTRA, NE]), ALU.is_ge)
            TT(big[1], jrow, cum.unsqueeze(1).to_broadcast([P, EXTRA, NE]), ALU.is_lt)
            v.drain()
            TT(jw, big[0], big[1], ALU.mult)
            v.drain()
            TT(jw, jw, C["iotaE"].unsqueeze(1).to_broadcast([P, EXTRA, NE]), ALU.mult)
            v.drain()
            RED(je, jw, AX, ALU.add)
            v.drain()
            CP(ctl[:, 0:EXTRA], je)
            CP(ctl[:, 8:9], cum[:, NE - 1:NE])
            v.drain().then_inc(tb_r, 1)
            v.wait_ge(tb_mm, 2 * NT)
            tab, emp = rt(NJ + 2), rt(NJ + 2)
            TSC(emp, ps[4][:, 0:NJ + 2], 0.5, ABSENT, ALU.is_lt, ALU.mult)
            v.drain()
            STT(tab, ps[4][:, 0:NJ + 2], -1.0, emp, ALU.add, ALU.add)
            v.drain()
            CP(jobs_i[:, NJ + 2:2 * NJ + 4], tab)
            v.drain()
            TSC(jobs_i[:, 0:NJ + 2], jobs_i[:, NJ + 2:2 * NJ + 4], 1, None, ALU.arith_shift_right).then_inc(tb_r, 1)

            def dve_rows(i, par):
                v.wait_ge(xt2, 2 * i + par + 1)
                CP(xgT[par][:, 4:8, :], ps[1][:, :].rearrange("p (k s) -> p k s", s=CAP)).then_inc(xtD, 1)

            def dve_job(i, par, first=False):
                j = 2 * i + par
                v.wait_ge(sl, j + 1)
                v.wait_ge(used[3 * par + 1], i + (used0[3 * par + 1] + 1))
                TT(hid, hs, ps[3][:, :].rearrange("p (k s) -> p k s", s=CAP), ALU.mult).then_inc(hd, 1)
                dve_rows(i + par, 1 - par)
                v.wait_ge(used[3 * par + 2], i + (used0[3 * par + 2] + 1))
                if not first:
                    v.wait_ge(sc2[par], i * 16)
                CP(yj[par][:, 512:1024], ps[5][:, :]).then_inc(yD, 1)

            dve_rows(0, 0)
            dve_job(0, 0, first=True)
            dve_job(0, 1, first=True)
            with v.Fori(1, NE // 2) as i:
                dve_job(i, 0)
                dve_job(i, 1)
            njobs = v.value_load(ctl[0:1, 8:9], min_val=0, max_val=EXTRA)
            with v.Fori(0, EXTRA // 2) as i:
                with v.If(njobs > 2 * i):
                    dve_job(i + NE // 2, 0)
                    dve_job(i + NE // 2, 1)
            def sum_row(t):
                r, y = rows(t), ybuf[t]
                y0, y1 = y[0:r, 0:D], y[0:r, D:2 * D]
                v.wait_ge(fin_w, t + 1)
                STT(y0, y0, wts[0:r, t:t + 1], y1, ALU.mult, ALU.add)
                v.drain()
                TT(y0, y0, gate2[0 if t < PT_ else 1][0:r, :], ALU.mult)
                v.drain()
                TT(y0, y0, res[0:r, t, :], ALU.add).then_inc(fin_a, 1)

            def scale_row(t):
                r, y0 = rows(t), ybuf[t][0:rows(t), 0:D]
                v.wait_ge(fin_s, t + 1)
                v.reciprocal(fss[0:r, t:t + 1], fss[0:r, t:t + 1])
                v.drain()
                STT(y0, y0, fss[0:r, t:t + 1], fgain[0:r, :], ALU.mult, ALU.mult).then_inc(fin_v, 1)

            sum_row(0)
            v.wait_ge(c_in, 16 * 9)
            for t in range(NT):
                if t + 1 < NT:
                    sum_row(t + 1)
                scale_row(t)


def shape_constants():
    import numpy as np
    c = np.zeros((P, NCONST), np.float32)

    def put(name, a):
        at, n = CONST[name]
        c[:, at:at + n] = np.asarray(a, np.float32).reshape(P, n)

    p, q = np.arange(P)[:, None], np.arange(P)[None, :]
    put("ident", p == q)
    put("before", p < q)
    put("ones", np.ones((P, P)))
    put("causal", np.where(q <= p, 0.0, -BIG))
    m, s = np.arange(14)[None, :, None], np.arange(8)[None, None, :]
    n2, t = (np.arange(P) // 64)[:, None, None], (np.arange(P) % 8)[:, None, None]
    put("newmask", np.where((m == n2 + 6) & (s <= t), 0.0, -BIG))
    put("fold", (p % 64) == np.arange(64)[None, :])
    half = 8
    inv = np.power(np.float32(500000.0), -(np.arange(half, dtype=np.float32) * np.float32(2.0) / np.float32(16)))
    pos = np.zeros((P, NT), np.float32)
    pos[:, 0:PT_] = np.arange(P)[:, None] + P * np.arange(PT_)[None, :]
    pos[:, PT_] = 2048 + np.arange(P) % TS
    ang = (pos[:, :, None] * inv[None, None, :]).astype(np.float32)
    put("cos", np.cos(ang))
    put("sin", np.sin(ang))
    put("iota", np.broadcast_to(q, (P, P)))
    put("ranks8", np.broadcast_to(8 - np.arange(8), (P, 8)))
    put("iotaE", np.broadcast_to(np.arange(NE), (P, NE)))
    put("seqmask", (p // TS) == np.arange(8)[None, :])
    put("tie", np.broadcast_to(np.arange(8)[None, :] < np.arange(8)[:, None], (P, 8, 8)))
    row = np.arange(P)[:, None] + P * np.arange(NT)[None, :]
    put("valid", row < T)
    put("payload", np.where(row < T, 2 * row + 1, 0))
    col = np.arange(T)
    put("reset", np.broadcast_to(np.where(col < SEQ, col % P != 0, col % TS != 0), (P, T)))
    lv = np.zeros((P, 8, P))
    for i, n in enumerate(LEVELS):
        lv[:, i] = (p // (2 * n) == q // (2 * n)) & (p % (2 * n) < n) & (q % (2 * n) >= n)
    lv[:, 7] = p == q
    put("levels", lv)
    return c


_INS = ["x_prompt", "x_sample", "c_prompt", "c_sample", "cache_k", "cache_v", "state_hgrn", "page_table", "w_ada",
        "b_ada", "norm_mix", "norm_ffn", "w_in", "hgrn_lb_logits", "hgrn_norm", "w_proj_a", "w_proj_b", "w_out",
        "w_group", "b_group", "w_expert_router", "b_expert_router", "w_gate", "w_up", "w_down", "norm_final"]
_OUTS = [(1, SEQ, D), (NSEQ, TS, D), (1, 1, BH, SEQ, DH), (1, 1, BH, SEQ, DH), (1, 1, AH, P, P),
         (1, NSEQ, BH, TS, DH), (1, NSEQ, BH, TS, DH), (1, NSEQ, AH, P, P)]


def kernel(**inputs):
    import numpy as _np
    import concourse.bacc as _bacc
    from concourse import mybir as _mybir
    from concourse.bass_utils import run_bass_kernel_spmd as _run

    nc = _bacc.Bacc("TRN2", target_bir_lowering=False, num_devices=1)
    arrays, args = {}, []
    given = [(name, _np.ascontiguousarray(inputs[name])) for name in _INS] + [("shape_constants", shape_constants())]
    for name, a in given:
        arrays[f"in_{name}_dram"] = a
        args.append(nc.dram_tensor(f"in_{name}_dram", a.shape, _mybir.dt.from_np(a.dtype), kind="ExternalInput").ap())
    for i, shape in enumerate(_OUTS):
        args.append(nc.dram_tensor(f"out_{i}_dram", shape, F32, kind="ExternalOutput").ap())
    bass_hybrid_step(nc, *args)
    r = _run(nc, [arrays], core_ids=[0])
    return tuple(r.results[0][f"out_{i}_dram"] for i in range(len(_OUTS)))
```
